# Optimizing a Trainium2 kernel written in Bass

```python
import math
import jax, jax.numpy as jnp
from jax import lax
import numpy as np

D_MODEL = 1024
BATCH = 1
SEQ = 2048
DEPTH = 1

HG_HEADS = 4
HG_HEAD_K = 128
HG_HEAD_V = 128
HG_K_DIM = HG_HEADS * HG_HEAD_K
HG_V_DIM = HG_HEADS * HG_HEAD_V
GDN_HEADS = 4
GDN_HEAD_K = 128
GDN_HEAD_V = 128
GDN_QK_DIM = GDN_HEADS * GDN_HEAD_K
GDN_V_DIM = GDN_HEADS * GDN_HEAD_V
GDN_QKV = 2 * GDN_QK_DIM + GDN_V_DIM
MIX_DIM = HG_V_DIM + GDN_V_DIM
CONV_K = 4
CHUNK = 64
IN_COLS = 2 * HG_K_DIM + 2 * HG_V_DIM + GDN_QKV + GDN_V_DIM + 2 * GDN_HEADS
N_GROUPS = 8
EXPERTS_PER_GROUP = 8
N_EXPERTS = N_GROUPS * EXPERTS_PER_GROUP
TOP_K = 2
EXPERT_FF = 256
MOE_BLOCK = 256
NORM_EPS = 1e-6

kernel_name = 'hybrid_hgrn2_gdn_hier_moe'

def rmsnorm(x, w):
    xf = x.astype(jnp.float32)
    y = xf * lax.rsqrt(jnp.mean(xf * xf, axis=-1, keepdims=True) + NORM_EPS)
    return (y * w.astype(jnp.float32)).astype(x.dtype)

def gated_head_rmsnorm(o, z, w, n_heads):
    b, s, _ = o.shape
    oh = o.astype(jnp.float32).reshape(b, s, n_heads, -1)
    y = oh * lax.rsqrt(jnp.mean(oh * oh, axis=-1, keepdims=True) + NORM_EPS) * w.astype(jnp.float32)
    zh = z.astype(jnp.float32).reshape(b, s, n_heads, -1)
    return (y * jax.nn.silu(zh)).reshape(b, s, -1)

def l2norm(t):
    return t * lax.rsqrt(jnp.sum(t * t, axis=-1, keepdims=True) + 1e-6)

def to_chunks(t):
    b, s, h = t.shape[:3]
    t = t.reshape((b, s // CHUNK, CHUNK, h) + t.shape[3:])
    return jnp.transpose(t, (1, 0, 3, 2) + tuple(range(4, t.ndim)))

def from_chunks(o):
    n, b, h, c, d = o.shape
    return jnp.transpose(o, (1, 0, 3, 2, 4)).reshape(b, n * c, h * d)

def causal_conv_silu(u, w):
    s = u.shape[1]
    up = jnp.pad(u, ((0, 0), (CONV_K - 1, 0), (0, 0)))
    y = up[:, 0:s] * w[0]
    for j in range(1, CONV_K):
        y = y + up[:, j:j + s] * w[j]
    return jax.nn.silu(y)

def hgrn2_mixer(q, f_logit, i, lb):
    f32 = jnp.float32
    b, s, _ = q.shape
    q = jax.nn.silu(q.astype(f32)) * HG_HEAD_K ** -0.5
    f = lb + (1.0 - lb) * jax.nn.sigmoid(f_logit.astype(f32))
    k = 1.0 - f
    log_f = jnp.log(f)
    qc = to_chunks(q.reshape(b, s, HG_HEADS, HG_HEAD_K))
    kc = to_chunks(k.reshape(b, s, HG_HEADS, HG_HEAD_K))
    lfc = to_chunks(log_f.reshape(b, s, HG_HEADS, HG_HEAD_K))
    vc = to_chunks(i.astype(f32).reshape(b, s, HG_HEADS, HG_HEAD_V))
    tri = jnp.tril(jnp.ones((CHUNK, CHUNK), dtype=bool))[:, :, None]

    def step(state, inp):
        qb, kb, vb, lfb = inp
        cum = jnp.cumsum(lfb, axis=2)
        diff = cum[:, :, :, None, :] - cum[:, :, None, :, :]
        dec = jnp.where(tri, jnp.exp(jnp.where(tri, diff, 0.0)), 0.0)
        att = jnp.einsum('bhtk,bhsk,bhtsk->bhts', qb, kb, dec)
        o = jnp.einsum('bhtk,bhkv->bhtv', qb * jnp.exp(cum), state) + jnp.einsum('bhts,bhsv->bhtv', att, vb)
        last = cum[:, :, -1:, :]
        state = jnp.exp(last)[:, :, 0, :, None] * state + jnp.einsum('bhsk,bhsv->bhkv', kb * jnp.exp(last - cum), vb)
        return state, o

    state0 = jnp.zeros((b, HG_HEADS, HG_HEAD_K, HG_HEAD_V), f32)
    _, o = lax.scan(step, state0, (qc, kc, vc, lfc))
    return from_chunks(o)

def gated_deltanet_mixer(q, k, v, a, b_logit, a_log, dt_bias):
    f32 = jnp.float32
    bsz, s, _ = q.shape
    q = l2norm(q.astype(f32).reshape(bsz, s, GDN_HEADS, GDN_HEAD_K)) * GDN_HEAD_K ** -0.5
    k = l2norm(k.astype(f32).reshape(bsz, s, GDN_HEADS, GDN_HEAD_K))
    v = v.astype(f32).reshape(bsz, s, GDN_HEADS, GDN_HEAD_V)
    beta = jax.nn.sigmoid(b_logit.astype(f32))
    g = -jnp.exp(a_log.astype(f32)) * jax.nn.softplus(a.astype(f32) + dt_bias.astype(f32))
    qc, kc, vc = to_chunks(q), to_chunks(k), to_chunks(v)
    bc = to_chunks(beta)
    gc = jnp.cumsum(to_chunks(g), axis=-1)
    incl = jnp.tril(jnp.ones((CHUNK, CHUNK), dtype=bool))
    strict = jnp.tril(jnp.ones((CHUNK, CHUNK), dtype=bool), k=-1)
    diff = gc[..., :, None] - gc[..., None, :]
    dec = jnp.where(incl, jnp.exp(jnp.where(incl, diff, 0.0)), 0.0)
    kk = jnp.einsum('nbhtk,nbhsk->nbhts', kc, kc)
    a_mat = jnp.where(strict, bc[..., :, None] * kk * dec, 0.0)
    rhs = jnp.concatenate([kc * (bc * jnp.exp(gc))[..., None], vc * bc[..., None]], axis=-1)
    sol = lax.linalg.triangular_solve(a_mat, rhs, left_side=True, lower=True, unit_diagonal=True)
    w_c, u_c = sol[..., :GDN_HEAD_K], sol[..., GDN_HEAD_K:]
    qk = jnp.einsum('nbhtk,nbhsk->nbhts', qc, kc) * dec
    qg = qc * jnp.exp(gc)[..., None]
    glast = gc[..., -1:]
    kdec = kc * jnp.exp(glast - gc)[..., None]
    gend = jnp.exp(glast[..., 0])

    def step(state, inp):
        qg_n, qk_n, w_n, u_n, kdec_n, gend_n = inp
        v_new = u_n - jnp.einsum('bhck,bhkv->bhcv', w_n, state)
        o = jnp.einsum('bhck,bhkv->bhcv', qg_n, state) + jnp.einsum('bhts,bhsv->bhtv', qk_n, v_new)
        state = gend_n[..., None, None] * state + jnp.einsum('bhck,bhcv->bhkv', kdec_n, v_new)
        return state, o

    state0 = jnp.zeros((bsz, GDN_HEADS, GDN_HEAD_K, GDN_HEAD_V), f32)
    _, o = lax.scan(step, state0, (qg, qk, w_c, u_c, kdec, gend))
    return from_chunks(o)

def hier_moe(xn, w_group, w_expert, w_gate, w_up, w_down):
    f32 = jnp.float32
    bsz, s, d = xn.shape
    t = bsz * s
    xt = xn.reshape(t, d)
    g_logits = (xt @ w_group).astype(f32)
    g_prob = jax.nn.softmax(g_logits, axis=-1)
    _, g_idx = lax.top_k(g_logits, 1)
    p_group = jnp.take_along_axis(g_prob, g_idx, axis=-1)
    e_logits = (xt @ w_expert).astype(f32).reshape(t, N_GROUPS, EXPERTS_PER_GROUP)
    e_sel = jnp.take_along_axis(e_logits, g_idx[:, :, None], axis=1)[:, 0]
    top_v, top_i = lax.top_k(e_sel, TOP_K)
    gate = (jax.nn.softmax(top_v, axis=-1) * p_group).reshape(-1)
    expert_id = (g_idx * EXPERTS_PER_GROUP + top_i).reshape(-1).astype(jnp.int32)
    tok = jnp.broadcast_to(jnp.arange(t, dtype=jnp.int32)[:, None], (t, TOP_K)).reshape(-1)
    n_assign = t * TOP_K
    n_blocks = n_assign // MOE_BLOCK + N_EXPERTS
    order = jnp.argsort(expert_id)
    se, stok, sgate = expert_id[order], tok[order], gate[order]
    counts = jax.ops.segment_sum(jnp.ones((n_assign,), jnp.int32), expert_id, num_segments=N_EXPERTS)
    starts = jnp.cumsum(counts) - counts
    padded = (counts + MOE_BLOCK - 1) // MOE_BLOCK * MOE_BLOCK
    pend = jnp.cumsum(padded)
    pstart = pend - padded
    dest = pstart[se] + jnp.arange(n_assign, dtype=jnp.int32) - starts[se]
    buf_tok = jnp.full((n_blocks * MOE_BLOCK,), t, jnp.int32).at[dest].set(stok)
    buf_gate = jnp.zeros((n_blocks * MOE_BLOCK,), f32).at[dest].set(sgate)
    block_start = jnp.arange(n_blocks, dtype=jnp.int32) * MOE_BLOCK
    block_expert = jnp.minimum(jnp.searchsorted(pend, block_start, side='right'), N_EXPERTS - 1).astype(jnp.int32)
    x_pad = jnp.concatenate([xt, jnp.zeros((1, d), xt.dtype)], axis=0)

    def block_fn(args):
        idx, gw, e = args
        xb = x_pad[idx]
        hb = jax.nn.silu(xb @ w_gate[e]) * (xb @ w_up[e])
        return (hb @ w_down[e]) * gw[:, None].astype(xb.dtype)

    yb = lax.map(block_fn, (buf_tok.reshape(n_blocks, MOE_BLOCK), buf_gate.reshape(n_blocks, MOE_BLOCK), block_expert))
    y = jax.ops.segment_sum(yb.reshape(-1, d), buf_tok, num_segments=t + 1)[:t]
    return y.reshape(bsz, s, d)

def setup_inputs(seed: int = 0) -> dict:
    key = jax.random.key(seed)
    ks = jax.random.split(key, 17)
    nrm = jax.random.normal
    dt = jnp.exp(jax.random.uniform(ks[7], (DEPTH, GDN_HEADS), minval=math.log(1e-3), maxval=math.log(1e-1)))
    return {
        'x': nrm(ks[0], (BATCH, SEQ, D_MODEL), jnp.float32),
        'norm_mix_w': 1.0 + 0.02 * nrm(ks[1], (DEPTH, D_MODEL), jnp.float32),
        'w_in': nrm(ks[2], (DEPTH, D_MODEL, IN_COLS), jnp.float32) * D_MODEL ** -0.5,
        'hgrn_lb_logits': 0.1 * nrm(ks[3], (DEPTH + 1, HG_K_DIM), jnp.float32),
        'hgrn_onorm_w': 1.0 + 0.02 * nrm(ks[4], (DEPTH, HG_HEAD_V), jnp.float32),
        'gdn_conv_w': nrm(ks[5], (DEPTH, CONV_K, GDN_QKV), jnp.float32) * CONV_K ** -0.5,
        'gdn_a_log': jnp.log(jax.random.uniform(ks[6], (DEPTH, GDN_HEADS), minval=1.0, maxval=16.0)),
        'gdn_dt_bias': dt + jnp.log(-jnp.expm1(-dt)),
        'gdn_onorm_w': 1.0 + 0.02 * nrm(ks[8], (DEPTH, GDN_HEAD_V), jnp.float32),
        'w_out': nrm(ks[9], (DEPTH, MIX_DIM, D_MODEL), jnp.float32) * MIX_DIM ** -0.5,
        'norm_moe_w': 1.0 + 0.02 * nrm(ks[10], (DEPTH, D_MODEL), jnp.float32),
        'router_group_w': nrm(ks[11], (DEPTH, D_MODEL, N_GROUPS), jnp.float32) * D_MODEL ** -0.5,
        'router_expert_w': nrm(ks[12], (DEPTH, D_MODEL, N_EXPERTS), jnp.float32) * D_MODEL ** -0.5,
        'expert_w_gate': nrm(ks[13], (DEPTH, N_EXPERTS, D_MODEL, EXPERT_FF), jnp.float32) * D_MODEL ** -0.5,
        'expert_w_up': nrm(ks[14], (DEPTH, N_EXPERTS, D_MODEL, EXPERT_FF), jnp.float32) * D_MODEL ** -0.5,
        'expert_w_down': nrm(ks[15], (DEPTH, N_EXPERTS, EXPERT_FF, D_MODEL), jnp.float32) * EXPERT_FF ** -0.5,
        'final_norm_w': 1.0 + 0.02 * nrm(ks[16], (D_MODEL,), jnp.float32),
    }

def reference(x, norm_mix_w, w_in, hgrn_lb_logits, hgrn_onorm_w, gdn_conv_w, gdn_a_log, gdn_dt_bias,
              gdn_onorm_w, w_out, norm_moe_w, router_group_w, router_expert_w, expert_w_gate,
              expert_w_up, expert_w_down, final_norm_w):
    sizes = (HG_K_DIM, HG_K_DIM, HG_V_DIM, HG_V_DIM, GDN_QKV, GDN_V_DIM, GDN_HEADS, GDN_HEADS)
    offsets = tuple(int(v) for v in np.cumsum(sizes)[:-1])
    lower_bounds = jnp.cumsum(jax.nn.softmax(hgrn_lb_logits.astype(jnp.float32), axis=0), axis=0)
    h = x
    for l in range(DEPTH):
        hn = rmsnorm(h, norm_mix_w[l])
        proj = hn @ w_in[l]
        hq, hf, hi, hg, gqkv, gz, ga, gb = jnp.split(proj, offsets, axis=-1)
        o_hg = hgrn2_mixer(hq, hf, hi, lower_bounds[l])
        o_hg = gated_head_rmsnorm(o_hg, hg, hgrn_onorm_w[l], HG_HEADS)
        qkv = causal_conv_silu(gqkv, gdn_conv_w[l])
        gq, gk, gv = jnp.split(qkv, (GDN_QK_DIM, 2 * GDN_QK_DIM), axis=-1)
        o_gd = gated_deltanet_mixer(gq, gk, gv, ga, gb, gdn_a_log[l], gdn_dt_bias[l])
        o_gd = gated_head_rmsnorm(o_gd, gz, gdn_onorm_w[l], GDN_HEADS)
        mix = jnp.concatenate([o_hg, o_gd], axis=-1).astype(h.dtype) @ w_out[l]
        h = h + mix
        h = h + hier_moe(rmsnorm(h, norm_moe_w[l]), router_group_w[l], router_expert_w[l],
                         expert_w_gate[l], expert_w_up[l], expert_w_down[l])
    return rmsnorm(h, final_norm_w)


_drawn_inputs = setup_inputs


def setup_inputs(seed=0):
    import zlib

    import numpy as np

    out = dict(_drawn_inputs(seed))
    spreads = {}
    factors = {'hgrn_lb_logits': 5.362,
     'hgrn_onorm_w': 4.196,
     'gdn_onorm_w': 4.373,
     'norm_moe_w': 2.714,
     'final_norm_w': 2.859}
    for name, (base, spread) in spreads.items():
        noise = np.random.default_rng([zlib.crc32(name.encode()), seed]).standard_normal(out[name].shape)
        drawn = base * np.exp(spread * noise) if base else spread * noise
        out[name] = __import__('jax').numpy.asarray(drawn.astype(out[name].dtype))
    for name, factor in factors.items():
        out[name] = (out[name] * factor).astype(out[name].dtype)
    return out
```

```python
import math
from contextlib import ExitStack

import numpy as np

import concourse.bass as bass
from concourse import mybir

F32 = mybir.dt.float32
I32 = mybir.dt.int32
U32 = mybir.dt.uint32
U8 = mybir.dt.uint8
ALU = mybir.AluOpType
ACT = mybir.ActivationFunctionType
AX = mybir.AxisListType

P = 128
T = 2048
D = 1024
KD = D // P
HEADS = 4
HALF = 1024
NHALF = T // HALF
NC = HALF // P
GRP = 512
NG = HALF // GRP
CPG = GRP // P
TAPS = 4
HALO = TAPS - 1
EPS = 1e-6
NE = 64
EPG = 8
FF = 256
NT = T // P
NSLOT = 96
OOB = 1 << 20
ATT_LEVELS = (64, 32, 16, 8)
SOLVE_LEVELS = (1, 2, 4, 8, 16, 32, 64)

C_ID, C_UI, C_US, C_ONE, C_SCAN = 0, 128, 256, 384, 512
C_I64 = C_SCAN + HALF
C_I8 = C_I64 + 64
C_SLOT = C_I8 + 8
C_COL = C_SLOT + NSLOT
COL_EPS, COL_EPS4, COL_LNHQ, COL_LNGQ = range(4)
C_TOK = C_COL + 4
C_N = C_TOK + NT
M_SOL = 0
M_SOLT = M_SOL + 7 * P
M_ATT = M_SOLT + 7 * P
M_ATTF = M_ATT + 4 * 64
M_N = M_ATTF + P


def constant_tables():
    c = np.zeros((P, C_N), np.float32)
    i = np.arange(P)
    c[:, C_ID:C_ID + P] = np.eye(P)
    c[:, C_UI:C_UI + P] = i[:, None] <= i[None, :]
    c[:, C_US:C_US + P] = i[:, None] < i[None, :]
    c[:, C_ONE:C_ONE + P] = 1.0
    c[:, C_SCAN:C_SCAN + HALF] = (np.arange(HALF) % P != 0)[None, :]
    c[:, C_I64:C_I64 + 64] = np.arange(64)[None, :]
    c[:, C_I8:C_I8 + 8] = np.arange(8)[None, :]
    c[:, C_SLOT:C_SLOT + NSLOT] = np.arange(NSLOT)[None, :]
    c[:, C_COL + COL_EPS] = EPS
    c[:, C_COL + COL_EPS4] = 4 * EPS
    c[:, C_COL + COL_LNHQ] = math.log(0.5 * P ** -0.5)
    c[:, C_COL + COL_LNGQ] = math.log(P ** -0.5)
    c[:, C_TOK:C_TOK + NT] = i[:, None] + P * np.arange(NT)[None, :]
    m = np.zeros((P, M_N), np.float32)
    for l, h in enumerate(SOLVE_LEVELS):
        late = (i[:, None] // h % 2 == 1) & (i[None, :] // h == i[:, None] // h - 1)
        m[:, M_SOL + l * P:M_SOL + (l + 1) * P] = late
        m[:, M_SOLT + l * P:M_SOLT + (l + 1) * P] = late.T
    for l, h in enumerate(ATT_LEVELS):
        t = np.concatenate([np.arange(b * 2 * h + h, (b + 1) * 2 * h) for b in range(P // (2 * h))])
        m[:, M_ATT + l * 64:M_ATT + (l + 1) * 64] = i[:, None] // h == t[None, :] // h - 1
    m[:, M_ATTF:M_ATTF + P] = (i[:, None] // 8 == i[None, :] // 8) & (i[:, None] <= i[None, :])
    return c, m


def ring_order():
    pair = lambda *names: [(n, g) for n in names for g in range(NG)]
    order = pair("F", "Q", "Z", "V", "Gq", "Gk", "Gv", "Gz", "GR") + [("A", l) for l in range(4)]
    order += pair("AF", "KL", "DS") + [("N", m) for m in range(4)] + pair("NH", "KK", "KT", "VT", "AT", "QK")
    for l in range(6):
        order += [("P", l, g) for g in range(NG)]
        for g in range(NG):
            order += ([("X", l, g)] if l < 5 else []) + [("Y", l, g)]
    order += pair("WT")
    for c in range(NC):
        order += [("VN", c), ("S", c)]
    return order + pair("NG")


RING = ring_order()


class Stages:

    def __init__(self, nc, prefix, per):
        self.per = per
        self.sem = {n: nc.alloc_semaphore(prefix + n) for n in per}

    def engine(self, eng, turn=0):
        return Turn(self, eng, turn)


class Turn:

    def __init__(self, stages, eng, turn):
        self.s, self.eng, self.turn, self.n, self.seen = stages, eng, turn, {}, {}

    def wait(self, name, count):
        if count > self.seen.get(name, -1):
            self.seen[name] = count
            self.eng.wait_ge(self.s.sem[name], self.turn * self.s.per[name] + count)

    def hold(self):
        self.eng.nop(nofuse=True)

    def done(self, ins, name, by=1):
        self.n[name] = self.n.get(name, 0) + by
        ins.then_inc(self.s.sem[name], by)

    def close(self):
        for name, n in self.n.items():
            assert n == self.s.per[name], (name, n, self.s.per[name])


def trunk(nc, a, pool_dma):
    with ExitStack() as ctx:
        def sb(name, *shape, dt=F32):
            return ctx.enter_context(nc.sbuf_tensor(name, [P, *shape], dt))

        cst, msk = sb("cst", C_N), sb("msk", M_N, dt=U8)
        hT = sb("hT", KD, HALF)
        WH = sb("WH", 4, KD, P)
        WG = sb("WG", 4, KD, P)
        H = {n: sb("h_" + n, HALF) for n in
             ("kh", "cum", "qh", "zh", "v", "d0", "d1", "e0", "e1", "m0", "m1", "att", "qe", "kl", "klt", "o", "lf")}
        SH = sb("SH", NC + 1, P)
        arena = sb("arena", 12 * (HALF + HALO))
        G = {n: arena[:, i * (HALF + HALO):(i + 1) * (HALF + HALO)] for i, n in enumerate(
            ("rq", "rk", "rv", "cq", "ck", "cv", "tq", "tk", "tv", "zg", "gb", "egr"))}
        X8 = arena[:, 0:NC * D].rearrange("p (t d) -> p t d", t=NC)
        raw = {n: G["r" + n] for n in "qkv"}
        conv = {n: G["c" + n][:, 0:HALF] for n in "qkv"}
        tmp = {n: G["t" + n][:, 0:HALF] for n in "qkv"}
        ZG, GB, EGR = (G[n][:, 0:HALF] for n in ("zg", "gb", "egr"))
        DM, DEC, DECT = (raw[n][:, 0:HALF] for n in "qkv")
        A_, AT_, X_, Y_, PP = (H[n] for n in ("d0", "d1", "e0", "e1", "m0"))
        RK, RV, KDEC, NW, QKD, QG = (H[n] for n in ("m1", "qe", "kl", "klt", "cum", "qh"))
        OG = H["lf"]
        SG = sb("SG", P)
        VN = sb("VN", 2, P)
        HALOS = sb("HALOS", HEADS, 3, HALO)
        SALL = sb("SALL", 2, HEADS, P)
        PT = sb("PT", HEADS, 15)
        PC = sb("PC", 15)
        GT = sb("GT", 7, NC, HEADS)
        GC = sb("GC", 7, NC)
        nw, onw = sb("nw", KD), sb("onw", 2)
        wab = sb("wab", KD, 8)
        lbt = sb("lbt", 2, HEADS)
        agt = sb("agt", 2, HEADS)
        ss = sb("ss", 6, NC)
        gtmp = sb("gtmp", 5, NC, HEADS)
        el = sb("el", NC)
        ps = [ctx.enter_context(nc.psum_tensor(f"ps{i}", [P, GRP], F32)) for i in range(8)]

        ident, UI, ones = cst[:, C_ID:C_ID + P], cst[:, C_UI:C_UI + P], cst[:, C_ONE:C_ONE + P]
        scanm = cst[:, C_SCAN:C_SCAN + HALF]

        def col(n):
            return cst[:, C_COL + n:C_COL + n + 1]

        def gs(b, g):
            return b[:, g * GRP:(g + 1) * GRP]

        def ck(b, c):
            return b[:, c * P:(c + 1) * P]

        def c4(ap):
            return ap.rearrange("p (c t) -> p c t", t=P)

        def per_chunk(cols, g):
            return cols[:, g * CPG:(g + 1) * CPG].unsqueeze(2).to_broadcast([P, CPG, P])

        def over_chunks(m):
            return m.unsqueeze(1).to_broadcast([P, CPG, m.shape[1]])

        KG, KGC, KB, KBG, KKD, KHB, KGE = range(7)

        N = Stages(nc, "n_", dict(
            const=64 + 128, xa=64, xb=64, sq=8, ln=1, r0=1, rs=1, newton=4, xs=8, tr=16, ht=16, ab=1, absb=1,
            gch=9, lbd=1, mask=1, gact=7, gcs=1, gtab=1, once=3, onceact=2))
        S = Stages(nc, "s_", dict(
            wh=16, wg=16, init=1, pF=2, pQ=2, pZ=2, pV=2, pGQ=2, pGK=2, pGV=2, pGZ=2, pGR=2,
            thF=2, thQ=2, thZ=2, v=2, lf=1, rawq=2, rawk=2, rawv=2, c0=3, thG=2, egr=2,
            qhat=2, zh=2, kh=1, cum=1, D=6, E=4, EF=2, EQ=1, EL=1, elast=1, M=4, MF=2, qe=1, kl=1,
            pA=6, att=6, pKL=2, klt=2, pDS=2, hs=8, pOH=2, sqh=2, oh=2, pNH=2, lnh=2, rh=2, h1=2, mixh=2, outh=16,
            conv=9, thc=3, c2=3, sqc=4, pN=4, lnc=4, rc=4, nrm=4, zg=2, dm=2, dx=4, dec=4,
            pKK=2, A=2, pAT=2, at=2, xy=2, eye=2, pP=12, P=12, pX=10, X=10, pY=12, Y=12,
            pKT=2, rk=2, kdec=2, pVT=2, rv=2, pWT=2, nw=2, pQK=2, qkd=2, qg=2,
            pVN=8, vn=8, pS=8, sg=8, pOG=2, og=2, sqg=2, pNG=2, lng=2, rg=2, g1=2, mixg=2, outg=16, save=1))

        bank_at = {key: ps[j % 6] for j, key in enumerate(RING)}
        block = ctx.enter_context(nc.Block())

        @block.sync
        def _(sp):
            sp.dma_start(cst[:], a["consts"]).then_inc(N.sem["const"], 16)
            sp.dma_start(arena[:, 0:M_N], a["masks"]).then_inc(N.sem["const"], 16)
            sp.dma_start(nw[:], a["norm_mix"]).then_inc(N.sem["const"], 16)
            sp.dma_start(onw[:], a["onorm"]).then_inc(N.sem["const"], 16)
            sp.dma_start(wab[:], a["w_ab"]).then_inc(N.sem["const"], 16)
            sp.dma_start(lbt[:], a["lb"]).then_inc(N.sem["const"], 16)
            sp.dma_start(agt[:, 0, :], a["a_log"].partition_broadcast(P)).then_inc(N.sem["const"], 16)
            sp.dma_start(agt[:, 1, :], a["dt_bias"].partition_broadcast(P)).then_inc(N.sem["const"], 16)
            for h in range(HEADS):
                sp.dma_start(PT[:, h, 3:15], a["conv_w"][:, h, :]).then_inc(N.sem["const"], 16)
            with sp.Fori(0, NHALF) as half:
                sp.wait_ge(S.sem["mixg"], half * (HEADS * 2))
                sp.nop(nofuse=True)
                sp.wait_ge(S.sem["save"], half * HEADS)
                sp.wait_ge(N.sem["mask"], 1)
                sp.nop(nofuse=True)
                for t in range(NC):
                    sp.dma_start(X8[:, t, :], a["x"][bass.ds(half * HALF + t * P, P), :])\
                        .then_inc(N.sem["xa" if t < 4 else "xb"], 16)
                with sp.Fori(0, HEADS) as head:
                    it = half * HEADS + head
                    sp.wait_ge(S.sem["pV"], it * 2)
                    sp.nop(nofuse=True)
                    sp.dma_start(WH[:], a["w_proj"][bass.ds(head, 1), :, 0:4].rearrange("h p b k c -> p (h b) k c"))\
                        .then_inc(S.sem["wh"], 16)
                    sp.wait_ge(S.sem["pGZ"], it * 2)
                    sp.nop(nofuse=True)
                    sp.dma_start(WG[:], a["w_proj"][bass.ds(head, 1), :, 4:8].rearrange("h p b k c -> p (h b) k c"))\
                        .then_inc(S.sem["wg"], 16)
                    t = S.engine(sp, it)
                    t.wait("mixh", 2)
                    t.hold()
                    sp.dma_start(a["mix"][bass.ds(head, 1), :, bass.ds(half * HALF, HALF)]
                                 .rearrange("h p t -> p (h t)"), H["o"][:]).then_inc(S.sem["outh"], 16)
                    t.wait("mixg", 2)
                    t.hold()
                    sp.dma_start(a["mix"][bass.ds(head + HEADS, 1), :, bass.ds(half * HALF, HALF)]
                                 .rearrange("h p t -> p (h t)"), OG[:]).then_inc(S.sem["outg"], 16)
            sp.wait_ge(S.sem["outh"], NHALF * HEADS * 16)
            sp.wait_ge(S.sem["outg"], NHALF * HEADS * 16)

        @block.gpsimd
        def _(pool):
            nc.gpsimd.memset(H["att"][:], 0.0).then_inc(N.sem["once"], 1)
            nc.gpsimd.memset(SALL[:], 0.0).then_inc(N.sem["once"], 1)
            nc.gpsimd.memset(HALOS[:], 0.0).then_inc(N.sem["once"], 1)
            with pool.Fori(0, NHALF * HEADS) as it:
                t = S.engine(pool, it)
                t.wait("cum", 1)
                for l in range(6):
                    d = H["d0" if l % 2 == 0 else "d1"]
                    if l >= 2:
                        t.wait("E", l - 1) if l < 5 else t.wait("E", 4)
                    if l < 4:
                        h = ATT_LEVELS[l]
                        v = "p (b w) -> p b w"
                        ci = H["cum"][:].rearrange(v, w=2 * h)
                        ref = ci[:, :, h - 1:h].to_broadcast([P, HALF // (2 * h), 2 * h])
                        out = d[:].rearrange(v, w=2 * h)
                    else:
                        w, at = (8, 3) if l == 4 else (P, P - 1)
                        if l == 5:
                            t.wait("E", 4)
                        ci = H["cum"][:].rearrange("p (b w) -> p b w", w=w)
                        ref = ci[:, :, at:at + 1].to_broadcast([P, HALF // w, w])
                        out = d[:].rearrange("p (b w) -> p b w", w=w)
                    t.done(nc.gpsimd.tensor_tensor(out, ci, ref, ALU.subtract), "D")
                for g in range(NG):
                    t.wait("dx", 2 * g + 1)
                    t.hold()
                    o = c4(gs(DECT, g))
                    t.done(nc.gpsimd.affine_select(out=o, in_=o, compare_op=ALU.is_ge, fill=0.0, base=0,
                                                   pattern=[[0, CPG], [1, P]], channel_multiplier=-1), "dec")
                    t.wait("dx", 2 * g + 2)
                    t.hold()
                    o = c4(gs(DEC, g))
                    t.done(nc.gpsimd.affine_select(out=o, in_=o, compare_op=ALU.is_gt, fill=0.0, base=0,
                                                   pattern=[[0, CPG], [-1, P]], channel_multiplier=1), "dec")
                for g in range(NG):
                    t.wait("nrm", g + 1)
                    t.wait("egr", 2)
                    t.wait("pOH", 2)
                    t.wait("qe", 1)
                    t.done(nc.gpsimd.tensor_tensor(gs(QG, g), gs(conv["q"], g), gs(EGR, g), ALU.mult), "qg")
                t.close()

        @block.scalar
        def _(act):
            A = nc.scalar.activation
            act.wait_ge(N.sem["const"], 192)
            act.wait_ge(N.sem["lbd"], 1)
            A(lbt[:, 0, :], lbt[:, 1, :], ACT.Exp).then_inc(N.sem["onceact"], 1)
            A(agt[:, 0, :], agt[:, 0, :], ACT.Exp).then_inc(N.sem["onceact"], 1)
            with act.Fori(0, NHALF) as half:
                n = N.engine(act, half)
                for t_ in range(NC):
                    if t_ % 4 == 0:
                        n.wait("xa" if t_ == 0 else "xb", 64)
                    if t_ >= 2:
                        n.wait("sq", t_ - 1)
                    n.done(A(hT[:, t_ % 2, :], X8[:, t_, :], ACT.Square, accum_out=ss[:, 0, t_:t_ + 1]), "sq")
                n.wait("sq", 8)
                n.done(A(ss[:, 1, :], ss[:, 0, :], ACT.Ln, scale=1.0 / D, bias=col(COL_EPS)), "ln")
                n.wait("ln", 1)
                n.done(A(ss[:, 2, :], ss[:, 1, :], ACT.Exp, scale=-0.5), "r0")
                n.wait("gch", 1)
                n.done(A(gtmp[:, 1], gtmp[:, 0], ACT.Abs), "gact")
                n.wait("gact", 1)
                n.done(A(gtmp[:, 1], gtmp[:, 1], ACT.Exp, scale=-1.0), "gact")
                n.wait("gact", 2)
                n.done(A(gtmp[:, 2], gtmp[:, 1], ACT.Ln, bias=cst[:, C_ONE:C_ONE + 1]), "gact")
                n.wait("absb", 1)
                n.done(A(gtmp[:, 3], gtmp[:, 4], ACT.Tanh, scale=0.5), "gact")
                n.wait("gch", 7)
                n.done(A(gtmp[:, 0], GT[:, KGC], ACT.Exp), "gact")
                n.done(A(GT[:, KGE], gtmp[:, 1], ACT.Exp), "gact")
                n.done(A(GT[:, KKD], gtmp[:, 2], ACT.Exp), "gact")
                with act.Fori(0, HEADS) as head:
                    t = S.engine(act, half * HEADS + head)
                    for g in range(NG):
                        t.wait("pF", g + 1)
                        t.done(A(gs(H["kh"], g), bank_at[("F", g)][:], ACT.Tanh, scale=0.5), "thF")
                    for g in range(NG):
                        t.wait("pQ", g + 1)
                        t.done(A(gs(H["e0"], g), bank_at[("Q", g)][:], ACT.Tanh, scale=0.5), "thQ")
                    for g in range(NG):
                        t.wait("pZ", g + 1)
                        t.done(A(gs(H["e1"], g), bank_at[("Z", g)][:], ACT.Tanh, scale=0.5), "thZ")
                    for g in range(NG):
                        t.wait("pV", g + 1)
                        t.done(A(gs(H["v"], g), bank_at[("V", g)][:], ACT.Copy), "v")
                    t.wait("init", 1)
                    t.wait("thF", 2)
                    t.wait("outg", 0)
                    t.done(A(H["lf"][:], H["kh"][:], ACT.Ln, scale=PC[:, 0:1], bias=PC[:, 1:2]), "lf")
                    for i, n_ in enumerate("qkv"):
                        for g in range(NG):
                            t.wait("pG" + n_.upper(), g + 1)
                            t.done(A(raw[n_][:, HALO + g * GRP:HALO + (g + 1) * GRP], bank_at[("G" + n_, g)][:],
                                     ACT.Copy), "raw" + n_)
                        t.wait("raw" + n_, 2)
                        t.done(A(conv[n_], raw[n_][:, 0:HALF], ACT.Copy, scale=PC[:, 3 + 4 * i:4 + 4 * i]), "c0")
                    t.wait("zh", 2)
                    for g in range(NG):
                        t.wait("pGZ", g + 1)
                        t.done(A(gs(tmp["q"], g), bank_at[("Gz", g)][:], ACT.Tanh, scale=0.5), "thG")
                    for g in range(NG):
                        t.wait("pGR", g + 1)
                        t.done(A(gs(EGR, g), bank_at[("GR", g)][:], ACT.Exp), "egr")
                    t.wait("qhat", 2)
                    for l, h in enumerate(ATT_LEVELS):
                        t.wait("D", l + 1)
                        if l >= 2:
                            t.wait("M", l - 1)
                        e = H["e0" if l % 2 == 0 else "e1"][:].rearrange("p (b w) -> p b w", w=2 * h)
                        d = H["d0" if l % 2 == 0 else "d1"][:].rearrange("p (b w) -> p b w", w=2 * h)
                        A(e[:, :, h:2 * h], d[:, :, h:2 * h], ACT.Exp, bias=col(COL_LNHQ))
                        t.done(A(e[:, :, 0:h], d[:, :, 0:h], ACT.Exp, scale=-1.0), "E")
                    t.wait("D", 5)
                    t.wait("M", 4)
                    t.done(A(H["e0"][:], H["d0"][:], ACT.Exp, bias=col(COL_LNHQ)), "EF")
                    t.done(A(H["e1"][:], H["d0"][:], ACT.Exp, scale=-1.0), "EF")
                    t.done(A(el[:], H["cum"][:].rearrange("p (c w) -> p c w", w=P)[:, :, P - 1], ACT.Exp), "elast")
                    t.done(A(H["qe"][:], H["cum"][:], ACT.Exp, bias=col(COL_LNHQ)), "EQ")
                    t.wait("D", 6)
                    t.done(A(H["kl"][:], H["d1"][:], ACT.Exp, scale=-1.0), "EL")
                    t.wait("conv", 9)
                    for g in range(NG):
                        t.wait("dm", g + 1)
                        t.done(A(gs(DECT, g), gs(DM, g), ACT.Exp), "dx")
                        t.done(A(gs(DEC, g), gs(DM, g), ACT.Exp, scale=-1.0), "dx")
                    t.wait("zg", 2)
                    for n_ in "qkv":
                        t.done(A(tmp[n_], conv[n_], ACT.Tanh, scale=0.5), "thc")
                    for i, n_ in enumerate("qk"):
                        t.wait("c2", i + 1)
                        for g in range(NG):
                            t.done(A(gs(tmp[n_], g), gs(conv[n_], g), ACT.Square), "sqc")
                    for g in range(NG):
                        t.wait("pKL", g + 1)
                        t.done(A(gs(H["klt"], g), bank_at[("KL", g)][:], ACT.Copy), "klt")
                    for i, n_ in enumerate("qk"):
                        for g in range(NG):
                            m = 2 * i + g
                            t.wait("pN", m + 1)
                            t.done(A(gs(tmp[n_], g), bank_at[("N", m)][:], ACT.Ln, bias=col(COL_EPS4)), "lnc")
                            t.wait("lnc", m + 1)
                            if i == 0:
                                A_ln = A(gs(tmp[n_], g), gs(tmp[n_], g), ACT.Exp, scale=-0.5, bias=col(COL_LNGQ))
                            else:
                                A_ln = A(gs(tmp[n_], g), gs(tmp[n_], g), ACT.Exp, scale=-0.5)
                            t.done(A_ln, "rc")
                    for g in range(NG):
                        t.wait("pOH", g + 1)
                        t.wait("outh", 0)
                        t.done(A(gs(H["o"], g), ps[6 + g][:], ACT.Copy), "oh")
                        t.done(A(gs(H["kh"], g), ps[6 + g][:], ACT.Square), "sqh")
                    for g in range(NG):
                        t.wait("pNH", g + 1)
                        t.done(A(gs(H["kh"], g), bank_at[("NH", g)][:], ACT.Ln, scale=1.0 / P, bias=col(COL_EPS)), "lnh")
                        t.wait("lnh", g + 1)
                        t.done(A(gs(H["kh"], g), gs(H["kh"], g), ACT.Exp, scale=-0.5), "rh")
                    for g in range(NG):
                        t.wait("pAT", g + 1)
                        t.done(A(gs(AT_, g), bank_at[("AT", g)][:], ACT.Copy), "at")
                    for l in range(6):
                        for g in range(NG):
                            t.wait("pP", 2 * l + g + 1)
                            t.done(A(gs(PP, g), bank_at[("P", l, g)][:], ACT.Copy), "P")
                    for g in range(NG):
                        t.wait("pWT", g + 1)
                        t.done(A(gs(NW, g), bank_at[("WT", g)][:], ACT.Copy, scale=-1.0), "nw")
                    for c in range(NC):
                        t.wait("pVN", c + 1)
                        t.done(A(VN[:, c % 2, :], bank_at[("VN", c)][:, 0:P], ACT.Copy), "vn")
                        if c % CPG == CPG - 1:
                            g = c // CPG
                            t.wait("pOG", g + 1)
                            t.done(A(gs(OG, g), ps[6 + g][:], ACT.Copy), "og")
                            t.done(A(gs(tmp["q"], g), ps[6 + g][:], ACT.Square), "sqg")
                    for g in range(NG):
                        t.wait("pNG", g + 1)
                        t.done(A(gs(tmp["k"], g), bank_at[("NG", g)][:], ACT.Ln, scale=1.0 / P, bias=col(COL_EPS)), "lng")
                        t.wait("lng", g + 1)
                        t.done(A(gs(tmp["k"], g), gs(tmp["k"], g), ACT.Exp, scale=-0.5), "rg")
                    t.close()

        @block.vector
        def _(dve):
            V = nc.vector
            dve.wait_ge(N.sem["const"], 192)
            once = [0]
            osem = nc.alloc_semaphore("once_dve")

            def link(ins):
                once[0] += 1
                ins.then_inc(osem, 1)
                dve.wait_ge(osem, once[0])

            V.tensor_tensor(lbt[:, 1, :], lbt[:, 1, :], lbt[:, 0, :], ALU.subtract).then_inc(N.sem["lbd"], 1)
            dve.wait_ge(N.sem["onceact"], 2)
            link(V.tensor_scalar(lbt[:, 0, :], lbt[:, 0, :], 1.0, None, ALU.add))
            link(V.reciprocal(lbt[:, 0, :], lbt[:, 0, :]))
            V.tensor_copy(msk[:], arena[:, 0:M_N]).then_inc(N.sem["mask"], 1)
            V.tensor_scalar(PT[:, :, 0], lbt[:, 0, :], -0.5, 0.5, ALU.mult, ALU.add)
            V.tensor_scalar(PT[:, :, 1], lbt[:, 0, :], 0.5, 0.5, ALU.mult, ALU.add)
            V.tensor_scalar(PT[:, :, 2], lbt[:, 0, :], 0.5, -0.5, ALU.mult, ALU.add)
            V.tensor_scalar(onw[:], onw[:], 0.5, None, ALU.mult)
            link(V.tensor_scalar(agt[:, 0, :], agt[:, 0, :], -1.0, None, ALU.mult))
            dve.wait_ge(N.sem["once"], 3)
            with dve.Fori(0, NHALF) as half:
                n = N.engine(dve, half)

                n.wait("r0", 1)
                V.tensor_scalar(ss[:, 3, :], ss[:, 0, :], 1.0 / D, EPS, ALU.mult, ALU.add)
                n.done(V.tensor_tensor(ss[:, 4, :], ss[:, 2, :], ss[:, 2, :], ALU.mult), "newton")
                n.wait("newton", 1)
                n.done(V.tensor_tensor(ss[:, 4, :], ss[:, 4, :], ss[:, 3, :], ALU.mult), "newton")
                n.wait("newton", 2)
                n.done(V.tensor_scalar(ss[:, 4, :], ss[:, 4, :], -0.5, 1.5, ALU.mult, ALU.add), "newton")
                n.wait("newton", 3)
                n.done(V.tensor_tensor(ss[:, 5, :], ss[:, 4, :], ss[:, 2, :], ALU.mult), "newton")
                n.wait("newton", 4)
                for t_ in range(NC):
                    n.done(V.tensor_scalar(X8[:, t_, :], X8[:, t_, :], ss[:, 5, t_:t_ + 1], None, ALU.mult), "xs")
                    if t_ >= 1:
                        for q in range(2):
                            ht_evac(nc, n, V, hT, nw, ps, t_ - 1, q)
                for q in range(2):
                    ht_evac(nc, n, V, hT, nw, ps, NC - 1, q)
                n.wait("ab", 1)
                abv = ps[7][:, 0:NC * 8].rearrange("p (c h) -> p c h", h=8)
                dt = agt[:, 1, :].unsqueeze(1).to_broadcast([P, NC, HEADS])
                na = agt[:, 0, :].unsqueeze(1).to_broadcast([P, NC, HEADS])

                def step(ins):
                    n.done(ins, "gch")
                    n.wait("gch", n.n["gch"])

                n.done(V.tensor_copy(gtmp[:, 4], abv[:, :, HEADS:2 * HEADS]), "absb")
                step(V.tensor_tensor(gtmp[:, 0], abv[:, :, 0:HEADS], dt, ALU.add))
                n.wait("gact", 3)
                step(V.scalar_tensor_tensor(gtmp[:, 0], gtmp[:, 0], 0.0, gtmp[:, 2], ALU.max, ALU.add))
                step(V.tensor_tensor(GT[:, KG], gtmp[:, 0], na, ALU.mult))
                n.wait("gact", 4)
                step(V.tensor_scalar(GT[:, KB], gtmp[:, 3], 0.5, 0.5, ALU.mult, ALU.add))
                step(V.tensor_scalar(GT[:, KHB], GT[:, KB], 0.5, None, ALU.mult))
                n.wait("gcs", 1)
                cs = ps[6][:, 0:2 * NC * HEADS].rearrange("p (k c h) -> p k c h", k=2, h=HEADS)
                V.tensor_copy(gtmp[:, 1], cs[:, 1])
                step(V.tensor_copy(GT[:, KGC], cs[:, 0]))
                step(V.tensor_tensor(gtmp[:, 2], gtmp[:, 1], GT[:, KGC], ALU.subtract))
                n.wait("gact", 7)
                step(V.tensor_tensor(GT[:, KBG], gtmp[:, 0], GT[:, KB], ALU.mult))
                step(V.tensor_scalar(GT[:, KB], GT[:, KB], -1.0, None, ALU.mult))
                n.hold()
                with dve.Fori(0, HEADS) as head:
                    t = S.engine(dve, half * HEADS + head)
                    t.hold()
                    V.tensor_copy(PC[:], PT[:, bass.ds(head, 1), :].rearrange("p h n -> p (h n)"))
                    V.tensor_copy(GC[:], GT[:, :, :, bass.ds(head, 1)].rearrange("p k c h -> p k (c h)"))
                    V.tensor_copy(SH[:, 0, :], SALL[:, 0, bass.ds(head, 1), :].rearrange("p h n -> p (h n)"))
                    V.tensor_copy(SG[:], SALL[:, 1, bass.ds(head, 1), :].rearrange("p h n -> p (h n)"))
                    for i, n_ in enumerate("qkv"):
                        V.tensor_copy(raw[n_][:, 0:HALO], HALOS[:, bass.ds(head, 1), i, :].rearrange("p h n -> p (h n)"))
                    t.done(V.tensor_copy(c4(GB), GT[:, KG, :, bass.ds(head, 1)].to_broadcast([P, NC, P])), "init")
                    for g in range(NG):
                        t.wait("thQ", g + 1)
                        t.done(V.scalar_tensor_tensor(gs(H["qh"], g), gs(H["e0"], g), 1.0, bank_at[("Q", g)][:],
                                                      ALU.add, ALU.mult), "qhat")
                    for g in range(NG):
                        t.wait("thZ", g + 1)
                        t.done(V.scalar_tensor_tensor(gs(H["zh"], g), gs(H["e1"], g), 1.0, bank_at[("Z", g)][:],
                                                      ALU.add, ALU.mult), "zh")
                    t.wait("init", 1)
                    t.wait("lf", 1)
                    t.done(V.tensor_tensor_scan(H["cum"][:], scanm, H["lf"][:], 0.0, ALU.mult, ALU.add), "cum")
                    t.done(V.tensor_scalar(H["kh"][:], H["kh"][:], PC[:, 2:3], PC[:, 0:1], ALU.mult, ALU.add), "kh")
                    t.wait("kh", 1)

                    def level(l):
                        h = ATT_LEVELS[l]
                        t.wait("E", l + 1)
                        if l >= 2:
                            t.wait("pA", l - 1)
                        v = lambda b: b[:].rearrange("p (b w) -> p b w", w=2 * h)
                        m, e = H[f"m{l % 2}"], H[f"e{l % 2}"]
                        V.tensor_tensor(v(m)[:, :, h:2 * h], v(H["qh"])[:, :, h:2 * h], v(e)[:, :, h:2 * h], ALU.mult)
                        t.done(V.tensor_tensor(v(m)[:, :, 0:h], v(H["kh"])[:, :, 0:h], v(e)[:, :, 0:h], ALU.mult), "M")

                    def att(l):
                        h = ATT_LEVELS[l]
                        t.wait("pA", l + 1)
                        if l:
                            t.wait("att", l)
                        out = H["att"][:].rearrange("p (b w) -> p b w", w=2 * h)[:, :, h:2 * h]
                        mk = msk[:, M_ATT + l * 64:M_ATT + (l + 1) * 64].unsqueeze(1).to_broadcast([P, NC, 64])
                        if h < 64:
                            mk = msk[:, M_ATT + l * 64:M_ATT + (l + 1) * 64].rearrange("p (b w) -> p b w", w=h)\
                                .unsqueeze(1).to_broadcast([P, NC, 64 // h, h])
                            out = H["att"][:].rearrange("p (c b w) -> p c b w", c=NC, w=2 * h)[:, :, :, h:2 * h]
                            src = bank_at[("A", l)][:].rearrange("p (c b w) -> p c b w", c=NC, w=h)
                        else:
                            src = bank_at[("A", l)][:].rearrange("p (b w) -> p b w", w=h)
                        t.hold()
                        t.done(V.copy_predicated(out, mk, src), "att")

                    def conv_taps(i):
                        n_ = "qkv"[i]
                        t.wait("c0", i + 1)
                        for j in range(1, TAPS):
                            t.done(V.scalar_tensor_tensor(conv[n_], raw[n_][:, j:j + HALF],
                                                          PC[:, 3 + 4 * i + j:4 + 4 * i + j], conv[n_],
                                                          ALU.mult, ALU.add), "conv")
                            t.wait("conv", 3 * i + j)

                    for g in range(NG):
                        t.wait("thG", g + 1)
                        t.done(V.scalar_tensor_tensor(gs(ZG, g), gs(tmp["q"], g), 1.0, bank_at[("Gz", g)][:],
                                                      ALU.add, ALU.mult), "zg")
                    level(0)
                    level(1)
                    conv_taps(0)
                    for g in range(NG):
                        t.wait("egr", g + 1)
                        t.done(V.tensor_tensor(c4(gs(DM, g)), c4(bank_at[("GR", g)][:]), per_chunk(GC[:, KGC], g),
                                               ALU.subtract), "dm")
                    att(0)
                    level(2)
                    att(1)
                    level(3)
                    conv_taps(1)
                    att(2)
                    att(3)
                    t.wait("EF", 2)
                    t.wait("pA", 4)
                    t.done(V.tensor_tensor(H["m0"][:], H["qh"][:], H["e0"][:], ALU.mult), "MF")
                    t.done(V.tensor_tensor(H["m1"][:], H["kh"][:], H["e1"][:], ALU.mult), "MF")
                    t.wait("EQ", 1)
                    t.done(V.tensor_tensor(H["qe"][:], H["qh"][:], H["qe"][:], ALU.mult), "qe")
                    t.wait("EL", 1)
                    t.done(V.tensor_tensor(H["kl"][:], H["kh"][:], H["kl"][:], ALU.mult), "kl")
                    conv_taps(2)
                    t.hold()
                    for i, n_ in enumerate("qkv"):
                        V.tensor_copy(HALOS[:, bass.ds(head, 1), i, :].rearrange("p h n -> p (h n)"),
                                      raw[n_][:, HALF:HALF + HALO])
                    for g in range(NG):
                        t.wait("pA", 5 + g)
                        t.wait("att", 4)
                        t.hold()
                        t.done(V.copy_predicated(c4(gs(H["att"], g)), over_chunks(msk[:, M_ATTF:M_ATTF + P]),
                                                 c4(bank_at[("AF", g)][:])), "att")
                    for i, n_ in enumerate("qkv"):
                        t.wait("thc", i + 1)
                        t.done(V.scalar_tensor_tensor(conv[n_], tmp[n_], 1.0, conv[n_], ALU.add, ALU.mult), "c2")
                    t.wait("elast", 1)
                    for c in range(NC):
                        t.wait("pDS", c // CPG + 1)
                        if c:
                            t.wait("hs", c)
                        t.done(V.scalar_tensor_tensor(SH[:, c + 1, :], SH[:, c, :], el[:, c:c + 1],
                                                      ck(bank_at[("DS", c // CPG)], c % CPG), ALU.mult, ALU.add), "hs")
                    for m in range(4):
                        t.wait("rc", m + 1)
                        b, g = conv["qk"[m // 2]], m % 2
                        t.done(V.tensor_tensor(gs(b, g), gs(b, g), gs(tmp["qk"[m // 2]], g), ALU.mult), "nrm")
                    for g in range(NG):
                        t.wait("rh", g + 1)
                        t.wait("oh", g + 1)
                        t.done(V.tensor_tensor(gs(H["o"], g), gs(H["o"], g), gs(H["kh"], g), ALU.mult), "h1")
                        t.wait("h1", g + 1)
                        t.done(V.scalar_tensor_tensor(gs(H["o"], g), gs(H["o"], g), onw[:, 0:1], gs(H["zh"], g),
                                                      ALU.mult, ALU.mult), "mixh")
                    for g in range(NG):
                        t.wait("pKK", g + 1)
                        t.wait("dec", 2 * g + 2)
                        for c in range(CPG * g, CPG * (g + 1)):
                            last = V.scalar_tensor_tensor(ck(A_, c), ck(bank_at[("KK", g)], c % CPG), GC[:, KB, c:c + 1],
                                                          ck(DEC, c), ALU.mult, ALU.mult)
                        t.done(last, "A")
                    for g in range(NG):
                        t.wait("pKT", g + 1)
                        kt = c4(bank_at[("KT", g)][:])
                        t.done(V.tensor_tensor(c4(gs(RK, g)), kt, per_chunk(GC[:, KBG], g), ALU.mult), "rk")
                        t.done(V.tensor_tensor(c4(gs(KDEC, g)), kt, per_chunk(GC[:, KKD], g), ALU.mult), "kdec")
                    for g in range(NG):
                        t.wait("pVT", g + 1)
                        t.done(V.tensor_tensor(c4(gs(RV, g)), c4(bank_at[("VT", g)][:]), per_chunk(GC[:, KHB], g),
                                               ALU.mult), "rv")
                    for g in range(NG):
                        t.wait("at", g + 1)
                        V.tensor_copy(c4(gs(X_, g)), over_chunks(ident))
                        t.done(V.tensor_copy(c4(gs(Y_, g)), over_chunks(ident)), "eye")
                        t.wait("eye", g + 1)
                        t.hold()
                        V.copy_predicated(c4(gs(X_, g)), over_chunks(msk[:, M_SOL:M_SOL + P]), c4(gs(A_, g)))
                        t.done(V.copy_predicated(c4(gs(Y_, g)), over_chunks(msk[:, M_SOLT:M_SOLT + P]),
                                                 c4(gs(AT_, g))), "xy")
                    for g in range(NG):
                        t.wait("pQK", g + 1)
                        t.wait("dec", 2 * g + 1)
                        t.done(V.tensor_tensor(gs(QKD, g), bank_at[("QK", g)][:], gs(DECT, g), ALU.mult), "qkd")
                    for l in range(6):
                        for g in range(NG):
                            if l < 5:
                                t.wait("pX", 2 * l + g + 1)
                                t.hold()
                                o = M_SOL + (l + 1) * P
                                t.done(V.copy_predicated(c4(gs(X_, g)), over_chunks(msk[:, o:o + P]),
                                                         c4(bank_at[("X", l, g)][:])), "X")
                            t.wait("pY", 2 * l + g + 1)
                            t.hold()
                            o = M_SOLT + (l + 1) * P
                            t.done(V.copy_predicated(c4(gs(Y_, g)), over_chunks(msk[:, o:o + P]),
                                                     c4(bank_at[("Y", l, g)][:])), "Y")
                    for c in range(NC):
                        t.wait("pS", c + 1)
                        t.done(V.scalar_tensor_tensor(SG[:], SG[:], GC[:, KGE, c:c + 1], bank_at[("S", c)][:, 0:P],
                                                      ALU.mult, ALU.add), "sg")
                    t.wait("sg", 8)
                    t.wait("hs", 8)
                    t.hold()
                    V.tensor_copy(SALL[:, 0, bass.ds(head, 1), :].rearrange("p h n -> p (h n)"), SH[:, NC, :])
                    t.done(V.tensor_copy(SALL[:, 1, bass.ds(head, 1), :].rearrange("p h n -> p (h n)"), SG[:]), "save")
                    for g in range(NG):
                        t.wait("rg", g + 1)
                        t.wait("og", g + 1)
                        t.done(V.tensor_tensor(gs(OG, g), gs(OG, g), gs(tmp["k"], g), ALU.mult), "g1")
                        t.wait("g1", g + 1)
                        t.done(V.scalar_tensor_tensor(gs(OG, g), gs(OG, g), onw[:, 1:2], gs(ZG, g),
                                                      ALU.mult, ALU.mult), "mixg")
                    t.wait("save", 1)
                    t.hold()
                    t.close()
                n.close()

        @block.tensor
        def _(pe):
            mm = nc.tensor.matmul
            pe.wait_ge(N.sem["const"], 192)
            with pe.Fori(0, NHALF) as half:
                n = N.engine(pe, half)
                for t_ in range(NC):
                    n.wait("xs", t_ + 1)
                    for q in range(2):
                        j = 2 * t_ + q
                        if j >= 6:
                            n.wait("ht", j - 5)
                        for k in range(4):
                            last = nc.tensor.transpose(ps[j % 6][:, k * P:(k + 1) * P],
                                                       X8[:, t_, (4 * q + k) * P:(4 * q + k + 1) * P], ident)
                        n.done(last, "tr")
                n.wait("ht", 16)
                for t_ in range(NC):
                    for k in range(KD):
                        last = mm(ps[7][:, t_ * 8:(t_ + 1) * 8], hT[:, k, t_ * P:(t_ + 1) * P], wab[:, k, :],
                                  start=(k == 0), stop=(k == KD - 1))
                n.done(last, "ab")
                n.wait("gch", 3)
                gv = GT[:, KG].rearrange("p c h -> p (c h)")
                w = NC * HEADS
                mm(ps[6][:, 0:w], UI, gv, start=True, stop=True)
                n.done(mm(ps[6][:, w:2 * w], ones, gv, start=True, stop=True), "gcs")
                n.wait("gch", 6)
                n.hold()
                with pe.Fori(0, HEADS) as head:
                    t = S.engine(pe, half * HEADS + head)
                    frees = []

                    def job(key, *free):
                        j = len(frees)
                        assert RING[j] == key, (RING[j], key)
                        if j >= 6:
                            t.wait(*frees[j - 6])
                        frees.append(free)
                        return ps[j % 6]

                    def project(W, b, g, out, stage):
                        for k in range(KD):
                            last = mm(out[:], W[:, b, k, :], hT[:, k, g * GRP:(g + 1) * GRP],
                                      start=(k == 0), stop=(k == KD - 1))
                        t.done(last, stage)

                    t.wait("wh", 16)
                    for b, (stage, free) in enumerate((("pF", "thF"), ("pQ", "qhat"), ("pZ", "zh"))):
                        for g in range(NG):
                            project(WH, b, g, job((stage[1:], g), free, g + 1), stage)
                    for g in range(NG):
                        out = job(("V", g), "v", g + 1)
                        for c in range(CPG):
                            s = (g * CPG + c) * P
                            for k in range(KD):
                                last = mm(out[:, c * P:(c + 1) * P], hT[:, k, s:s + P], WH[:, 3, k, :],
                                          start=(k == 0), stop=(k == KD - 1))
                        t.done(last, "pV")
                    t.wait("wg", 16)
                    for b, (stage, free) in enumerate((("pGQ", "rawq"), ("pGK", "rawk"), ("pGV", "rawv"), ("pGZ", "zg"))):
                        for g in range(NG):
                            project(WG, b, g, job(("G" + "qkvz"[b], g), free, g + 1), stage)
                    t.wait("init", 1)
                    for g in range(NG):
                        out = job(("GR", g), "dm", g + 1)
                        for c in range(CPG):
                            last = mm(ck(out, c), ck(GB, g * CPG + c), UI, start=True, stop=True)
                        t.done(last, "pGR")
                    for l, h in enumerate(ATT_LEVELS):
                        t.wait("M", l + 1)
                        out = job(("A", l), "att", l + 1)
                        m = H[f"m{l % 2}"]
                        for c in range(NC):
                            late = ck(m, c).rearrange("p (b w) -> p b w", w=2 * h)[:, :, h:2 * h]
                            last = mm(out[:, c * 64:(c + 1) * 64], ck(m, c), late, start=True, stop=True)
                        t.done(last, "pA")
                    t.wait("MF", 2)
                    for g in range(NG):
                        out = job(("AF", g), "att", 5 + g)
                        for c in range(CPG):
                            last = mm(ck(out, c), ck(H["m1"], g * CPG + c), ck(H["m0"], g * CPG + c), start=True, stop=True)
                        t.done(last, "pA")
                    t.wait("kl", 1)
                    for g in range(NG):
                        out = job(("KL", g), "klt", g + 1)
                        for c in range(CPG):
                            last = nc.tensor.transpose(ck(out, c), ck(H["kl"], g * CPG + c), ident)
                        t.done(last, "pKL")
                    for g in range(NG):
                        t.wait("klt", g + 1)
                        out = job(("DS", g), "hs", 4 * (g + 1))
                        for c in range(CPG):
                            last = mm(ck(out, c), ck(H["klt"], g * CPG + c), ck(H["v"], g * CPG + c), start=True, stop=True)
                        t.done(last, "pDS")
                    for i in range(2):
                        for g in range(NG):
                            t.wait("sqc", 2 * i + g + 1)
                            out = job(("N", 2 * i + g), "lnc", 2 * i + g + 1)
                            t.done(mm(out[:], ones, gs(tmp["qk"[i]], g), start=True, stop=True), "pN")
                    t.wait("att", 6)
                    t.wait("qe", 1)
                    for g in range(NG):
                        t.wait("hs", CPG * g + CPG - 1)
                        out = ps[6 + g]
                        for c in range(g * CPG, (g + 1) * CPG):
                            mm(ck(out, c % CPG), SH[:, c, :], ck(H["qe"], c), start=True, stop=False)
                            last = mm(ck(out, c % CPG), ck(H["v"], c), ck(H["att"], c), start=False, stop=True)
                        t.done(last, "pOH")
                    for g in range(NG):
                        t.wait("sqh", g + 1)
                        out = job(("NH", g), "lnh", g + 1)
                        t.done(mm(out[:], ones, gs(H["kh"], g), start=True, stop=True), "pNH")
                    t.wait("nrm", 4)
                    for g in range(NG):
                        out = job(("KK", g), "A", g + 1)
                        for c in range(CPG):
                            k_ = ck(conv["k"], g * CPG + c)
                            last = mm(ck(out, c), k_, k_, start=True, stop=True)
                        t.done(last, "pKK")
                    for stage, src, free, per in (("pKT", "k", "kdec", 1), ("pVT", "v", "rv", 1)):
                        t.wait("c2", 3)
                        for g in range(NG):
                            out = job((stage[1:], g), free, g + 1)
                            for c in range(CPG):
                                last = nc.tensor.transpose(ck(out, c), ck(conv[src], g * CPG + c), ident)
                            t.done(last, stage)
                    for g in range(NG):
                        t.wait("A", g + 1)
                        out = job(("AT", g), "at", g + 1)
                        for c in range(CPG):
                            last = nc.tensor.transpose(ck(out, c), ck(A_, g * CPG + c), ident)
                        t.done(last, "pAT")
                    for g in range(NG):
                        out = job(("QK", g), "qkd", g + 1)
                        for c in range(CPG):
                            last = mm(ck(out, c), ck(conv["k"], g * CPG + c), ck(conv["q"], g * CPG + c), start=True, stop=True)
                        t.done(last, "pQK")
                    for l in range(6):
                        for g in range(NG):
                            if l == 0:
                                t.wait("xy", g + 1)
                                t.wait("at", g + 1)
                            else:
                                t.wait("X", 2 * (l - 1) + g + 1)
                            out = job(("P", l, g), "P", 2 * l + g + 1)
                            for c in range(g * CPG, (g + 1) * CPG):
                                last = mm(ck(out, c % CPG), ck(AT_, c), ck(X_, c), start=True, stop=True)
                            t.done(last, "pP")
                        for g in range(NG):
                            t.wait("P", 2 * l + g + 1)
                            if l:
                                t.wait("Y", 2 * (l - 1) + g + 1)
                            if l < 5:
                                out = job(("X", l, g), "X", 2 * l + g + 1)
                                for c in range(g * CPG, (g + 1) * CPG):
                                    last = mm(ck(out, c % CPG), ck(Y_, c), ck(PP, c), start=True, stop=True)
                                t.done(last, "pX")
                            out = job(("Y", l, g), "Y", 2 * l + g + 1)
                            for c in range(g * CPG, (g + 1) * CPG):
                                last = mm(ck(out, c % CPG), ck(PP, c), ck(Y_, c), start=True, stop=True)
                            t.done(last, "pY")
                    for g in range(NG):
                        t.wait("rk", g + 1)
                        t.wait("Y", 10 + g + 1)
                        out = job(("WT", g), "nw", g + 1)
                        for c in range(g * CPG, (g + 1) * CPG):
                            last = mm(ck(out, c % CPG), ck(RK, c), ck(Y_, c), start=True, stop=True)
                        t.done(last, "pWT")
                    for c in range(NC):
                        g = c // CPG
                        if c % CPG == 0:
                            t.wait("rv", g + 1)
                            t.wait("nw", g + 1)
                            t.wait("kdec", g + 1)
                            t.wait("qkd", g + 1)
                            t.wait("qg", g + 1)
                        if c:
                            t.wait("sg", c)
                        out = job(("VN", c), "vn", c + 1)
                        mm(out[:, 0:P], ck(Y_, c), ck(RV, c), start=True, stop=False)
                        t.done(mm(out[:, 0:P], ck(NW, c), SG[:], start=False, stop=True), "pVN")
                        o = ck(ps[6 + g], c % CPG)
                        mm(o, SG[:], ck(QG, c), start=True, stop=False)
                        t.wait("vn", c + 1)
                        out = job(("S", c), "sg", c + 1)
                        t.done(mm(out[:, 0:P], ck(KDEC, c), VN[:, c % 2, :], start=True, stop=True), "pS")
                        last = mm(o, VN[:, c % 2, :], ck(QKD, c), start=False, stop=True)
                        if c % CPG == CPG - 1:
                            t.done(last, "pOG")
                    for g in range(NG):
                        t.wait("sqg", g + 1)
                        out = job(("NG", g), "lng", g + 1)
                        t.done(mm(out[:], ones, gs(tmp["q"], g), start=True, stop=True), "pNG")
                    t.wait("mixg", 2)
                    t.wait("save", 1)
                    t.hold()
                    t.close()
                n.close()


def ht_evac(nc, n, V, hT, nw, ps, t_, q):
    j = 2 * t_ + q
    n.wait("tr", j + 1)
    w = nw[:, 4 * q:4 * q + 4].unsqueeze(2).to_broadcast([P, 4, P])
    n.done(V.tensor_tensor(hT[:, 4 * q:4 * q + 4, t_ * P:(t_ + 1) * P],
                           ps[j % 6][:].rearrange("p (k t) -> p k t", t=P), w, ALU.mult), "ht")


def router(nc, a, pool_dma):
    with ExitStack() as ctx:
        def sb(name, *shape, dt=F32):
            return ctx.enter_context(nc.sbuf_tensor("r_" + name, [P, *shape], dt))

        cst = sb("cst", C_N)
        wo, wr = sb("wo", KD, D), sb("wr", KD, EPG + NE)
        wn = sb("wn", D)
        mixT = [sb(f"mixT{i}", KD, P) for i in range(2)]
        xt = [sb(f"xt{i}", D) for i in range(2)]
        xn = [sb(f"xn{i}", D) for i in range(2)]
        xnT = [sb(f"xnT{i}", KD, P) for i in range(2)]
        junk = sb("junk", D)
        st = sb("st", 2, 8)
        lg = sb("lg", 2, EPG + NE)
        rt = sb("rt", 32)
        m8, i8, i8b = sb("m8", 3, 8), sb("i8", 8, dt=U32), sb("i8b", 8, dt=U32)
        prod, esel = sb("prod", EPG, EPG), sb("esel", EPG)
        oh = sb("oh", 4, NE)
        cnt = sb("cnt", NE)
        tab = sb("tab", NT, 8)
        big = sb("big", NSLOT, NE)
        blk, base = sb("blk", 2, NE), sb("base", NE)
        ri = sb("ri", 3, 2 * NT, dt=I32)
        rf = sb("rf", 5, 2 * NT)
        pos, tok = sb("pos", 2, NT, dt=I32), sb("tok", 2, NT, dt=I32)
        slots = sb("slots", 2, NSLOT, dt=I32)
        sf = sb("sf", NSLOT)
        fill = sb("fill", NSLOT, dt=I32)
        ps = [ctx.enter_context(nc.psum_tensor(f"r_ps{i}", [P, GRP], F32)) for i in range(8)]
        ident, US, ones = cst[:, C_ID:C_ID + P], cst[:, C_US:C_US + P], cst[:, C_ONE:C_ONE + P]
        i64, i8c = cst[:, C_I64:C_I64 + NE], cst[:, C_I8:C_I8 + EPG]

        S = Stages(nc, "r_", dict(
            xt0=32, xt1=32, po=4, h=4, ln=2, r0=2, nt=8, sq=2, xn=2, hout=32, xnout=32,
            ptr=4, ev=4, plg=2, lg=2, v=52, pe=4, prk=2, cnt=2))
        once = Stages(nc, "r1_", dict(const=64, start=2, v=1, fillout=16, tabout=32))
        O = {**once.sem, "scat": pool_dma["r1_scat"]}
        block = ctx.enter_context(nc.Block())

        @block.sync
        def _(sp):
            sp.dma_start(cst[:], a["consts"]).then_inc(O["const"], 16)
            sp.dma_start(wo[:], a["w_out"]).then_inc(O["const"], 16)
            sp.dma_start(wr[:], a["w_router"]).then_inc(O["const"], 16)
            sp.dma_start(wn[:], a["norm_moe"].partition_broadcast(P)).then_inc(O["const"], 16)
            with sp.Fori(0, NT // 2) as j:
                t = S.engine(sp, j)
                for i in range(2):
                    rows = bass.ds((j * 2 + i) * P, P)
                    sp.wait_ge(S.sem["hout"], j * 32)
                    t.hold()
                    sp.wait_ge(S.sem["xn"], j * 2)
                    t.hold()
                    sp.wait_ge(S.sem["po"], j * 4)
                    t.hold()
                    sp.dma_start(mixT[i][:], a["mix"][:, :, rows].rearrange("k p t -> p k t")).then_inc(S.sem[f"xt{i}"], 16)
                    sp.dma_start(xt[i][:], a["x"][rows, :]).then_inc(S.sem[f"xt{i}"], 16)
            sp.wait_ge(O["start"], 1)
            sp.dma_start(a["rows_tab"].rearrange("(p n) -> p n", p=P), fill[:]).then_inc(O["fillout"], 16)
            sp.wait_ge(O["v"], TABLE_STEPS)
            sp.dma_start(a["slot_tab"], slots[0:1, :, :].rearrange("p k n -> p (k n)")).then_inc(O["tabout"], 16)
            sp.dma_start(a["gate_tab"], tab[:]).then_inc(O["tabout"], 16)
            sp.wait_ge(O["tabout"], 32)
            sp.wait_ge(O["fillout"], 16)
            sp.wait_ge(S.sem["hout"], NT * 16)
            sp.wait_ge(S.sem["xnout"], NT * 16)

        @block.gpsimd
        def _(pool):
            nc.gpsimd.memset(cnt[:], 0.0).then_inc(O["start"], 1)
            pool.wait_ge(O["fillout"], 16)
            pool.wait_ge(O["v"], TABLE_STEPS)
            for i in range(2):
                for n in range(NT):
                    pool.indirect_dma_start(
                        out=a["rows_tab"].rearrange("(n o) -> n o", o=1),
                        out_offset=bass.IndirectOffsetOnAxis(ap=pos[:, i, n:n + 1], axis=0),
                        in_=tok[:, i, n:n + 1], in_offset=None).then_inc(O["scat"], 16)
            pool.wait_ge(O["scat"], 512)

        @block.scalar
        def _(act):
            A = nc.scalar.activation
            act.wait_ge(O["const"], 64)
            with act.Fori(0, NT // 2) as j:
                t = S.engine(act, j)
                for i in range(2):
                    rows = bass.ds((j * 2 + i) * P, P)
                    t.wait("h", 2 * i + 2)
                    act.dma_start(a["h"][rows, :], xt[i][:]).then_inc(S.sem["hout"], 16)
                    if i:
                        t.wait("sq", 1)
                    else:
                        t.wait("sq", 0)
                    t.done(A(junk[:], xt[i][:], ACT.Square, accum_out=st[:, i, 0:1]), "sq")
                    t.wait("sq", i + 1)
                    t.done(A(st[:, i, 1:2], st[:, i, 0:1], ACT.Ln, scale=1.0 / D,
                             bias=cst[:, C_COL + COL_EPS:C_COL + COL_EPS + 1]), "ln")
                    t.wait("ln", i + 1)
                    t.done(A(st[:, i, 2:3], st[:, i, 1:2], ACT.Exp, scale=-0.5), "r0")
                    t.wait("xn", i + 1)
                    act.dma_start(a["xn"][rows, :], xn[i][:]).then_inc(S.sem["xnout"], 16)
                    for q in range(2):
                        t.wait("ptr", 2 * i + q + 1)
                        t.done(A(xnT[i][:, 4 * q:4 * q + 4, :].rearrange("p k t -> p (k t)"), ps[4 + q][:], ACT.Copy), "ev")
                    t.wait("v", 26 * i + 2)
                    t.done(A(rt[:, 8:16], lg[:, i, 0:EPG], ACT.Exp, bias=rt[:, 0:1], accum_out=rt[:, 1:2]), "pe")
                    t.wait("v", 26 * i + 10)
                    t.done(A(rt[:, 3:4], rt[:, 2:3], ACT.Exp), "pe")
                t.n["hout"] = t.n["xnout"] = 32
                t.close()

        @block.vector
        def _(dve):
            V = nc.vector
            dve.wait_ge(O["const"], 64)
            dve.wait_ge(O["start"], 1)
            V.memset(fill[:], OOB).then_inc(O["start"], 1)
            with dve.Fori(0, NT // 2) as j:
                t = S.engine(dve, j)

                def v(ins, hold=False):
                    t.done(ins, "v")
                    t.wait("v", t.n["v"])
                    if hold:
                        t.hold()

                for i in range(2):
                    t.wait(f"xt{i}", 32)
                    for q in range(2):
                        t.wait("po", 2 * i + q + 1)
                        hq = xt[i][:, q * GRP:(q + 1) * GRP]
                        t.done(V.tensor_tensor(hq, hq, ps[2 * i + q][:], ALU.add), "h")
                    t.wait("r0", i + 1)
                    y = lambda k: st[:, i, k:k + 1]
                    V.tensor_scalar(y(3), y(0), 1.0 / D, EPS, ALU.mult, ALU.add)
                    t.done(V.tensor_tensor(y(4), y(2), y(2), ALU.mult), "nt")
                    t.wait("nt", 4 * i + 1)
                    t.done(V.tensor_tensor(y(5), y(4), y(3), ALU.mult), "nt")
                    t.wait("nt", 4 * i + 2)
                    t.done(V.tensor_scalar(y(6), y(5), -0.5, 1.5, ALU.mult, ALU.add), "nt")
                    t.wait("nt", 4 * i + 3)
                    t.done(V.tensor_tensor(y(7), y(6), y(2), ALU.mult), "nt")
                    t.wait("nt", 4 * i + 4)
                    dve.wait_ge(S.sem["xnout"], j * 32)
                    t.done(V.scalar_tensor_tensor(xn[i][:], xt[i][:], y(7), wn[:], ALU.mult, ALU.mult), "xn")
                    t.wait("plg", i + 1)
                    t.done(V.tensor_copy(lg[:, i, :], ps[6][:, 0:EPG + NE]), "lg")
                    t.wait("lg", i + 1)
                    t.hold()
                    v(V.max(m8[:, 0], lg[:, i, 0:EPG]))
                    v(V.tensor_scalar(rt[:, 0:1], m8[:, 0, 0:1], -1.0, None, ALU.mult), hold=True)
                    v(V.max_index(i8[:], m8[:, 0], lg[:, i, 0:EPG]))
                    v(V.tensor_copy(rt[:, 4:5], i8[:, 0:1]))
                    v(V.tensor_scalar(m8[:, 2], i8c, rt[:, 4:5], None, ALU.is_equal))
                    v(V.tensor_tensor(prod[:], lg[:, i, EPG:].rearrange("p (g e) -> p e g", g=EPG),
                                      m8[:, 2].unsqueeze(1).to_broadcast([P, EPG, EPG]), ALU.mult))
                    v(V.tensor_reduce(esel[:], prod[:], AX.X, ALU.add), hold=True)
                    v(V.max(m8[:, 1], esel[:]), hold=True)
                    v(V.max_index(i8b[:], m8[:, 1], esel[:]))
                    v(V.tensor_tensor(rt[:, 2:3], m8[:, 1, 1:2], m8[:, 1, 0:1], ALU.subtract))
                    v(V.tensor_copy(rt[:, 16:18], i8b[:, 0:2]))
                    v(V.tensor_scalar(rt[:, 5:6], rt[:, 4:5], float(EPG), None, ALU.mult))
                    v(V.tensor_scalar(rt[:, 24:26], rt[:, 16:18], rt[:, 5:6], None, ALU.add))
                    v(V.tensor_scalar(oh[:, 0], i64, rt[:, 24:25], None, ALU.is_equal))
                    v(V.tensor_scalar(oh[:, 1], i64, rt[:, 25:26], None, ALU.is_equal))
                    v(V.tensor_tensor(oh[:, 2], oh[:, 0], oh[:, 1], ALU.add))
                    t.wait("pe", 2 * i + 2)
                    v(V.tensor_scalar(rt[:, 6:7], rt[:, 3:4], 1.0, rt[:, 1:2], ALU.add, ALU.mult))
                    v(V.reciprocal(rt[:, 28:29], rt[:, 6:7]))
                    v(V.tensor_tensor(rt[:, 29:30], rt[:, 28:29], rt[:, 3:4], ALU.mult))
                    t.wait("prk", i + 1)
                    v(V.tensor_tensor(oh[:, 3], ps[7][:, 0:NE], cnt[:], ALU.add))
                    v(V.tensor_tensor(oh[:, 0], oh[:, 0], oh[:, 3], ALU.mult))
                    v(V.tensor_reduce(rt[:, 26:27], oh[:, 0], AX.X, ALU.add))
                    v(V.tensor_tensor(oh[:, 1], oh[:, 1], oh[:, 3], ALU.mult))
                    v(V.tensor_reduce(rt[:, 27:28], oh[:, 1], AX.X, ALU.add))
                    t.done(V.tensor_tensor(cnt[:], ps[7][:, NE:2 * NE], cnt[:], ALU.add), "cnt")
                    t.wait("cnt", i + 1)
                    v(V.memset(rt[:, 30:32], 0.0), hold=True)
                    v(V.tensor_copy(tab[:, bass.ds(j * 2 + i, 1), :].rearrange("p n k -> p (n k)"), rt[:, 24:32]))
                t.close()
            n = [0]

            def w(ins):
                n[0] += 1
                ins.then_inc(O["v"], 1)
                dve.wait_ge(O["v"], n[0])

            w(V.tensor_scalar(blk[:, 0], cnt[:], 0.0, None, ALU.is_gt))
            for m in range(1, T // P):
                w(V.scalar_tensor_tensor(blk[:, m % 2], cnt[:], float(m * P), blk[:, 1 - m % 2], ALU.is_gt, ALU.add))
            nb, up = blk[:, (T // P - 1) % 2], blk[:, (T // P) % 2]
            w(V.tensor_tensor_scan(up, ones[:, 0:NE], nb, 0.0, ALU.mult, ALU.add))
            w(V.tensor_tensor(base[:], up, nb, ALU.subtract))
            w(V.tensor_tensor(big[:], up.unsqueeze(1).to_broadcast([P, NSLOT, NE]),
                              cst[:, C_SLOT:C_SLOT + NSLOT].unsqueeze(2).to_broadcast([P, NSLOT, NE]), ALU.is_le))
            w(V.tensor_reduce(sf[:], big[:], AX.X, ALU.add))
            w(V.tensor_scalar(sf[:], sf[:], float(NE - 1), None, ALU.min))
            w(V.tensor_copy(slots[:, 0], sf[:]))
            w(V.tensor_copy(slots[:, 1], up[:, NE - 1:NE].to_broadcast([P, NSLOT])))
            for i in range(2):
                sel = big[:, 0:NT, :]
                w(V.tensor_tensor(sel, i64.unsqueeze(1).to_broadcast([P, NT, NE]),
                                  tab[:, :, i:i + 1].to_broadcast([P, NT, NE]), ALU.is_equal))
                w(V.tensor_tensor(sel, sel, base[:].unsqueeze(1).to_broadcast([P, NT, NE]), ALU.mult))
                w(V.tensor_reduce(rf[:, 0, i * NT:(i + 1) * NT], sel, AX.X, ALU.add))
                w(V.tensor_copy(ri[:, 0, i * NT:(i + 1) * NT], tab[:, :, 2 + i]))
            w(V.tensor_scalar(ri[:, 1], ri[:, 0], 7, None, ALU.arith_shift_right))
            w(V.tensor_scalar(ri[:, 2], ri[:, 0], P - 1, None, ALU.bitwise_and))
            w(V.tensor_copy(rf[:, 1], ri[:, 1]))
            w(V.tensor_copy(rf[:, 2], ri[:, 2]))
            w(V.tensor_tensor(rf[:, 3], rf[:, 0], rf[:, 1], ALU.add))
            w(V.scalar_tensor_tensor(rf[:, 4], rf[:, 2], float(NSLOT), rf[:, 3], ALU.mult, ALU.add))
            w(V.tensor_copy(pos[:].rearrange("p i n -> p (i n)"), rf[:, 4]))
            w(V.tensor_copy(tok[:, 0], cst[:, C_TOK:C_TOK + NT]))
            w(V.tensor_scalar(tok[:, 1], cst[:, C_TOK:C_TOK + NT], float(T), None, ALU.add))
            assert n[0] == TABLE_STEPS

        @block.tensor
        def _(pe):
            mm = nc.tensor.matmul
            pe.wait_ge(O["const"], 64)
            with pe.Fori(0, NT // 2) as j:
                t = S.engine(pe, j)

                def out_proj(i):
                    t.wait(f"xt{i}", 32)
                    for q in range(2):
                        pe.wait_ge(S.sem["h"], j * 4 )
                        for k in range(KD):
                            last = mm(ps[2 * i + q][:], mixT[i][:, k, :], wo[:, k, q * GRP:(q + 1) * GRP],
                                      start=(k == 0), stop=(k == KD - 1))
                        t.done(last, "po")

                def route(i):
                    t.wait("xn", i + 1)
                    for q in range(2):
                        if i:
                            t.wait("ev", q + 1)
                        for k in range(4):
                            last = nc.tensor.transpose(ps[4 + q][:, k * P:(k + 1) * P],
                                                       xn[i][:, (4 * q + k) * P:(4 * q + k + 1) * P], ident)
                        t.done(last, "ptr")
                    t.wait("ev", 2 * i + 2)
                    if i:
                        t.wait("lg", 1)
                    for k in range(KD):
                        last = mm(ps[6][:, 0:EPG + NE], xnT[i][:, k, :], wr[:, k, :], start=(k == 0), stop=(k == KD - 1))
                    t.done(last, "plg")

                def ranks(i):
                    t.wait("v", 26 * i + 16)
                    mm(ps[7][:, 0:NE], US, oh[:, 2], start=True, stop=True)
                    t.done(mm(ps[7][:, NE:2 * NE], ones, oh[:, 2], start=True, stop=True), "prk")

                out_proj(0)
                out_proj(1)
                route(0)
                ranks(0)
                route(1)
                ranks(1)
                t.wait("cnt", 2)
                t.close()


def experts(nc, a, pool_dma):
    with ExitStack() as ctx:
        def sb(name, *shape, dt=F32):
            return ctx.enter_context(nc.sbuf_tensor("e_" + name, [P, *shape], dt))

        NB = 3
        KF = FF // P
        cst = sb("cst", P)
        rows, tok, late = sb("rows", NSLOT, dt=I32), sb("tok", NSLOT + NB, dt=I32), sb("late", NSLOT)
        gi = [sb(f"gi{i}", 1, dt=I32) for i in range(NB)]
        oi = [sb(f"oi{i}", 1, dt=I32) for i in range(NB)]
        slots = sb("slots", 2 * NSLOT, dt=I32)
        wg = [sb(f"wg{i}", KD, FF) for i in range(NB)]
        wu = [sb(f"wu{i}", KD, FF) for i in range(NB)]
        wd = [sb(f"wd{i}", KF, D) for i in range(NB)]
        xg = [sb(f"xg{i}", D) for i in range(NB)]
        xT = [sb(f"xT{i}", KD, P) for i in range(NB)]
        th, h = sb("th", FF), sb("h", FF)
        hT = sb("hT", KF, P)
        y = [sb(f"y{i}", D) for i in range(NB)]
        pgu = ctx.enter_context(nc.psum_tensor("e_gu", [P, 2 * FF], F32))
        px = [ctx.enter_context(nc.psum_tensor(f"e_px{i}", [P, GRP], F32)) for i in range(2)]
        ph = ctx.enter_context(nc.psum_tensor("e_ph", [P, GRP], F32))
        py = [ctx.enter_context(nc.psum_tensor(f"e_py{i}", [P, GRP], F32)) for i in range(2)]
        ident = cst[:]
        names = ["start", "zero", "tok", "gi", "oi", "px", "xT", "pgu", "th", "g", "h", "ph", "hT", "py", "y"] \
            + [f"{n}{i}" for i in range(NB) for n in ("w",)]
        E = {n: nc.alloc_semaphore("e_" + n) for n in names}
        E |= {n[2:]: sem for n, sem in pool_dma.items() if n.startswith("e_")}
        block = ctx.enter_context(nc.Block())

        @block.sync
        def _(sp):
            sp.dma_start(cst[:], a["consts"][:, C_ID:C_ID + P]).then_inc(E["start"], 16)
            sp.dma_start(rows[:], a["rows_tab"].rearrange("(p n) -> p n", p=P)).then_inc(E["start"], 16)
            sp.dma_start(slots[:], a["slot_tab"].rearrange("o n -> (o n)").partition_broadcast(P)).then_inc(E["start"], 16)
            sp.wait_ge(E["start"], 48)
            count = sp.value_load(slots[0:1, NSLOT:NSLOT + 1], min_val=1, max_val=NSLOT)
            with sp.Fori(0, NSLOT // NB) as j:
                for i in range(NB):
                    s = j * NB + i
                    with sp.If(s < count):
                        e = sp.value_load(slots[0:1, bass.ds(s, 1)], min_val=0, max_val=NE - 1)
                        sp.wait_ge(E[f"out{i}"], j * 16)
                        sp.nop(nofuse=True)
                        sp.dma_start(wg[i][:], a["w_gate"][bass.ds(e, 1)].rearrange("e (p k) f -> p (e k) f", k=KD))\
                            .then_inc(E[f"w{i}"], 16)
                        sp.dma_start(wu[i][:], a["w_up"][bass.ds(e, 1)].rearrange("e (p k) f -> p (e k) f", k=KD))\
                            .then_inc(E[f"w{i}"], 16)
                        sp.dma_start(wd[i][:], a["w_down"][bass.ds(e, 1)].rearrange("e (p k) d -> p (e k) d", k=KF))\
                            .then_inc(E[f"w{i}"], 16)

        @block.gpsimd
        def _(pool):
            for i in range(NB):
                last = nc.gpsimd.memset(xg[i][:], 0.0)
            last.then_inc(E["zero"], 1)
            pool.wait_ge(E["zero"], 1)
            pool.wait_ge(E["start"], 48)
            count = pool.value_load(slots[0:1, NSLOT:NSLOT + 1], min_val=1, max_val=NSLOT)
            pool.wait_ge(E["tok"], 2)

            def gather(n, i, turn):
                nc.gpsimd.tensor_copy(gi[i][:], tok[:, bass.ds(n, 1)]).then_inc(E["gi"], 1)
                pool.wait_ge(E["gi"], n + 1)
                pool.nop(nofuse=True)
                pool.indirect_dma_start(out=xg[i][:], out_offset=None, in_=a["xn"],
                                        in_offset=bass.IndirectOffsetOnAxis(ap=gi[i][:], axis=0),
                                        bounds_check=T - 1, oob_is_err=False).then_inc(E[f"x{i}"], 16)

            gather(0, 0, 0)
            with pool.If(count > 1):
                gather(1, 1, 0)
            with pool.Fori(0, NSLOT // NB) as j:
                for i in range(NB):
                    s = j * NB + i
                    with pool.If(s + 2 < count):
                        pool.wait_ge(E["px"], 2 * s)
                        pool.nop(nofuse=True)
                        gather(s + 2, (i + 2) % NB, j)
                    with pool.If(s < count):
                        pool.wait_ge(E[f"out{i}"], j * 16)
                        pool.nop(nofuse=True)
                        nc.gpsimd.tensor_copy(oi[i][:], rows[:, bass.ds(s, 1)]).then_inc(E["oi"], 1)
                        pool.wait_ge(E["oi"], s + 1)
                        pool.nop(nofuse=True)
                        pool.wait_ge(E["y"], 2 * s + 2)
                        pool.nop(nofuse=True)
                        pool.indirect_dma_start(out=a["y"], in_=y[i][:], in_offset=None,
                                                out_offset=bass.IndirectOffsetOnAxis(ap=oi[i][:], axis=0),
                                                bounds_check=2 * T - 1, oob_is_err=False).then_inc(E[f"out{i}"], 16)
            for i in range(NB):
                pool.wait_ge(E[f"out{i}"], ((count + (NB - 1 - i)) // NB) * 16)
                pool.nop(nofuse=True)

        @block.scalar
        def _(act):
            A = nc.scalar.activation
            act.wait_ge(E["start"], 48)
            count = act.value_load(slots[0:1, NSLOT:NSLOT + 1], min_val=1, max_val=NSLOT)
            with act.Fori(0, NSLOT // NB) as j:
                for i in range(NB):
                    s = j * NB + i
                    with act.If(s < count):
                        act.wait_ge(E["px"], 2 * s + 1)
                        A(xT[i][:, 0:4, :].rearrange("p k t -> p (k t)"), px[0][:], ACT.Copy).then_inc(E["xT"], 1)
                        act.wait_ge(E["pgu"], s + 1)
                        act.wait_ge(E["h"], s)
                        A(th[:], pgu[:, 0:FF], ACT.Tanh, scale=0.5).then_inc(E["th"], 1)
                        act.wait_ge(E["ph"], s + 1)
                        A(hT[:].rearrange("p k t -> p (k t)"), ph[:, 0:FF], ACT.Copy, scale=0.5).then_inc(E["hT"], 1)
                        act.wait_ge(E["py"], 2 * s + 1)
                        act.wait_ge(E[f"out{i}"], j * 16)
                        A(y[i][:, 0:GRP], py[0][:], ACT.Copy).then_inc(E["y"], 1)

        @block.vector
        def _(dve):
            V = nc.vector
            dve.wait_ge(E["start"], 48)
            V.tensor_scalar(late[:], rows[:], float(T), -float(T), ALU.is_ge, ALU.mult).then_inc(E["tok"], 1)
            dve.wait_ge(E["tok"], 1)
            V.tensor_tensor(tok[:, 0:NSLOT], rows[:], late[:], ALU.add).then_inc(E["tok"], 1)
            count = dve.value_load(slots[0:1, NSLOT:NSLOT + 1], min_val=1, max_val=NSLOT)
            with dve.Fori(0, NSLOT // NB) as j:
                for i in range(NB):
                    s = j * NB + i
                    with dve.If(s < count):
                        dve.wait_ge(E["px"], 2 * s + 2)
                        V.tensor_copy(xT[i][:, 4:8, :].rearrange("p k t -> p (k t)"), px[1][:]).then_inc(E["xT"], 1)
                        dve.wait_ge(E["th"], s + 1)
                        V.scalar_tensor_tensor(th[:], th[:], 1.0, pgu[:, 0:FF], ALU.add, ALU.mult).then_inc(E["g"], 1)
                        dve.wait_ge(E["g"], s + 1)
                        dve.wait_ge(E["ph"], s)
                        V.tensor_tensor(h[:], th[:], pgu[:, FF:2 * FF], ALU.mult).then_inc(E["h"], 1)
                        dve.wait_ge(E["py"], 2 * s + 2)
                        dve.wait_ge(E[f"out{i}"], j * 16)
                        V.tensor_copy(y[i][:, GRP:D], py[1][:]).then_inc(E["y"], 1)

        @block.tensor
        def _(pe):
            mm = nc.tensor.matmul
            pe.wait_ge(E["start"], 48)
            count = pe.value_load(slots[0:1, NSLOT:NSLOT + 1], min_val=1, max_val=NSLOT)
            with pe.Fori(0, NSLOT // NB) as j:
                for i in range(NB):
                    s = j * NB + i
                    with pe.If(s < count):
                        pe.wait_ge(E[f"x{i}"], (j + 1) * 16)
                        xv = xg[i][:].rearrange("t (p k) -> t k p", k=KD)
                        pe.wait_ge(E["xT"], 2 * s)
                        for q in range(2):
                            for k in range(4):
                                last = nc.tensor.transpose(px[q][:, k * P:(k + 1) * P], xv[:, 4 * q + k, :], ident)
                            last.then_inc(E["px"], 1)
                        pe.wait_ge(E[f"w{i}"], (j + 1) * 48)
                        pe.wait_ge(E["xT"], 2 * s + 2)
                        for q, w in enumerate((wg[i], wu[i])):
                            for k in range(KD):
                                last = mm(pgu[:, q * FF:(q + 1) * FF], xT[i][:, k, :], w[:, k, :],
                                          start=(k == 0), stop=(k == KD - 1))
                        last.then_inc(E["pgu"], 1)
                        pe.wait_ge(E["h"], s + 1)
                        hv = h[:].rearrange("t (p k) -> t k p", k=KF)
                        for k in range(KF):
                            last = nc.tensor.transpose(ph[:, k * P:(k + 1) * P], hv[:, k, :], ident)
                        last.then_inc(E["ph"], 1)
                        pe.wait_ge(E["hT"], s + 1)
                        pe.wait_ge(E["y"], 2 * s)
                        for q in range(2):
                            for k in range(KF):
                                last = mm(py[q][:], hT[:, k, :], wd[i][:, k, q * GRP:(q + 1) * GRP],
                                          start=(k == 0), stop=(k == KF - 1))
                            last.then_inc(E["py"], 1)


def combine(nc, a, pool_dma):
    with ExitStack() as ctx:
        def sb(name, *shape, dt=F32):
            return ctx.enter_context(nc.sbuf_tensor("c_" + name, [P, *shape], dt))

        NB = 4
        tab = sb("tab", NT, 8)
        wn, eps = sb("wn", D), sb("eps", 4)
        ht = [sb(f"ht{i}", D) for i in range(NB)]
        yt = [sb(f"y{i}", 2, D) for i in range(NB)]
        junk, st = sb("junk", D), sb("st", NT, 8)
        names = ["start", "s1", "s2", "sq", "ln", "r0", "nt", "o"] + [f"{n}{i}" for i in range(NB) for n in ("h", "y", "out")]
        E = {n: nc.alloc_semaphore("c_" + n) for n in names}
        block = ctx.enter_context(nc.Block())

        @block.sync
        def _(sp):
            sp.dma_start(tab[:], a["gate_tab"]).then_inc(E["start"], 16)
            sp.dma_start(wn[:], a["final_norm"].partition_broadcast(P)).then_inc(E["start"], 16)
            sp.dma_start(eps[:], a["consts"][:, C_COL:C_COL + 4]).then_inc(E["start"], 16)
            for t in range(NT):
                i = t % NB
                if t >= NB:
                    sp.wait_ge(E[f"out{i}"], 16 * (t // NB))
                sp.dma_start(ht[i][:], a["h"][t * P:(t + 1) * P, :]).then_inc(E[f"h{i}"], 16)
                if t >= NB:
                    sp.wait_ge(E["s2"], t - NB + 1)
                sp.dma_start(yt[i][:], a["y"].rearrange("(k n p) d -> n p k d", k=2, p=P)[t]).then_inc(E[f"y{i}"], 16)

        @block.vector
        def _(dve):
            V = nc.vector
            dve.wait_ge(E["start"], 48)

            def norm(t):
                i = t % NB
                y = lambda k: st[:, t, k:k + 1]
                dve.wait_ge(E["r0"], t + 1)
                V.tensor_scalar(y(3), y(0), 1.0 / D, EPS, ALU.mult, ALU.add)
                V.tensor_tensor(y(4), y(2), y(2), ALU.mult).then_inc(E["nt"], 1)
                dve.wait_ge(E["nt"], 4 * t + 1)
                V.tensor_tensor(y(5), y(4), y(3), ALU.mult).then_inc(E["nt"], 1)
                dve.wait_ge(E["nt"], 4 * t + 2)
                V.tensor_scalar(y(6), y(5), -0.5, 1.5, ALU.mult, ALU.add).then_inc(E["nt"], 1)
                dve.wait_ge(E["nt"], 4 * t + 3)
                V.tensor_tensor(y(7), y(6), y(2), ALU.mult).then_inc(E["nt"], 1)
                dve.wait_ge(E["nt"], 4 * t + 4)
                V.scalar_tensor_tensor(ht[i][:], ht[i][:], y(7), wn[:], ALU.mult, ALU.mult).then_inc(E["o"], 1)

            for t in range(NT):
                i = t % NB
                dve.wait_ge(E[f"h{i}"], 16 * (t // NB + 1))
                dve.wait_ge(E[f"y{i}"], 16 * (t // NB + 1))
                V.scalar_tensor_tensor(ht[i][:], yt[i][:, 0], tab[:, t, 4:5], ht[i][:], ALU.mult, ALU.add)\
                    .then_inc(E["s1"], 1)
                dve.wait_ge(E["s1"], t + 1)
                V.scalar_tensor_tensor(ht[i][:], yt[i][:, 1], tab[:, t, 5:6], ht[i][:], ALU.mult, ALU.add)\
                    .then_inc(E["s2"], 1)
                if t:
                    norm(t - 1)
            norm(NT - 1)

        @block.scalar
        def _(act):
            A = nc.scalar.activation
            act.wait_ge(E["start"], 48)
            for t in range(NT):
                i = t % NB
                act.wait_ge(E["s2"], t + 1)
                if t:
                    act.wait_ge(E["sq"], t)
                A(junk[:], ht[i][:], ACT.Square, accum_out=st[:, t, 0:1]).then_inc(E["sq"], 1)
                act.wait_ge(E["sq"], t + 1)
                A(st[:, t, 1:2], st[:, t, 0:1], ACT.Ln, scale=1.0 / D, bias=eps[:, COL_EPS:COL_EPS + 1]).then_inc(E["ln"], 1)
                act.wait_ge(E["ln"], t + 1)
                A(st[:, t, 2:3], st[:, t, 1:2], ACT.Exp, scale=-0.5).then_inc(E["r0"], 1)
                if t:
                    act.wait_ge(E["o"], t)
                    act.dma_start(a["out"][(t - 1) * P:t * P, :], ht[(t - 1) % NB][:]).then_inc(E[f"out{(t - 1) % NB}"], 16)
            act.wait_ge(E["o"], NT)
            act.dma_start(a["out"][(NT - 1) * P:, :], ht[(NT - 1) % NB][:]).then_inc(E[f"out{(NT - 1) % NB}"], 16)
            for i in range(NB):
                act.wait_ge(E[f"out{i}"], 16 * NT // NB)


def build(nc, a):
    pool_dma = {n: nc.alloc_semaphore(n) for n in ("r1_scat", "e_x0", "e_x1", "e_x2", "e_out0", "e_out1", "e_out2")}
    for part in (trunk, router, experts, combine):
        before = set(nc.free_semaphores)
        part(nc, a, pool_dma)
        if part is not combine:
            nc.clear_and_free_semaphores(sorted(before - set(nc.free_semaphores)))
            nc.all_engine_barrier()


TABLE_STEPS = 40

SCRATCH = {
    "mix": ((2 * HEADS, P, T), F32), "h": ((T, D), F32), "xn": ((T, D), F32), "y": ((2 * T, D), F32),
    "rows_tab": ((P * NSLOT,), I32), "slot_tab": ((1, 2 * NSLOT), I32),     "gate_tab": ((P, NT, 8), F32),
}



def layout(x, norm_mix_w, w_in, hgrn_lb_logits, hgrn_onorm_w, gdn_conv_w, gdn_a_log, gdn_dt_bias,
           gdn_onorm_w, w_out, norm_moe_w, router_group_w, router_expert_w, expert_w_gate,
           expert_w_up, expert_w_down, final_norm_w):
    asc = np.ascontiguousarray
    w = np.asarray(w_in)[0]
    starts = [512, 0, 1536, 1024, 2048, 2560, 3072, 3584]
    blocks = np.stack([w[:, s:s + 512].reshape(KD, P, HEADS, P) for s in starts])
    consts, masks = constant_tables()
    return {
        "consts": consts, "masks": masks,
        "x": asc(np.asarray(x)[0]),
        "norm_mix": asc(np.asarray(norm_mix_w)[0].reshape(KD, P).T),
        "onorm": asc(np.stack([np.asarray(hgrn_onorm_w)[0], np.asarray(gdn_onorm_w)[0]], 1)),
        "w_proj": asc(blocks.transpose(3, 2, 0, 1, 4)),
        "w_ab": asc(w[:, 4096:4104].reshape(KD, P, 8).transpose(1, 0, 2)),
        "lb": asc(np.asarray(hgrn_lb_logits).reshape(2, HEADS, P).transpose(2, 0, 1)),
        "a_log": asc(np.asarray(gdn_a_log)[0]), "dt_bias": asc(np.asarray(gdn_dt_bias)[0]),
        "conv_w": asc(np.asarray(gdn_conv_w)[0].reshape(TAPS, 3, HEADS, P).transpose(3, 2, 1, 0)
                      .reshape(P, HEADS, 3 * TAPS)),
        "w_out": asc(np.asarray(w_out)[0].reshape(KD, P, D).transpose(1, 0, 2)),
        "norm_moe": asc(np.asarray(norm_moe_w)[0]), "final_norm": asc(np.asarray(final_norm_w)),
        "w_router": asc(np.concatenate([np.asarray(router_group_w)[0], np.asarray(router_expert_w)[0]], 1)
                        .reshape(KD, P, 72).transpose(1, 0, 2)),
        "w_gate": np.asarray(expert_w_gate)[0], "w_up": np.asarray(expert_w_up)[0],
        "w_down": np.asarray(expert_w_down)[0],
    }


def kernel(**inputs):
    import concourse.bacc as bacc
    from concourse.bass_utils import run_bass_kernel_spmd

    nc = bacc.Bacc("TRN2", target_bir_lowering=False, num_devices=1)
    arrays = layout(**inputs)
    a = {n: nc.dram_tensor("in_" + n, v.shape, mybir.dt.from_np(v.dtype), kind="ExternalInput").ap()
         for n, v in arrays.items()}
    for n, (shape, dt) in SCRATCH.items():
        a[n] = nc.dram_tensor("tmp_" + n, shape, dt).ap()
    a["out"] = nc.dram_tensor("out", (T, D), F32, kind="ExternalOutput").ap()
    build(nc, a)
    r = run_bass_kernel_spmd(nc, [{"in_" + n: v for n, v in arrays.items()}], core_ids=[0])
    return r.results[0]["out"].reshape(1, T, D)
```

```python
import math
from contextlib import ExitStack

import numpy as np

import concourse.bass as bass
from concourse import mybir

F32 = mybir.dt.float32
I32 = mybir.dt.int32
U32 = mybir.dt.uint32
U8 = mybir.dt.uint8
F32R = mybir.dt.float32r
ALU = mybir.AluOpType
ACT = mybir.ActivationFunctionType
AX = mybir.AxisListType

P = 128
T = 2048
D = 1024
KD = D // P
HEADS = 4
HALF = 1024
NHALF = T // HALF
NC = HALF // P
GRP = 512
NG = HALF // GRP
CPG = GRP // P
TAPS = 4
HALO = TAPS - 1
EPS = 1e-6
NE = 64
EPG = 8
FF = 256
NT = T // P
NSLOT = 96
EB = 4
OOB = 1 << 20
ATT_LEVELS = (64, 32, 16, 8)
SOLVE_LEVELS = (1, 2, 4, 8, 16, 32, 64)

C_ID, C_UI, C_US, C_ONE, C_SCAN = 0, 128, 256, 384, 512
C_I64 = C_SCAN + HALF
C_I8 = C_I64 + 64
C_SLOT = C_I8 + 8
C_COL = C_SLOT + P
COL_EPS, COL_EPS4, COL_LNHQ, COL_LNGQ = range(4)
C_TOK = C_COL + 4
C_N = C_TOK + NT
M_SOL = 0
M_SOLT = M_SOL + 7 * 64
M_ATTF = M_SOLT + 7 * 64
M_N = M_ATTF + P


def constant_tables():
    c = np.zeros((P, C_N), np.float32)
    i = np.arange(P)
    c[:, C_ID:C_ID + P] = np.eye(P)
    c[:, C_UI:C_UI + P] = i[:, None] <= i[None, :]
    c[:, C_US:C_US + P] = i[:, None] < i[None, :]
    c[:, C_ONE:C_ONE + P] = 1.0
    c[:, C_SCAN:C_SCAN + HALF] = (np.arange(HALF) % P != 0)[None, :]
    c[:, C_I64:C_I64 + 64] = np.arange(64)[None, :]
    c[:, C_I8:C_I8 + 8] = np.arange(8)[None, :]
    c[:, C_SLOT:C_SLOT + P] = np.arange(P)[None, :]
    c[:, C_COL + COL_EPS] = EPS
    c[:, C_COL + COL_EPS4] = 4 * EPS
    c[:, C_COL + COL_LNHQ] = math.log(0.5 * P ** -0.5)
    c[:, C_COL + COL_LNGQ] = math.log(P ** -0.5)
    c[:, C_TOK:C_TOK + NT] = i[:, None] + P * np.arange(NT)[None, :]
    m = np.zeros((P, M_N), np.float32)
    for l, h in enumerate(SOLVE_LEVELS):
        early = i[i // h % 2 == 0]
        late = early + h
        m[:, M_SOL + l * 64:M_SOL + (l + 1) * 64] = i[:, None] // h == early[None, :] // h + 1
        m[:, M_SOLT + l * 64:M_SOLT + (l + 1) * 64] = i[:, None] // h == late[None, :] // h - 1
    m[:, M_ATTF:M_ATTF + P] = (i[:, None] // 8 == i[None, :] // 8) & (i[:, None] <= i[None, :])
    return c, m


def psum_banks():
    pair = lambda *names: [((n, g), None) for n in names for g in range(NG)]
    level = lambda l: [(("A", l, g), None) for g in range(NG)]
    solve = lambda l: [(("P", l, 0), None)] + [(("XT", l - 1, g), None) for g in range(NG if l else 0)] + \
        [(("P", l, 1), None)] + [(("X" if l < 5 else "Y", l, g), None) for g in range(NG)]
    jobs = pair("F", "Q", "Z") + level(0) + level(1) + pair("V") + level(2) + level(3)
    jobs += pair("Gq", "KL", "AF", "DS", "Gk", "GR")
    jobs += [(("OH", g), 6 + g) for g in range(NG)] + [(("Gv", 0), None)]
    jobs += pair("NH") + [(("N", m), None) for m in range(4)] + [(("Gv", 1), 7)] + pair("KK", "KT", "AT")
    for l in range(5):
        jobs += solve(l)
    jobs += pair("VT", "QK") + solve(5) + pair("WT")
    jobs += [(("OG", g), 6 + g) for g in range(NG)] + [(("Gz", g), 4 + g) for g in range(NG)]
    for c in range(NC):
        jobs += [(("VN", c), c % 2), (("S", c), 2 + c % 2)]
    jobs += [(("NG", g), g) for g in range(NG)]
    bank, free = {}, 0
    for key, b in jobs:
        bank[key] = free % 6 if b is None else b
        free += b is None
    return bank


BANK = psum_banks()


class Stages:

    def __init__(self, nc, prefix, per, given={}):
        self.per = per
        self.sem = {n: given.get(prefix + n) or nc.alloc_semaphore(prefix + n) for n in per}

    def engine(self, eng, turn=0):
        return Turn(self, eng, turn)


class Turn:

    def __init__(self, stages, eng, turn):
        self.s, self.eng, self.turn, self.n, self.seen = stages, eng, turn, {}, {}

    def wait(self, name, count):
        if count > self.seen.get(name, -1):
            self.seen[name] = count
            self.eng.wait_ge(self.s.sem[name], self.turn * self.s.per[name] + count)

    def wait_last(self, name):
        with self.eng.If(self.turn > 0):
            self.eng.wait_ge(self.s.sem[name], self.turn * self.s.per[name])
            self.eng.nop(nofuse=True)

    def hold(self):
        self.eng.nop(nofuse=True)

    def done(self, ins, name, by=1):
        self.n[name] = self.n.get(name, 0) + by
        ins.then_inc(self.s.sem[name], by)

    def close(self):
        for name, n in self.n.items():
            assert n == self.s.per[name], (name, n, self.s.per[name])


def trunk(nc, a, pool_dma, kept):
    with ExitStack() as ctx:
        def sb(name, *shape, dt=F32):
            return ctx.enter_context(nc.sbuf_tensor(name, [P, *shape], dt))

        cst, msk = sb("cst", C_N), sb("msk", M_N, dt=U8)
        hT = sb("hT", KD, HALF)
        WH = sb("WH", 4, KD, P)
        WG = sb("WG", 4, KD, P)
        H = {n: sb("h_" + n, HALF) for n in
             ("kh", "cum", "qh", "zh", "v", "d0", "d1", "e0", "e1", "m0", "m1", "att", "qe", "kl", "klt", "o", "lf")}
        SH = sb("SH", NC + 1, P)
        arena = sb("arena", 12 * (HALF + HALO))
        G = {n: arena[:, i * (HALF + HALO):(i + 1) * (HALF + HALO)] for i, n in enumerate(
            ("rq", "rk", "rv", "cq", "ck", "cv", "tq", "tk", "tv", "zg", "gb", "egr"))}
        X8 = arena[:, 0:NC * D].rearrange("p (t d) -> p t d", t=NC)
        raw = {n: G["r" + n] for n in "qkv"}
        conv = {n: G["c" + n][:, 0:HALF] for n in "qkv"}
        tmp = {n: G["t" + n][:, 0:HALF] for n in "qkv"}
        ZG, GB, EGR = (G[n][:, 0:HALF] for n in ("zg", "gb", "egr"))
        DM, DEC, DECT = (raw[n][:, 0:HALF] for n in "qkv")
        A_, AT_, X_, Y_, PP = (H[n] for n in ("d0", "d1", "e0", "e1", "m0"))
        RK, RV, KDEC, NW, QKD, QG = (H[n] for n in ("m1", "qe", "kl", "klt", "cum", "d0"))
        OG = H["lf"]
        SG = sb("SG", P)
        VN = sb("VN", 2, P)
        HALOS = sb("HALOS", HEADS, 3, HALO)
        SALL = sb("SALL", 2, HEADS, P)
        PT = sb("PT", HEADS, 15)
        PC = sb("PC", 15)
        GT = sb("GT", 7, NC, HEADS)
        GC = sb("GC", 7, NC)
        nw, onw = sb("nw", KD), sb("onw", 2)
        wab = sb("wab", KD, 8)
        lbt = sb("lbt", 2, HEADS)
        agt = sb("agt", 2, HEADS)
        ss = sb("ss", 6, NC)
        gtmp = sb("gtmp", 5, NC, HEADS)
        el = sb("el", NC)
        ps = [ctx.enter_context(nc.psum_tensor(f"ps{i}", [P, GRP], F32)) for i in range(8)]

        ident, UI, ones = cst[:, C_ID:C_ID + P], cst[:, C_UI:C_UI + P], cst[:, C_ONE:C_ONE + P]
        scanm = cst[:, C_SCAN:C_SCAN + HALF]

        def col(n):
            return cst[:, C_COL + n:C_COL + n + 1]

        def gs(b, g):
            return b[:, g * GRP:(g + 1) * GRP]

        def ck(b, c):
            return b[:, c * P:(c + 1) * P]

        def c4(ap):
            return ap.rearrange("p (c t) -> p c t", t=P)

        def halves(ap, h, late):
            return ap.rearrange("p (b w) -> p b w", w=2 * h)[:, :, h:2 * h] if late \
                else ap.rearrange("p (b w) -> p b w", w=2 * h)[:, :, 0:h]

        def merge(V, buf, g, l, late, data):
            h = SOLVE_LEVELS[l]
            o = (M_SOLT if late else M_SOL) + l * 64
            mk = msk[:, o:o + 64]
            if h == 64:
                return V.copy_predicated(halves(gs(buf, g), h, late), mk.unsqueeze(1).to_broadcast([P, CPG, 64]), data)
            out = gs(buf, g).rearrange("p (c b w) -> p c b w", c=CPG, w=2 * h)
            out = out[:, :, :, h:2 * h] if late else out[:, :, :, 0:h]
            mk = mk.rearrange("p (b w) -> p b w", w=h).unsqueeze(1).to_broadcast([P, CPG, 64 // h, h])
            return V.copy_predicated(out, mk, data)

        def half_data(group, h, late):
            if h == 64:
                return halves(group, h, late)
            v = group.rearrange("p (c b w) -> p c b w", c=CPG, w=2 * h)
            return v[:, :, :, h:2 * h] if late else v[:, :, :, 0:h]

        def per_chunk(cols, g):
            return cols[:, g * CPG:(g + 1) * CPG].unsqueeze(2).to_broadcast([P, CPG, P])

        def over_chunks(m):
            return m.unsqueeze(1).to_broadcast([P, CPG, m.shape[1]])

        KG, KGC, KB, KBG, KKD, KHB, KGE = range(7)

        N = Stages(nc, "n_", dict(
            const=64 + 128, xa=64, xb=64, sq=8, ln=1, r0=1, rs=1, newton=4, xs=8, tr=16, ht=16, ab=1, absb=1,
            gch=9, lbd=1, mask=1, gact=7, gcs=1, gtab=1, once=3, onceact=2))
        S = Stages(nc, "s_", dict(
            wh=16, wg=16, init=1, pF=2, pQ=2, pZ=2, pV=2, pGQ=2, pGK=2, pGV=2, pGZ=2, pGR=2,
            thF=2, thQ=2, thZ=2, v=2, lf=1, rawq=2, rawk=2, rawv=2, c0=3, thG=2, egr=2,
            qhat=2, zh=2, kh=1, cum=1, D=6, E=4, EF=2, EQ=1, EL=1, elast=1, M=4, MF=2, qe=1, kl=1,
            pA=10, att=10, pKL=2, klt=2, pDS=2, hs=8, pOH=2, sqh=2, oh=2, pNH=2, lnh=2, rh=2, h1=2, mixh=2, outh=16,
            conv=9, thc=3, c2=3, sqc=4, pN=4, lnc=4, rc=4, nrm=4, zg=2, dm=2, dx=4, dec=4,
            pKK=2, A=2, pAT=2, at=2, xy=2, eye=2, pP=12, P=12, pX=10, X=10, pXT=10, XT=10, pY=2, Y=2,
            pKT=2, rk=2, kdec=2, pVT=2, rv=2, pWT=2, nw=2, pQK=2, qkd=2, qg=2,
            pVN=8, vn=8, pS=8, sg=8, pOG=2, og=2, sqg=2, pNG=2, lng=2, rg=2, g1=2, mixg=2, outg=16, save=1), pool_dma)

        bank_at = {key: ps[b] for key, b in BANK.items()}
        block = ctx.enter_context(nc.Block())

        @block.sync
        def _(sp):
            sp.dma_start(cst[:], a["consts"]).then_inc(N.sem["const"], 16)
            sp.dma_start(arena[:, 0:M_N], a["masks"]).then_inc(N.sem["const"], 16)
            sp.dma_start(nw[:], a["norm_mix"]).then_inc(N.sem["const"], 16)
            sp.dma_start(onw[:], a["onorm"]).then_inc(N.sem["const"], 16)
            sp.dma_start(wab[:], a["w_ab"]).then_inc(N.sem["const"], 16)
            sp.dma_start(lbt[:], a["lb"]).then_inc(N.sem["const"], 16)
            sp.dma_start(agt[:, 0, :], a["a_log"].partition_broadcast(P)).then_inc(N.sem["const"], 16)
            sp.dma_start(agt[:, 1, :], a["dt_bias"].partition_broadcast(P)).then_inc(N.sem["const"], 16)
            for h in range(HEADS):
                sp.dma_start(PT[:, h, 3:15], a["conv_w"][:, h, :]).then_inc(N.sem["const"], 16)
            sp.wait_ge(N.sem["mask"], 1)
            with sp.Fori(0, NHALF) as half:
                with sp.If(half > 0):
                    sp.wait_ge(S.sem["mixg"], half * (HEADS * 2))
                    sp.nop(nofuse=True)
                for t in range(NC):
                    sp.dma_start(X8[:, t, :], a["x"][bass.ds(half * HALF + t * P, P), :])\
                        .then_inc(N.sem["xa" if t < 4 else "xb"], 16)
                with sp.Fori(0, HEADS) as head:
                    t = S.engine(sp, half * HEADS + head)
                    t.wait_last("pV")
                    sp.dma_start(WH[:], a["w_proj"][bass.ds(head, 1), :, 0:4].rearrange("h p b k c -> p (h b) k c"))\
                        .then_inc(S.sem["wh"], 16)
                    t.wait_last("pGZ")
                    sp.dma_start(WG[:], a["w_proj"][bass.ds(head, 1), :, 4:8].rearrange("h p b k c -> p (h b) k c"))\
                        .then_inc(S.sem["wg"], 16)

        @block.gpsimd
        def _(pool):
            nc.gpsimd.memset(H["att"][:], 0.0).then_inc(N.sem["once"], 1)
            nc.gpsimd.memset(SALL[:], 0.0).then_inc(N.sem["once"], 1)
            nc.gpsimd.memset(HALOS[:], 0.0).then_inc(N.sem["once"], 1)
            with pool.Fori(0, NHALF) as half, pool.Fori(0, HEADS) as head:
                t = S.engine(pool, half * HEADS + head)
                t.wait("cum", 1)
                for l in range(6):
                    d = H["d0" if l % 2 == 0 else "d1"]
                    if l >= 2:
                        t.wait("E", l - 1) if l < 5 else t.wait("E", 4)
                    if l < 4:
                        h = ATT_LEVELS[l]
                        v = "p (b w) -> p b w"
                        ci = H["cum"][:].rearrange(v, w=2 * h)
                        ref = ci[:, :, h - 1:h].to_broadcast([P, HALF // (2 * h), 2 * h])
                        out = d[:].rearrange(v, w=2 * h)
                    else:
                        w, at = (8, 3) if l == 4 else (P, P - 1)
                        if l == 5:
                            t.wait("E", 4)
                        ci = H["cum"][:].rearrange("p (b w) -> p b w", w=w)
                        ref = ci[:, :, at:at + 1].to_broadcast([P, HALF // w, w])
                        out = d[:].rearrange("p (b w) -> p b w", w=w)
                    t.done(nc.gpsimd.tensor_tensor(out, ci, ref, ALU.subtract), "D")
                for g in range(NG):
                    t.wait("dx", g + 1)
                    t.hold()
                    o = c4(gs(DEC, g))
                    t.done(nc.gpsimd.affine_select(out=o, in_=o, compare_op=ALU.is_gt, fill=0.0, base=0,
                                                   pattern=[[0, CPG], [-1, P]], channel_multiplier=1), "dec")
                for g in range(NG):
                    t.wait("nrm", NG + g + 1)
                    t.wait("egr", 2)
                    t.wait("xy", 2)
                    t.done(nc.gpsimd.tensor_tensor(gs(QG, g), gs(conv["q"], g), gs(EGR, g), ALU.mult), "qg")
                for g in range(NG):
                    t.wait("dx", NG + g + 1)
                    t.hold()
                    o = c4(gs(DECT, g))
                    t.done(nc.gpsimd.affine_select(out=o, in_=o, compare_op=ALU.is_ge, fill=0.0, base=0,
                                                   pattern=[[0, CPG], [1, P]], channel_multiplier=-1), "dec")
                for stage, rows, src, out in (("mixh", head, H["o"], "outh"), ("mixg", head + HEADS, OG, "outg")):
                    t.wait(stage, 2)
                    t.hold()
                    pool.dma_start(a["mix"][bass.ds(rows, 1), :, bass.ds(half * HALF, HALF)]
                                   .rearrange("h p t -> p (h t)"), src[:]).then_inc(S.sem[out], 16)
                t.close()
            pool.wait_ge(S.sem["outh"], NHALF * HEADS * 16)
            pool.wait_ge(S.sem["outg"], NHALF * HEADS * 16)

        @block.scalar
        def _(act):
            A = nc.scalar.activation
            act.wait_ge(N.sem["const"], 192)
            act.wait_ge(N.sem["lbd"], 1)
            A(lbt[:, 0, :], lbt[:, 1, :], ACT.Exp).then_inc(N.sem["onceact"], 1)
            A(agt[:, 0, :], agt[:, 0, :], ACT.Exp).then_inc(N.sem["onceact"], 1)
            with act.Fori(0, NHALF) as half:
                n = N.engine(act, half)
                for t_ in range(NC):
                    if t_ % 4 == 0:
                        n.wait("xa" if t_ == 0 else "xb", 64)
                    if t_ >= 2:
                        n.wait("sq", t_ - 1)
                    n.done(A(hT[:, t_ % 2, :], X8[:, t_, :], ACT.Square, accum_out=ss[:, 0, t_:t_ + 1]), "sq")
                n.wait("sq", 8)
                n.done(A(ss[:, 1, :], ss[:, 0, :], ACT.Ln, scale=1.0 / D, bias=col(COL_EPS)), "ln")
                n.wait("ln", 1)
                n.done(A(ss[:, 2, :], ss[:, 1, :], ACT.Exp, scale=-0.5), "r0")
                n.wait("gch", 1)
                n.done(A(gtmp[:, 1], gtmp[:, 0], ACT.Abs), "gact")
                n.wait("gact", 1)
                n.done(A(gtmp[:, 1], gtmp[:, 1], ACT.Exp, scale=-1.0), "gact")
                n.wait("gact", 2)
                n.done(A(gtmp[:, 2], gtmp[:, 1], ACT.Ln, bias=cst[:, C_ONE:C_ONE + 1]), "gact")
                n.wait("absb", 1)
                n.done(A(gtmp[:, 3], gtmp[:, 4], ACT.Tanh, scale=0.5), "gact")
                n.wait("gch", 7)
                n.done(A(gtmp[:, 0], GT[:, KGC], ACT.Exp), "gact")
                n.done(A(GT[:, KGE], gtmp[:, 1], ACT.Exp), "gact")
                n.done(A(GT[:, KKD], gtmp[:, 2], ACT.Exp), "gact")
                with act.Fori(0, HEADS) as head:
                    t = S.engine(act, half * HEADS + head)
                    def copies(g, stage, out, src, func=ACT.Copy, need=None, **kw):
                        if need:
                            t.wait(need, g + 1)
                        t.done(A(out, src, func, **kw), stage)

                    def project_out(n_, stage, buf, func=ACT.Copy, off=0, **kw):
                        for g in range(NG):
                            copies(g, stage, buf[:, off + g * GRP:off + (g + 1) * GRP], bank_at[(n_, g)][:], func,
                                   need="p" + n_.upper(), **kw)

                    def first_tap(i):
                        n_ = "qkv"[i]
                        t.wait("raw" + n_, 2)
                        t.done(A(conv[n_], raw[n_][:, 0:HALF], ACT.Copy, scale=PC[:, 3 + 4 * i:4 + 4 * i]), "c0")

                    def decays(l):
                        h = ATT_LEVELS[l]
                        t.wait("D", l + 1)
                        if l >= 2:
                            t.wait("M", l - 1)
                        e = H["e0" if l % 2 == 0 else "e1"][:].rearrange("p (b w) -> p b w", w=2 * h)
                        d = H["d0" if l % 2 == 0 else "d1"][:].rearrange("p (b w) -> p b w", w=2 * h)
                        A(e[:, :, h:2 * h], d[:, :, h:2 * h], ACT.Exp, bias=col(COL_LNHQ))
                        t.done(A(e[:, :, 0:h], d[:, :, 0:h], ACT.Exp, scale=-1.0), "E")

                    def solve_out(l):
                        for g in range(NG):
                            t.wait("pP", 2 * l + g + 1)
                            t.done(A(gs(PP, g), bank_at[("P", l, g)][:], ACT.Copy), "P")
                            for i in range(NG if l and g == 0 else 0):
                                t.wait("pXT", 2 * (l - 1) + i + 1)
                                t.done(A(gs(Y_, i), bank_at[("XT", l - 1, i)][:], ACT.Copy), "XT")

                    project_out("F", "thF", H["kh"], ACT.Tanh, scale=0.5)
                    t.wait_last("outg")
                    t.wait("init", 1)
                    t.wait("thF", 2)
                    t.done(A(H["lf"][:], H["kh"][:], ACT.Ln, scale=PC[:, 0:1], bias=PC[:, 1:2]), "lf")
                    project_out("Q", "thQ", H["kl"], ACT.Tanh, scale=0.5)
                    decays(0)
                    decays(1)
                    project_out("Z", "thZ", H["klt"], ACT.Tanh, scale=0.5)
                    decays(2)
                    decays(3)
                    t.wait("D", 5)
                    t.wait("M", 3)
                    t.done(A(H["e0"][:], H["d0"][:], ACT.Exp, bias=col(COL_LNHQ)), "EF")
                    t.wait("M", 4)
                    t.done(A(H["e1"][:], H["d0"][:], ACT.Exp, scale=-1.0), "EF")
                    t.done(A(el[:], H["cum"][:].rearrange("p (c w) -> p c w", w=P)[:, :, P - 1], ACT.Exp), "elast")
                    t.done(A(H["qe"][:], H["cum"][:], ACT.Exp, bias=col(COL_LNHQ)), "EQ")
                    t.wait("D", 6)
                    t.wait("qhat", 2)
                    t.done(A(H["kl"][:], H["d1"][:], ACT.Exp, scale=-1.0), "EL")
                    project_out("V", "v", H["v"])
                    project_out("Gq", "rawq", raw["q"], off=HALO)
                    first_tap(0)
                    t.wait("zh", 2)
                    project_out("KL", "klt", H["klt"])
                    t.wait("conv", 3)
                    t.done(A(tmp["q"], conv["q"], ACT.Tanh, scale=0.5), "thc")
                    project_out("Gk", "rawk", raw["k"], off=HALO)
                    first_tap(1)
                    project_out("GR", "egr", EGR, ACT.Exp)
                    t.wait("c2", 1)
                    for g in range(NG):
                        t.done(A(gs(tmp["q"], g), gs(conv["q"], g), ACT.Square), "sqc")
                    t.wait_last("outh")
                    for g in range(NG):
                        t.wait("pOH", g + 1)
                        t.done(A(gs(H["o"], g), ps[6 + g][:], ACT.Copy), "oh")
                        t.done(A(gs(H["kh"], g), ps[6 + g][:], ACT.Square), "sqh")
                    t.wait("conv", 6)
                    t.done(A(tmp["k"], conv["k"], ACT.Tanh, scale=0.5), "thc")
                    t.wait("dm", 2)
                    for g in range(NG):
                        t.done(A(gs(DEC, g), gs(DM, g), ACT.Exp, scale=-1.0), "dx")
                    t.wait("c2", 2)
                    for g in range(NG):
                        t.done(A(gs(tmp["k"], g), gs(conv["k"], g), ACT.Square), "sqc")
                    copies(0, "rawv", raw["v"][:, HALO:HALO + GRP], bank_at[("Gv", 0)][:], need="pGV")
                    for g in range(NG):
                        t.wait("pNH", g + 1)
                        t.done(A(gs(H["kh"], g), bank_at[("NH", g)][:], ACT.Ln, scale=1.0 / P, bias=col(COL_EPS)), "lnh")
                    norms = [("k", 0), ("k", 1), ("q", 0), ("q", 1)]
                    for m, (n_, g) in enumerate(norms):
                        t.wait("pN", m + 1)
                        t.done(A(gs(tmp[n_], g), bank_at[("N", m)][:], ACT.Ln, bias=col(COL_EPS4)), "lnc")
                    for m, (n_, g) in enumerate(norms):
                        t.wait("lnc", m + 1)
                        if n_ == "q":
                            t.done(A(gs(tmp[n_], g), gs(tmp[n_], g), ACT.Exp, scale=-0.5, bias=col(COL_LNGQ)), "rc")
                        else:
                            t.done(A(gs(tmp[n_], g), gs(tmp[n_], g), ACT.Exp, scale=-0.5), "rc")
                    for g in range(NG):
                        t.wait("lnh", g + 1)
                        t.done(A(gs(H["kh"], g), gs(H["kh"], g), ACT.Exp, scale=-0.5), "rh")
                    copies(1, "rawv", raw["v"][:, HALO + GRP:HALO + HALF], bank_at[("Gv", 1)][:], need="pGV")
                    first_tap(2)
                    for g in range(NG):
                        copies(g, "at", gs(AT_, g), bank_at[("AT", g)][:], need="pAT")
                    for l in range(4):
                        solve_out(l)
                    t.wait("conv", 9)
                    t.done(A(tmp["v"], conv["v"], ACT.Tanh, scale=0.5), "thc")
                    for g in range(NG):
                        t.done(A(gs(DECT, g), gs(DM, g), ACT.Exp), "dx")
                    solve_out(4)
                    solve_out(5)
                    project_out("WT", "nw", NW, scale=-1.0)
                    for c in range(NC):
                        t.wait("pVN", c + 1)
                        t.done(A(VN[:, c % 2, :], bank_at[("VN", c)][:, 0:P], ACT.Copy), "vn")
                        if c == CPG:
                            t.wait("pOG", 1)
                            t.done(A(gs(OG, 0), ps[6][:], ACT.Copy), "og")
                        if c == CPG + 1:
                            t.done(A(gs(tmp["q"], 0), ps[6][:], ACT.Square), "sqg")
                        if c == CPG + 2:
                            copies(0, "thG", gs(tmp["v"], 0), bank_at[("Gz", 0)][:], ACT.Tanh, need="pGZ", scale=0.5)
                    t.wait("pOG", 2)
                    t.done(A(gs(tmp["q"], 1), ps[7][:], ACT.Square), "sqg")
                    t.done(A(gs(OG, 1), ps[7][:], ACT.Copy), "og")
                    copies(1, "thG", gs(tmp["v"], 1), bank_at[("Gz", 1)][:], ACT.Tanh, need="pGZ", scale=0.5)
                    project_out("NG", "lng", tmp["k"], ACT.Ln, scale=1.0 / P, bias=col(COL_EPS))
                    for g in range(NG):
                        t.wait("lng", g + 1)
                        t.done(A(gs(tmp["k"], g), gs(tmp["k"], g), ACT.Exp, scale=-0.5), "rg")
                    t.close()

        @block.vector
        def _(dve):
            V = nc.vector
            dve.wait_ge(N.sem["const"], 192)
            once = [0]
            osem = nc.alloc_semaphore("once_dve")

            def link(ins):
                once[0] += 1
                ins.then_inc(osem, 1)
                dve.wait_ge(osem, once[0])

            V.tensor_tensor(lbt[:, 1, :], lbt[:, 1, :], lbt[:, 0, :], ALU.subtract).then_inc(N.sem["lbd"], 1)
            dve.wait_ge(N.sem["onceact"], 2)
            link(V.tensor_scalar(lbt[:, 0, :], lbt[:, 0, :], 1.0, None, ALU.add))
            link(V.reciprocal(lbt[:, 0, :], lbt[:, 0, :]))
            V.tensor_copy(msk[:], arena[:, 0:M_N]).then_inc(N.sem["mask"], 1)
            V.tensor_scalar(PT[:, :, 0], lbt[:, 0, :], -0.5, 0.5, ALU.mult, ALU.add)
            V.tensor_scalar(PT[:, :, 1], lbt[:, 0, :], 0.5, 0.5, ALU.mult, ALU.add)
            V.tensor_scalar(PT[:, :, 2], lbt[:, 0, :], 0.5, -0.5, ALU.mult, ALU.add)
            V.tensor_scalar(onw[:], onw[:], 0.5, None, ALU.mult)
            link(V.tensor_scalar(agt[:, 0, :], agt[:, 0, :], -1.0, None, ALU.mult))
            dve.wait_ge(N.sem["once"], 3)
            with dve.Fori(0, NHALF) as half:
                n = N.engine(dve, half)

                n.wait("r0", 1)
                V.tensor_scalar(ss[:, 3, :], ss[:, 0, :], 1.0 / D, EPS, ALU.mult, ALU.add)
                n.done(V.tensor_tensor(ss[:, 4, :], ss[:, 2, :], ss[:, 2, :], ALU.mult), "newton")
                n.wait("newton", 1)
                n.done(V.tensor_tensor(ss[:, 4, :], ss[:, 4, :], ss[:, 3, :], ALU.mult), "newton")
                n.wait("newton", 2)
                n.done(V.tensor_scalar(ss[:, 4, :], ss[:, 4, :], -0.5, 1.5, ALU.mult, ALU.add), "newton")
                n.wait("newton", 3)
                n.done(V.tensor_tensor(ss[:, 5, :], ss[:, 4, :], ss[:, 2, :], ALU.mult), "newton")
                n.wait("newton", 4)
                for t_ in range(NC):
                    n.done(V.tensor_scalar(X8[:, t_, :], X8[:, t_, :], ss[:, 5, t_:t_ + 1], None, ALU.mult), "xs")
                    if t_ >= 1:
                        for q in range(2):
                            ht_evac(nc, n, V, hT, nw, ps, t_ - 1, q)
                for q in range(2):
                    ht_evac(nc, n, V, hT, nw, ps, NC - 1, q)
                n.wait("ab", 1)
                abv = ps[7][:, 0:NC * 8].rearrange("p (c h) -> p c h", h=8)
                dt = agt[:, 1, :].unsqueeze(1).to_broadcast([P, NC, HEADS])
                na = agt[:, 0, :].unsqueeze(1).to_broadcast([P, NC, HEADS])

                def step(ins):
                    n.done(ins, "gch")
                    n.wait("gch", n.n["gch"])

                n.done(V.tensor_copy(gtmp[:, 4], abv[:, :, HEADS:2 * HEADS]), "absb")
                step(V.tensor_tensor(gtmp[:, 0], abv[:, :, 0:HEADS], dt, ALU.add))
                n.wait("gact", 3)
                step(V.scalar_tensor_tensor(gtmp[:, 0], gtmp[:, 0], 0.0, gtmp[:, 2], ALU.max, ALU.add))
                step(V.tensor_tensor(GT[:, KG], gtmp[:, 0], na, ALU.mult))
                n.wait("gact", 4)
                step(V.tensor_scalar(GT[:, KB], gtmp[:, 3], 0.5, 0.5, ALU.mult, ALU.add))
                step(V.tensor_scalar(GT[:, KHB], GT[:, KB], 0.5, None, ALU.mult))
                n.wait("gcs", 1)
                cs = ps[6][:, 0:2 * NC * HEADS].rearrange("p (k c h) -> p k c h", k=2, h=HEADS)
                V.tensor_copy(gtmp[:, 1], cs[:, 1])
                step(V.tensor_copy(GT[:, KGC], cs[:, 0]))
                step(V.tensor_tensor(gtmp[:, 2], gtmp[:, 1], GT[:, KGC], ALU.subtract))
                n.wait("gact", 7)
                step(V.tensor_tensor(GT[:, KBG], gtmp[:, 0], GT[:, KB], ALU.mult))
                step(V.tensor_scalar(GT[:, KB], GT[:, KB], -1.0, None, ALU.mult))
                n.hold()
                with dve.Fori(0, HEADS) as head:
                    t = S.engine(dve, half * HEADS + head)
                    t.hold()
                    V.tensor_copy(PC[:], PT[:, bass.ds(head, 1), :].rearrange("p h n -> p (h n)"))
                    V.tensor_copy(GC[:], GT[:, :, :, bass.ds(head, 1)].rearrange("p k c h -> p k (c h)"))
                    V.tensor_copy(SH[:, 0, :], SALL[:, 0, bass.ds(head, 1), :].rearrange("p h n -> p (h n)"))
                    V.tensor_copy(SG[:], SALL[:, 1, bass.ds(head, 1), :].rearrange("p h n -> p (h n)"))
                    for i, n_ in enumerate("qkv"):
                        V.tensor_copy(raw[n_][:, 0:HALO], HALOS[:, bass.ds(head, 1), i, :].rearrange("p h n -> p (h n)"))
                    t.done(V.tensor_copy(c4(GB), GT[:, KG, :, bass.ds(head, 1)].to_broadcast([P, NC, P])), "init")
                    def silu(g, stage, out, th, n_):
                        t.wait({"Q": "thQ", "Z": "thZ", "Gz": "thG"}[n_], g + 1)
                        t.done(V.scalar_tensor_tensor(gs(out, g), gs(th, g), 1.0, bank_at[(n_, g)][:],
                                                      ALU.add, ALU.mult), stage)

                    def level(l):
                        h = ATT_LEVELS[l]
                        t.wait("E", l + 1)
                        if l >= 2:
                            t.wait("pA", 2 * (l - 1))
                        v = lambda b: b[:].rearrange("p (b w) -> p b w", w=2 * h)
                        m, e = H[f"m{l % 2}"], H[f"e{l % 2}"]
                        V.tensor_tensor(v(m)[:, :, h:2 * h], v(H["qh"])[:, :, h:2 * h], v(e)[:, :, h:2 * h], ALU.mult)
                        t.done(V.tensor_tensor(v(m)[:, :, 0:h], v(H["kh"])[:, :, 0:h], v(e)[:, :, 0:h], ALU.mult), "M")

                    def att(l):
                        h = ATT_LEVELS[l]
                        for g in range(NG):
                            t.wait("pA", 2 * l + g + 1)
                            if l:
                                t.wait("att", 2 * (l - 1) + g + 1)
                            t.hold()
                            t.done(merge(V, H["att"], g, SOLVE_LEVELS.index(h), True,
                                         half_data(bank_at[("A", l, g)][:], h, True)), "att")

                    def conv_tap(i, j):
                        n_ = "qkv"[i]
                        if j == 1:
                            t.wait("c0", i + 1)
                        else:
                            t.wait("conv", 3 * i + j - 1)
                        t.done(V.scalar_tensor_tensor(conv[n_], raw[n_][:, j:j + HALF],
                                                      PC[:, 3 + 4 * i + j:4 + 4 * i + j], conv[n_],
                                                      ALU.mult, ALU.add), "conv")

                    def conv_silu(i):
                        n_ = "qkv"[i]
                        t.wait("thc", i + 1)
                        t.done(V.scalar_tensor_tensor(conv[n_], tmp[n_], 1.0, conv[n_], ALU.add, ALU.mult), "c2")

                    def solve_merge(l):
                        h = SOLVE_LEVELS[l + 1]
                        for g in range(NG):
                            if l < 5:
                                t.wait("pX", 2 * l + g + 1)
                                t.hold()
                                t.done(merge(V, X_, g, l + 1, False, half_data(bank_at[("X", l, g)][:], h, False)), "X")
                            else:
                                t.wait("pY", g + 1)
                                t.hold()
                                t.done(merge(V, Y_, g, l + 1, True, half_data(bank_at[("Y", l, g)][:], h, True)), "Y")

                    t.wait("init", 1)
                    t.wait("lf", 1)
                    t.done(V.tensor_tensor_scan(H["cum"][:], scanm, H["lf"][:], 0.0, ALU.mult, ALU.add), "cum")
                    t.done(V.tensor_scalar(H["kh"][:], H["kh"][:], PC[:, 2:3], PC[:, 0:1], ALU.mult, ALU.add), "kh")
                    for g in range(NG):
                        silu(g, "qhat", H["qh"], H["kl"], "Q")
                    t.wait("kh", 1)
                    t.wait("qhat", 2)
                    level(0)
                    level(1)
                    for g in range(NG):
                        silu(g, "zh", H["zh"], H["klt"], "Z")
                    level(2)
                    level(3)
                    att(0)
                    att(1)
                    t.wait("EQ", 1)
                    t.done(V.tensor_tensor(H["qe"][:], H["qh"][:], H["qe"][:], ALU.mult), "qe")
                    t.wait("EL", 1)
                    t.done(V.tensor_tensor(H["kl"][:], H["kh"][:], H["kl"][:], ALU.mult), "kl")
                    att(2)
                    att(3)
                    t.wait("EF", 2)
                    t.done(V.tensor_tensor(H["m0"][:], H["qh"][:], H["e0"][:], ALU.mult), "MF")
                    t.done(V.tensor_tensor(H["m1"][:], H["kh"][:], H["e1"][:], ALU.mult), "MF")
                    for j in range(1, TAPS):
                        conv_tap(0, j)
                    for g in range(NG):
                        t.wait("pA", 9 + g)
                        t.wait("att", 7 + g)
                        t.hold()
                        t.done(V.copy_predicated(c4(gs(H["att"], g)), over_chunks(msk[:, M_ATTF:M_ATTF + P]),
                                                 c4(bank_at[("AF", g)][:])), "att")
                    t.wait("elast", 1)
                    for c in range(NC):
                        t.wait("pDS", c // CPG + 1)
                        if c:
                            t.wait("hs", c)
                        t.done(V.scalar_tensor_tensor(SH[:, c + 1, :], SH[:, c, :], el[:, c:c + 1],
                                                      ck(bank_at[("DS", c // CPG)], c % CPG), ALU.mult, ALU.add), "hs")
                    conv_silu(0)
                    for j in range(1, TAPS):
                        conv_tap(1, j)
                    for g in range(NG):
                        t.wait("egr", g + 1)
                        t.done(V.tensor_tensor(c4(gs(DM, g)), c4(bank_at[("GR", g)][:]), per_chunk(GC[:, KGC], g),
                                               ALU.subtract), "dm")
                    conv_silu(1)
                    for m in range(4):
                        t.wait("rc", m + 1)
                        b, g = conv["kq"[m // 2]], m % 2
                        t.done(V.tensor_tensor(gs(b, g), gs(b, g), gs(tmp["kq"[m // 2]], g), ALU.mult), "nrm")
                    for g in range(NG):
                        t.wait("pKK", g + 1)
                        t.wait("dec", g + 1)
                        for c in range(CPG * g, CPG * (g + 1)):
                            last = V.scalar_tensor_tensor(ck(A_, c), ck(bank_at[("KK", g)], c % CPG), GC[:, KB, c:c + 1],
                                                          ck(DEC, c), ALU.mult, ALU.mult)
                        t.done(last, "A")
                        V.tensor_copy(c4(gs(X_, g)), over_chunks(ident))
                        t.done(V.tensor_copy(c4(gs(Y_, g)), over_chunks(ident)), "eye")
                    for g in range(NG):
                        t.wait("at", g + 1)
                        t.wait("eye", g + 1)
                        t.wait("A", g + 1)
                        t.hold()
                        merge(V, X_, g, 0, False, half_data(gs(A_, g), 1, False))
                        t.done(merge(V, Y_, g, 0, True, half_data(gs(AT_, g), 1, True)), "xy")
                    for g in range(NG):
                        t.wait("pKT", g + 1)
                        kt = c4(bank_at[("KT", g)][:])
                        t.done(V.tensor_tensor(c4(gs(RK, g)), kt, per_chunk(GC[:, KBG], g), ALU.mult), "rk")
                        t.done(V.tensor_tensor(c4(gs(KDEC, g)), kt, per_chunk(GC[:, KKD], g), ALU.mult), "kdec")
                    for l in range(6):
                        solve_merge(l)
                        if l < 3:
                            conv_tap(2, l + 1)
                        if l == 3:
                            conv_silu(2)
                            t.hold()
                            for i, n_ in enumerate("qkv"):
                                V.tensor_copy(HALOS[:, bass.ds(head, 1), i, :].rearrange("p h n -> p (h n)"),
                                              raw[n_][:, HALF:HALF + HALO])
                        if l == 4:
                            for g in range(NG):
                                t.wait("pVT", g + 1)
                                t.done(V.tensor_tensor(c4(gs(RV, g)), c4(bank_at[("VT", g)][:]),
                                                       per_chunk(GC[:, KHB], g), ALU.mult), "rv")
                            for g in range(NG):
                                t.wait("pQK", g + 1)
                                t.wait("dec", NG + g + 1)
                                t.done(V.tensor_tensor(gs(QKD, g), bank_at[("QK", g)][:], gs(DECT, g), ALU.mult), "qkd")
                    for c in range(NC):
                        t.wait("pS", c + 1)
                        t.done(V.scalar_tensor_tensor(SG[:], SG[:], GC[:, KGE, c:c + 1], bank_at[("S", c)][:, 0:P],
                                                      ALU.mult, ALU.add), "sg")
                        if c < 4:
                            g = c // 2
                            t.wait("rh", g + 1)
                            t.wait("oh", g + 1)
                            if c % 2 == 0:
                                t.done(V.tensor_tensor(gs(H["o"], g), gs(H["o"], g), gs(H["kh"], g), ALU.mult), "h1")
                            else:
                                t.wait("h1", g + 1)
                                t.done(V.scalar_tensor_tensor(gs(H["o"], g), gs(H["o"], g), onw[:, 0:1],
                                                              gs(H["zh"], g), ALU.mult, ALU.mult), "mixh")
                        if c == NC - 1:
                            silu(0, "zg", ZG, tmp["v"], "Gz")
                    silu(1, "zg", ZG, tmp["v"], "Gz")
                    t.wait("sg", 8)
                    t.wait("hs", 8)
                    t.hold()
                    V.tensor_copy(SALL[:, 0, bass.ds(head, 1), :].rearrange("p h n -> p (h n)"), SH[:, NC, :])
                    t.done(V.tensor_copy(SALL[:, 1, bass.ds(head, 1), :].rearrange("p h n -> p (h n)"), SG[:]), "save")
                    for g in range(NG):
                        t.wait("rg", g + 1)
                        t.wait("og", g + 1)
                        t.done(V.tensor_tensor(gs(OG, g), gs(OG, g), gs(tmp["k"], g), ALU.mult), "g1")
                        t.wait("g1", g + 1)
                        t.done(V.scalar_tensor_tensor(gs(OG, g), gs(OG, g), onw[:, 1:2], gs(ZG, g),
                                                      ALU.mult, ALU.mult), "mixg")
                    t.wait("save", 1)
                    t.hold()
                    t.close()
                n.close()

        @block.tensor
        def _(pe):
            mm = nc.tensor.matmul
            pe.wait_ge(N.sem["const"], 192)
            with pe.Fori(0, NHALF) as half:
                n = N.engine(pe, half)
                for t_ in range(NC):
                    n.wait("xs", t_ + 1)
                    for q in range(2):
                        j = 2 * t_ + q
                        if j >= 6:
                            n.wait("ht", j - 5)
                        for k in range(4):
                            last = nc.tensor.transpose(ps[j % 6][:, k * P:(k + 1) * P],
                                                       X8[:, t_, (4 * q + k) * P:(4 * q + k + 1) * P], ident)
                        n.done(last, "tr")
                n.wait("ht", 16)
                for t_ in range(NC):
                    for k in range(KD):
                        last = mm(ps[7][:, t_ * 8:(t_ + 1) * 8], hT[:, k, t_ * P:(t_ + 1) * P], wab[:, k, :],
                                  start=(k == 0), stop=(k == KD - 1))
                n.done(last, "ab")
                n.wait("gch", 3)
                gv = GT[:, KG].rearrange("p c h -> p (c h)")
                w = NC * HEADS
                mm(ps[6][:, 0:w], UI, gv, start=True, stop=True)
                n.done(mm(ps[6][:, w:2 * w], ones, gv, start=True, stop=True), "gcs")
                n.wait("gch", 6)
                n.hold()
                with pe.Fori(0, HEADS) as head:
                    t = S.engine(pe, half * HEADS + head)
                    emptied = {}

                    def job(key, *free):
                        b = BANK[key]
                        if b in emptied:
                            t.wait(*emptied[b])
                        emptied[b] = free
                        return ps[b]

                    def part(W, b, g, out, ks):
                        for k in ks:
                            last = mm(out[:], W[:, b, k, :], hT[:, k, g * GRP:(g + 1) * GRP],
                                      start=(k == 0), stop=(k == KD - 1))
                        return last

                    def project(W, b, n_, g, free):
                        t.done(part(W, b, g, job((n_, g), free, g + 1), range(KD)), "p" + n_.upper())

                    def level(l):
                        t.wait("M", l + 1)
                        for g in range(NG):
                            out = job(("A", l, g), "att", 2 * l + g + 1)
                            for c in range(CPG):
                                m = ck(H[f"m{l % 2}"], g * CPG + c)
                                last = mm(ck(out, c), m, m, start=True, stop=True)
                            t.done(last, "pA")

                    def products(n_, free, lhs, rhs, need=None, stage=None, per=1, at=0):
                        for g in range(NG):
                            if need:
                                t.wait(need, g + 1)
                            out = job((n_, g), free, at + per * (g + 1))
                            for c in range(CPG):
                                last = mm(ck(out, c), ck(lhs, g * CPG + c), ck(rhs, g * CPG + c), start=True, stop=True)
                            t.done(last, stage or "p" + n_)

                    def turned(n_, free, src, need=None):
                        for g in range(NG):
                            if need:
                                t.wait(need, g + 1)
                            out = job((n_, g), free, g + 1)
                            for c in range(CPG):
                                last = nc.tensor.transpose(ck(out, c), ck(src, g * CPG + c), ident)
                            t.done(last, "p" + n_)

                    def solve(l):
                        for g in range(NG):
                            if l == 0:
                                t.wait("xy", g + 1)
                                t.wait("at", g + 1)
                            else:
                                t.wait("X", 2 * (l - 1) + g + 1)
                            out = job(("P", l, g), "P", 2 * l + g + 1)
                            for c in range(g * CPG, (g + 1) * CPG):
                                last = mm(ck(out, c % CPG), ck(AT_, c), ck(X_, c), start=True, stop=True)
                            t.done(last, "pP")
                            for i in range(NG if l and g == 0 else 0):
                                t.wait("X", 2 * (l - 1) + i + 1)
                                out = job(("XT", l - 1, i), "XT", 2 * (l - 1) + i + 1)
                                for c in range(i * CPG, (i + 1) * CPG):
                                    last = nc.tensor.transpose(ck(out, c % CPG), ck(X_, c), ident)
                                t.done(last, "pXT")
                        for g in range(NG):
                            t.wait("P", 2 * l + g + 1)
                            if l:
                                t.wait("XT", 2 * (l - 1) + g + 1)
                            if l < 5:
                                out = job(("X", l, g), "X", 2 * l + g + 1)
                                for c in range(g * CPG, (g + 1) * CPG):
                                    last = mm(ck(out, c % CPG), ck(Y_, c), ck(PP, c), start=True, stop=True)
                                t.done(last, "pX")
                            else:
                                out = job(("Y", l, g), "Y", g + 1)
                                for c in range(g * CPG, (g + 1) * CPG):
                                    last = mm(ck(out, c % CPG), ck(PP, c), ck(Y_, c), start=True, stop=True)
                                t.done(last, "pY")

                    t.wait("wh", 16)
                    for b, (n_, free) in enumerate((("F", "thF"), ("Q", "qhat"), ("Z", "zh"))):
                        for g in range(NG):
                            project(WH, b, n_, g, free)
                    level(0)
                    level(1)
                    for g in range(NG):
                        out = job(("V", g), "v", g + 1)
                        for c in range(CPG):
                            s = (g * CPG + c) * P
                            for k in range(KD):
                                last = mm(out[:, c * P:(c + 1) * P], hT[:, k, s:s + P], WH[:, 3, k, :],
                                          start=(k == 0), stop=(k == KD - 1))
                        t.done(last, "pV")
                    level(2)
                    level(3)
                    t.wait("wg", 16)
                    for g in range(NG):
                        project(WG, 0, "Gq", g, "rawq")
                    t.wait("kl", 1)
                    turned("KL", "klt", H["kl"])
                    t.wait("MF", 2)
                    products("AF", "att", H["m1"], H["m0"], stage="pA", at=8)
                    products("DS", "hs", H["klt"], H["v"], need="klt", per=CPG)
                    for g in range(NG):
                        project(WG, 1, "Gk", g, "rawk")
                    t.wait("init", 1)
                    for g in range(NG):
                        out = job(("GR", g), "dm", g + 1)
                        for c in range(CPG):
                            last = mm(ck(out, c), ck(GB, g * CPG + c), UI, start=True, stop=True)
                        t.done(last, "pGR")
                    t.wait("att", 10)
                    t.wait("qe", 1)
                    for g in range(NG):
                        t.wait("hs", CPG * g + CPG - 1)
                        out = job(("OH", g), "sqh", g + 1)
                        for c in range(g * CPG, (g + 1) * CPG):
                            mm(ck(out, c % CPG), SH[:, c, :], ck(H["qe"], c), start=True, stop=False)
                            last = mm(ck(out, c % CPG), ck(H["v"], c), ck(H["att"], c), start=False, stop=True)
                        t.done(last, "pOH")
                    project(WG, 2, "Gv", 0, "rawv")
                    for g in range(NG):
                        t.wait("sqh", g + 1)
                        t.done(mm(job(("NH", g), "lnh", g + 1)[:], ones, gs(H["kh"], g), start=True, stop=True), "pNH")
                    for m, (n_, g) in enumerate((("k", 0), ("k", 1), ("q", 0), ("q", 1))):
                        t.wait("sqc", (3 if n_ == "k" else 1) + g)
                        out = job(("N", m), "lnc", m + 1)
                        t.done(mm(out[:], ones, gs(tmp[n_], g), start=True, stop=True), "pN")
                    project(WG, 2, "Gv", 1, "rawv")
                    t.wait("nrm", 2)
                    products("KK", "A", conv["k"], conv["k"])
                    turned("KT", "kdec", conv["k"])
                    turned("AT", "at", A_, need="A")
                    for l in range(5):
                        solve(l)
                    t.wait("c2", 3)
                    turned("VT", "rv", conv["v"])
                    t.wait("nrm", 4)
                    products("QK", "qkd", conv["k"], conv["q"])
                    solve(5)
                    for g in range(NG):
                        t.wait("rk", g + 1)
                        t.wait("Y", g + 1)
                        out = job(("WT", g), "nw", g + 1)
                        for c in range(g * CPG, (g + 1) * CPG):
                            last = mm(ck(out, c % CPG), ck(RK, c), ck(Y_, c), start=True, stop=True)
                        t.done(last, "pWT")
                    for c in range(NC):
                        g = c // CPG
                        if c % CPG == 0:
                            for stage in ("rv", "nw", "kdec", "qkd", "qg"):
                                t.wait(stage, g + 1)
                            o, gate = job(("OG", g), "sqg", g + 1), job(("Gz", g), "zg", g + 1)
                        out = job(("VN", c), "vn", c + 1)
                        mm(out[:, 0:P], ck(Y_, c), ck(RV, c), start=True, stop=False)
                        if c:
                            t.wait("sg", c)
                        t.done(mm(out[:, 0:P], ck(NW, c), SG[:], start=False, stop=True), "pVN")
                        mm(ck(o, c % CPG), SG[:], ck(QG, c), start=True, stop=False)
                        part(WG, 3, g, gate, [2 * (c % CPG)])
                        t.wait("vn", c + 1)
                        out = job(("S", c), "sg", c + 1)
                        t.done(mm(out[:, 0:P], ck(KDEC, c), VN[:, c % 2, :], start=True, stop=True), "pS")
                        last = mm(ck(o, c % CPG), VN[:, c % 2, :], ck(QKD, c), start=False, stop=True)
                        if c % CPG == CPG - 1:
                            t.done(last, "pOG")
                        last = part(WG, 3, g, gate, [2 * (c % CPG) + 1])
                        if c % CPG == CPG - 1:
                            t.done(last, "pGZ")
                    for g in range(NG):
                        t.wait("sqg", g + 1)
                        t.done(mm(job(("NG", g), "lng", g + 1)[:], ones, gs(tmp["q"], g), start=True, stop=True), "pNG")
                    for free in sorted(emptied.values(), reverse=True):
                        t.wait(*free)
                    t.hold()
                    t.close()
                n.close()


def ht_evac(nc, n, V, hT, nw, ps, t_, q):
    j = 2 * t_ + q
    n.wait("tr", j + 1)
    w = nw[:, 4 * q:4 * q + 4].unsqueeze(2).to_broadcast([P, 4, P])
    n.done(V.tensor_tensor(hT[:, 4 * q:4 * q + 4, t_ * P:(t_ + 1) * P],
                           ps[j % 6][:].rearrange("p (k t) -> p k t", t=P), w, ALU.mult), "ht")


def router(nc, a, pool_dma, kept):
    with ExitStack() as ctx:
        def sb(name, *shape, dt=F32):
            return ctx.enter_context(nc.sbuf_tensor("r_" + name, [P, *shape], dt))

        cst = sb("cst", C_N)
        wo, wr = sb("wo", KD, D), sb("wr", KD, EPG + NE)
        wo_hi, wo_lo = sb("wo_hi", KD, D, dt=F32R), sb("wo_lo", KD, D, dt=F32R)
        mix_hi = [sb(f"mix_hi{i}", KD, P, dt=F32R) for i in range(2)]
        mix_lo = [sb(f"mix_lo{i}", KD, P, dt=F32R) for i in range(2)]
        wn = sb("wn", D)
        mixT = [sb(f"mixT{i}", KD, P) for i in range(2)]
        xt = [sb(f"xt{i}", D) for i in range(2)]
        xn = [sb(f"xn{i}", D) for i in range(2)]
        xnT = [sb(f"xnT{i}", KD, P) for i in range(2)]
        junk = sb("junk", D)
        st = sb("st", 2, 8)
        lg = sb("lg", 2, EPG + NE)
        rt = sb("rt", 2, 32)
        m8, i8, i8b = sb("m8", 3, 8), sb("i8", 8, dt=U32), sb("i8b", 8, dt=U32)
        prod, esel = sb("prod", EPG, EPG), sb("esel", EPG)
        oh = sb("oh", 2, 4, NE)
        cnt = sb("cnt", NE)
        tab = kept["gates"]
        sel = sb("sel", NT, NE)
        blk, base = sb("blk", 3, NE), sb("base", NE)
        blk_i = sb("blk_i", 2, NE, dt=I32)
        row_hot, block_id = sb("row_hot", 2 * NT, P), sb("block_id", 2 * NT, NSLOT)
        ri = sb("ri", 3, 2 * NT, dt=I32)
        rf = sb("rf", 5, 2 * NT)
        number = sb("number", 2 * NT)
        rows, slots = kept["rows"], kept["slots"]
        late, expert, miss = sb("late", NE), sb("expert", P), sb("miss", NSLOT)
        ps = [ctx.enter_context(nc.psum_tensor(f"r_ps{i}", [P, GRP], F32)) for i in range(8)]
        ident, US, ones = cst[:, C_ID:C_ID + P], cst[:, C_US:C_US + P], cst[:, C_ONE:C_ONE + P]
        i64, i8c = cst[:, C_I64:C_I64 + NE], cst[:, C_I8:C_I8 + EPG]

        PER = dict(hi=1, lo=1, po=2, h=2, sq=1, ln=1, r0=1, nt=4, xn=1, ptr=2, ev=2, plg=1, lg=1, v=19, pe=2, prk=1, rk=7)
        O = {n: nc.alloc_semaphore("r_" + n) for n in PER}
        O |= {n + str(i): nc.alloc_semaphore(f"r_{n}{i}") for n in ("mix", "xt", "hout", "xnout") for i in range(2)}
        O |= {n: nc.alloc_semaphore("r_" + n) for n in ("const", "start", "whi", "wlo", "table", "placed", "pexpert", "prows")}
        block = ctx.enter_context(nc.Block())

        def steps(eng, step, lag):
            for n in range(2):
                step(n, n, 0)
            with eng.Fori(1, NT // 2 - 1) as j:
                for i in range(2):
                    step(j * 2 + i, i, j)
            for n in range(NT - 2, NT + lag):
                step(n, n % 2, n // 2)

        def within(n, lo=0):
            return lo <= n < NT if isinstance(n, int) else True

        def waits(eng):
            def wait(name, n, count):
                eng.wait_ge(O[name], n * PER[name] + count)
            return wait

        @block.sync
        def _(sp):
            sp.dma_start(cst[:], a["consts"]).then_inc(O["const"], 16)
            sp.dma_start(kept["ident"][:], a["consts"][:, C_ID:C_ID + P]).then_inc(O["const"], 16)
            sp.dma_start(wo[:], a["w_out"]).then_inc(O["const"], 16)
            sp.dma_start(wr[:], a["w_router"]).then_inc(O["const"], 16)
            sp.dma_start(wn[:], a["norm_moe"].partition_broadcast(P)).then_inc(O["const"], 16)
            wait = waits(sp)

            def load(n, i, j):
                rows = bass.ds(n * P, P)
                if within(n, 2):
                    wait("lo", n - 2, 1)
                    sp.nop(nofuse=True)
                sp.dma_start(mixT[i][:], a["mix"][:, :, rows].rearrange("k p t -> p k t")).then_inc(O[f"mix{i}"], 16)
                if within(n, 2):
                    sp.wait_ge(O[f"hout{i}"], j * 16)
                    sp.nop(nofuse=True)
                    wait("xn", n - 2, 1)
                    sp.nop(nofuse=True)
                sp.dma_start(xt[i][:], a["x"][rows, :]).then_inc(O[f"xt{i}"], 16)

            steps(sp, load, 0)
            for i in range(2):
                sp.wait_ge(O[f"hout{i}"], NT // 2 * 16)
                sp.wait_ge(O[f"xnout{i}"], NT // 2 * 16)

        @block.gpsimd
        def _(pool):
            nc.gpsimd.memset(cnt[:], 0.0).then_inc(O["start"], 1)

        @block.scalar
        def _(act):
            A = nc.scalar.activation
            act.wait_ge(O["const"], 80)
            wait = waits(act)

            def split_hi(n, i, j):
                act.wait_ge(O[f"mix{i}"], j * 16 + 16)
                A(mix_hi[i][:], mixT[i][:], ACT.Copy).then_inc(O["hi"], 1)

            for k in range(KD):
                A(wo_hi[:, k], wo[:, k], ACT.Copy).then_inc(O["whi"], 1)
            for i in range(2):
                split_hi(i, i, 0)

            def step(n, i, j):
                rows = bass.ds(n * P, P)
                if within(n):
                    wait("h", n, 2)
                    act.dma_start(a["h"][rows, :], xt[i][:]).then_inc(O[f"hout{i}"], 16)
                    A(junk[:], xt[i][:], ACT.Square, accum_out=st[:, i, 0:1]).then_inc(O["sq"], 1)
                    wait("sq", n, 1)
                    A(st[:, i, 1:2], st[:, i, 0:1], ACT.Ln, scale=1.0 / D,
                      bias=cst[:, C_COL + COL_EPS:C_COL + COL_EPS + 1]).then_inc(O["ln"], 1)
                    wait("ln", n, 1)
                    A(st[:, i, 2:3], st[:, i, 1:2], ACT.Exp, scale=-0.5).then_inc(O["r0"], 1)
                if within(n + 2):
                    split_hi(n + 2, i, j + 1)
                if within(n - 1):
                    r = rt[:, 1 - i]
                    wait("v", n - 1, 2)
                    A(r[:, 8:16], lg[:, 1 - i, 0:EPG], ACT.Exp, bias=r[:, 0:1], accum_out=r[:, 1:2]).then_inc(O["pe"], 1)
                    wait("v", n - 1, 10)
                    A(r[:, 3:4], r[:, 2:3], ACT.Exp).then_inc(O["pe"], 1)
                if within(n):
                    wait("xn", n, 1)
                    act.dma_start(a["xn"][rows, :], xn[i][:]).then_inc(O[f"xnout{i}"], 16)
                    for q in range(2):
                        wait("ptr", n, q + 1)
                        A(xnT[i][:, 4 * q:4 * q + 4, :].rearrange("p k t -> p (k t)"), ps[4 + q][:], ACT.Copy)\
                            .then_inc(O["ev"], 1)

            steps(act, step, 1)

        @block.vector
        def _(dve):
            V = nc.vector
            dve.wait_ge(O["const"], 80)
            dve.wait_ge(O["start"], 1)
            wait = waits(dve)

            def chain(name, n):
                done = [0]

                def v(ins, hold=False):
                    ins.then_inc(O[name], 1)
                    done[0] += 1
                    wait(name, n, done[0])
                    if hold:
                        dve.nop(nofuse=True)
                return v

            def split_lo(n, i):
                wait("hi", n, 1)
                V.tensor_tensor(mix_lo[i][:], mixT[i][:], mix_hi[i][:].bitcast(F32), ALU.subtract).then_inc(O["lo"], 1)

            for k in range(KD):
                dve.wait_ge(O["whi"], k + 1)
                V.tensor_tensor(wo_lo[:, k], wo[:, k], wo_hi[:, k].bitcast(F32), ALU.subtract).then_inc(O["wlo"], 1)
            for i in range(2):
                split_lo(i, i)

            def residual(n, i, j):
                dve.wait_ge(O[f"xt{i}"], j * 16 + 16)
                for q in range(2):
                    wait("po", n, q + 1)
                    hq = xt[i][:, q * GRP:(q + 1) * GRP]
                    V.tensor_tensor(hq, hq, ps[2 * i + q][:], ALU.add).then_inc(O["h"], 1)

            def norm(n, i, j):
                y = lambda k: st[:, i, k:k + 1]
                wait("r0", n, 1)
                V.tensor_scalar(y(3), y(0), 1.0 / D, EPS, ALU.mult, ALU.add)
                V.tensor_tensor(y(4), y(2), y(2), ALU.mult).then_inc(O["nt"], 1)
                wait("nt", n, 1)
                V.tensor_tensor(y(5), y(4), y(3), ALU.mult).then_inc(O["nt"], 1)
                wait("nt", n, 2)
                V.tensor_scalar(y(6), y(5), -0.5, 1.5, ALU.mult, ALU.add).then_inc(O["nt"], 1)
                wait("nt", n, 3)
                V.tensor_tensor(y(7), y(6), y(2), ALU.mult).then_inc(O["nt"], 1)
                wait("nt", n, 4)
                if within(n, 2):
                    dve.wait_ge(O[f"xnout{i}"], j * 16)
                V.scalar_tensor_tensor(xn[i][:], xt[i][:], y(7), wn[:], ALU.mult, ALU.mult).then_inc(O["xn"], 1)

            def choose(n, i):
                v = chain("v", n)
                r = rt[:, i]
                wait("plg", n, 1)
                V.tensor_copy(lg[:, i, :], ps[6][:, 0:EPG + NE]).then_inc(O["lg"], 1)
                wait("lg", n, 1)
                dve.nop(nofuse=True)
                v(V.max(m8[:, 0], lg[:, i, 0:EPG]))
                v(V.tensor_scalar(r[:, 0:1], m8[:, 0, 0:1], -1.0, None, ALU.mult), hold=True)
                v(V.max_index(i8[:], m8[:, 0], lg[:, i, 0:EPG]))
                v(V.tensor_copy(r[:, 4:5], i8[:, 0:1]))
                v(V.tensor_scalar(m8[:, 2], i8c, r[:, 4:5], None, ALU.is_equal))
                v(V.tensor_tensor(prod[:], lg[:, i, EPG:].rearrange("p (g e) -> p e g", g=EPG),
                                  m8[:, 2].unsqueeze(1).to_broadcast([P, EPG, EPG]), ALU.mult))
                v(V.tensor_reduce(esel[:], prod[:], AX.X, ALU.add), hold=True)
                v(V.max(m8[:, 1], esel[:]), hold=True)
                v(V.max_index(i8b[:], m8[:, 1], esel[:]))
                v(V.tensor_tensor(r[:, 2:3], m8[:, 1, 1:2], m8[:, 1, 0:1], ALU.subtract))
                v(V.tensor_copy(r[:, 16:18], i8b[:, 0:2]))
                v(V.tensor_scalar(r[:, 5:6], r[:, 4:5], float(EPG), None, ALU.mult))
                v(V.tensor_scalar(r[:, 24:26], r[:, 16:18], r[:, 5:6], None, ALU.add))
                v(V.tensor_scalar(oh[:, i, 0], i64, r[:, 24:25], None, ALU.is_equal))
                v(V.tensor_scalar(oh[:, i, 1], i64, r[:, 25:26], None, ALU.is_equal))
                v(V.tensor_tensor(oh[:, i, 2], oh[:, i, 0], oh[:, i, 1], ALU.add))
                wait("pe", n, 2)
                v(V.tensor_scalar(r[:, 6:7], r[:, 3:4], 1.0, r[:, 1:2], ALU.add, ALU.mult))
                v(V.reciprocal(r[:, 28:29], r[:, 6:7]))
                v(V.tensor_tensor(r[:, 29:30], r[:, 28:29], r[:, 3:4], ALU.mult))

            def rank(n, i):
                k = chain("rk", n)
                r, o = rt[:, i], oh[:, i]
                wait("prk", n, 1)
                k(V.tensor_tensor(o[:, 3], ps[7][:, 0:NE], cnt[:], ALU.add))
                V.tensor_tensor(o[:, 0], o[:, 0], o[:, 3], ALU.mult)
                k(V.tensor_tensor(o[:, 1], o[:, 1], o[:, 3], ALU.mult))
                k(V.tensor_reduce(r[:, 26:27], o[:, 0], AX.X, ALU.add))
                k(V.tensor_reduce(r[:, 27:28], o[:, 1], AX.X, ALU.add))
                k(V.tensor_tensor(cnt[:], ps[7][:, NE:2 * NE], cnt[:], ALU.add))
                k(V.memset(r[:, 30:32], 0.0), hold=True)
                k(V.tensor_copy(tab[:, bass.ds(n, 1), :].rearrange("p n k -> p (n k)"), r[:, 24:32]))

            def step(n, i, j):
                if within(n):
                    residual(n, i, j)
                if within(n - 2):
                    rank(n - 2, i)
                if within(n):
                    norm(n, i, j)
                if within(n + 2):
                    split_lo(n + 2, i)
                if within(n - 1):
                    choose(n - 1, 1 - i)

            steps(dve, step, 2)
            n = [0]

            def w(ins):
                n[0] += 1
                ins.then_inc(O["table"], 1)
                dve.wait_ge(O["table"], n[0])

            w(V.tensor_scalar(blk[:, 2], cnt[:], float(P - 1), None, ALU.add))
            w(V.tensor_copy(blk_i[:, 0], blk[:, 2]))
            w(V.tensor_scalar(blk_i[:, 1], blk_i[:, 0], 7, None, ALU.arith_shift_right))
            nb, up = blk[:, 0], blk[:, 1]
            w(V.tensor_copy(nb, blk_i[:, 1]))
            w(V.tensor_tensor_scan(up, ones[:, 0:NE], nb, 0.0, ALU.mult, ALU.add))
            w(V.tensor_tensor(base[:], up, nb, ALU.subtract))
            w(V.tensor_scalar(late[:], up, cst[:, C_TOK:C_TOK + 1], None, ALU.is_le))
            w(V.tensor_reduce(rf[:, 0, 0:1], late[:], AX.X, ALU.add))
            w(V.tensor_scalar(rf[:, 0, 0:1], rf[:, 0, 0:1], float(NE - 1), None, ALU.min))
            w(V.tensor_copy(expert[:], rf[:, 0, 0:1].to_broadcast([P, P])))
            assert n[0] == EXPERT_STEP
            w(V.tensor_copy(slots[:, NSLOT:2 * NSLOT], up[:, NE - 1:NE].to_broadcast([P, NSLOT])))
            for i in range(2):
                w(V.tensor_tensor(sel[:], i64.unsqueeze(1).to_broadcast([P, NT, NE]),
                                  tab[:, :, i:i + 1].to_broadcast([P, NT, NE]), ALU.is_equal))
                w(V.tensor_tensor(sel[:], sel[:], base[:].unsqueeze(1).to_broadcast([P, NT, NE]), ALU.mult))
                w(V.tensor_reduce(rf[:, 0, i * NT:(i + 1) * NT], sel[:], AX.X, ALU.add))
                w(V.tensor_copy(ri[:, 0, i * NT:(i + 1) * NT], tab[:, :, 2 + i]))
                w(V.tensor_scalar(number[:, i * NT:(i + 1) * NT], cst[:, C_TOK:C_TOK + NT], float(T * i + 1), None, ALU.add))
            w(V.tensor_scalar(ri[:, 1], ri[:, 0], 7, None, ALU.arith_shift_right))
            w(V.tensor_scalar(ri[:, 2], ri[:, 0], P - 1, None, ALU.bitwise_and))
            w(V.tensor_copy(rf[:, 1], ri[:, 1]))
            w(V.tensor_copy(rf[:, 2], ri[:, 2]))
            w(V.tensor_tensor(rf[:, 3], rf[:, 0], rf[:, 1], ALU.add))
            dve.wait_ge(O["pexpert"], 1)
            w(V.tensor_copy(slots[:, 0:NSLOT], ps[1][:, 0:NSLOT]))
            w(V.tensor_tensor(row_hot[:], cst[:, C_SLOT:C_SLOT + P].unsqueeze(1).to_broadcast([P, 2 * NT, P]),
                              rf[:, 2].unsqueeze(2).to_broadcast([P, 2 * NT, P]), ALU.is_equal))
            assert n[0] == TABLE_STEPS
            for k in range(2 * NT):
                V.tensor_scalar(block_id[:, k], cst[:, C_SLOT:C_SLOT + NSLOT], rf[:, 3, k:k + 1], number[:, k:k + 1],
                                ALU.is_equal, ALU.mult).then_inc(O["placed"], 1)
            dve.wait_ge(O["prows"], 1)
            V.tensor_scalar(miss[:], ps[0][:, 0:NSLOT], 1.0, float(OOB), ALU.is_lt, ALU.mult).then_inc(O["placed"], 1)
            dve.wait_ge(O["placed"], 2 * NT + 1)
            V.scalar_tensor_tensor(rows[:], ps[0][:, 0:NSLOT], -1.0, miss[:], ALU.add, ALU.add)

        @block.tensor
        def _(pe):
            mm = nc.tensor.matmul
            pe.wait_ge(O["const"], 80)
            pe.wait_ge(O["wlo"], KD)
            wait = waits(pe)

            def out_proj(n, i, j):
                wait("lo", n, 1)
                for q in range(2):
                    if within(n, 2):
                        wait("h", n - 2, q + 1)
                    for k in range(KD):
                        cols = slice(q * GRP, (q + 1) * GRP)
                        mm(ps[2 * i + q][:], mix_hi[i][:, k, :], wo_hi[:, k, cols], start=(k == 0), stop=False)
                        mm(ps[2 * i + q][:], mix_hi[i][:, k, :], wo_lo[:, k, cols], start=False, stop=False)
                        last = mm(ps[2 * i + q][:], mix_lo[i][:, k, :], wo_hi[:, k, cols], start=False, stop=(k == KD - 1))
                    last.then_inc(O["po"], 1)

            def transposes(n, i):
                wait("xn", n, 1)
                for q in range(2):
                    if within(n, 1):
                        wait("ev", n - 1, q + 1)
                    for k in range(4):
                        last = nc.tensor.transpose(ps[4 + q][:, k * P:(k + 1) * P],
                                                   xn[i][:, (4 * q + k) * P:(4 * q + k + 1) * P], ident)
                    last.then_inc(O["ptr"], 1)

            def logits(n, i):
                wait("ev", n, 2)
                if within(n, 1):
                    wait("lg", n - 1, 1)
                for k in range(KD):
                    last = mm(ps[6][:, 0:EPG + NE], xnT[i][:, k, :], wr[:, k, :], start=(k == 0), stop=(k == KD - 1))
                last.then_inc(O["plg"], 1)

            def ranks(n, i):
                wait("v", n, 16)
                if within(n, 1):
                    wait("rk", n - 1, 5)
                mm(ps[7][:, 0:NE], US, oh[:, i, 2], start=True, stop=True)
                mm(ps[7][:, NE:2 * NE], ones, oh[:, i, 2], start=True, stop=True).then_inc(O["prk"], 1)

            def step(n, i, j):
                if within(n + 1):
                    out_proj(n + 1, 1 - i, j + i)
                if within(n):
                    transposes(n, i)
                if within(n - 1):
                    ranks(n - 1, 1 - i)
                if within(n):
                    logits(n, i)

            out_proj(0, 0, 0)
            steps(pe, step, 1)
            pe.wait_ge(O["table"], EXPERT_STEP)
            mm(ps[1][:, 0:P], expert[:], ident, start=True, stop=True).then_inc(O["pexpert"], 1)
            pe.wait_ge(O["table"], TABLE_STEPS)
            for k in range(2 * NT):
                pe.wait_ge(O["placed"], k + 1)
                last = mm(ps[0][:, 0:NSLOT], row_hot[:, k], block_id[:, k], start=(k == 0), stop=(k == 2 * NT - 1))
            last.then_inc(O["prows"], 1)


def experts(nc, a, pool_dma, kept):
    with ExitStack() as ctx:
        def sb(name, *shape, dt=F32):
            return ctx.enter_context(nc.sbuf_tensor("e_" + name, [P, *shape], dt))

        NB = EB
        KF = FF // P
        rows, slots, ident = kept["rows"], kept["slots"], kept["ident"][:]
        tok, late = sb("tok", NSLOT + NB, dt=I32), sb("late", NSLOT)
        gi = [sb(f"gi{i}", 1, dt=I32) for i in range(NB)]
        oi = [sb(f"oi{i}", 1, dt=I32) for i in range(NB)]
        wg = [sb(f"wg{i}", KD, FF) for i in range(NB)]
        wu = [sb(f"wu{i}", KD, FF) for i in range(NB)]
        wd = [sb(f"wd{i}", KF, D) for i in range(NB)]
        xg = [sb(f"xg{i}", D) for i in range(NB)]
        xT = [sb(f"xT{i}", KD, P) for i in range(NB)]
        th = [sb(f"th{i}", FF) for i in range(2)]
        h = sb("h", FF)
        hT = sb("hT", KF, P)
        y = [sb(f"y{i}", D) for i in range(NB)]
        pgu = [ctx.enter_context(nc.psum_tensor(f"e_gu{i}", [P, 2 * FF], F32)) for i in range(2)]
        px = [ctx.enter_context(nc.psum_tensor(f"e_px{i}", [P, GRP], F32)) for i in range(2)]
        ph = ctx.enter_context(nc.psum_tensor("e_ph", [P, GRP], F32))
        py = [ctx.enter_context(nc.psum_tensor(f"e_py{i}", [P, GRP], F32)) for i in range(2)]
        names = ["zero", "tok", "gi", "oi", "px", "xT", "pgu", "th", "g", "h", "ph", "hT", "py", "y"] \
            + [f"w{i}" for i in range(NB)]
        E = {n: nc.alloc_semaphore("e_" + n) for n in names}
        E |= {n[2:]: sem for n, sem in pool_dma.items() if n.startswith("e_")}
        block = ctx.enter_context(nc.Block())

        def load_count(eng):
            return eng.value_load(slots[0:1, NSLOT:NSLOT + 1], min_val=2 * T // P, max_val=NSLOT - 1)

        def uses(j, i):
            return j + 1 + i // NB

        def y_written_out(eng, i, j):
            with eng.If(j > 0):
                eng.wait_ge(E[f"out{i}"], j * 16)
                eng.nop(nofuse=True)

        @block.sync
        def _(sp):
            count = load_count(sp)
            with sp.Fori(0, NSLOT // NB) as j:
                for i in range(NB):
                    s = j * NB + i
                    with sp.If(s < count):
                        e = sp.value_load(slots[0:1, bass.ds(s, 1)], min_val=0, max_val=NE - 1)
                        sp.wait_ge(E["pgu"], s + 1)
                        sp.nop(nofuse=True)
                        sp.dma_start(wg[i][:], a["w_gate"][bass.ds(e, 1)].rearrange("e (p k) f -> p (e k) f", k=KD))\
                            .then_inc(E[f"w{i}"], 16)
                        sp.dma_start(wu[i][:], a["w_up"][bass.ds(e, 1)].rearrange("e (p k) f -> p (e k) f", k=KD))\
                            .then_inc(E[f"w{i}"], 16)
                        sp.wait_ge(E["py"], s * 2 + 2)
                        sp.nop(nofuse=True)
                        sp.dma_start(wd[i][:], a["w_down"][bass.ds(e, 1)].rearrange("e (p k) d -> p (e k) d", k=KF))\
                            .then_inc(E[f"w{i}"], 16)

        @block.gpsimd
        def _(pool):
            for i in range(NB):
                last = nc.gpsimd.memset(xg[i][:], 0.0)
            last.then_inc(E["zero"], 1)
            pool.wait_ge(E["zero"], 1)
            count = load_count(pool)
            pool.wait_ge(E["tok"], 2)

            def gather(n, i):
                nc.gpsimd.tensor_copy(gi[i][:], tok[:, bass.ds(n, 1)]).then_inc(E["gi"], 1)
                pool.wait_ge(E["gi"], n + 1)
                pool.nop(nofuse=True)
                pool.indirect_dma_start(out=xg[i][:], out_offset=None, in_=a["xn"],
                                        in_offset=bass.IndirectOffsetOnAxis(ap=gi[i][:], axis=0),
                                        bounds_check=T - 1, oob_is_err=False).then_inc(E[f"x{i}"], 16)

            for i in range(NB):
                gather(i, i)
            with pool.Fori(0, NSLOT // NB) as j:
                for i in range(NB):
                    s = j * NB + i
                    with pool.If(s < count):
                        y_written_out(pool, i, j)
                        nc.gpsimd.tensor_copy(oi[i][:], rows[:, bass.ds(s, 1)]).then_inc(E["oi"], 1)
                        pool.wait_ge(E["oi"], s + 1)
                        pool.nop(nofuse=True)
                        pool.wait_ge(E["y"], 2 * s + 4)
                        pool.nop(nofuse=True)
                        pool.indirect_dma_start(out=a["y"], in_=y[i][:], in_offset=None,
                                                out_offset=bass.IndirectOffsetOnAxis(ap=oi[i][:], axis=0),
                                                bounds_check=2 * T - 1, oob_is_err=False).then_inc(E[f"out{i}"], 16)
                    with pool.If(s + NB < count):
                        pool.wait_ge(E["px"], 2 * s + 2)
                        pool.nop(nofuse=True)
                        gather(s + NB, i)
            for i in range(NB):
                pool.wait_ge(E[f"out{i}"], ((count + (NB - 1 - i)) // NB) * 16)
                pool.nop(nofuse=True)

        @block.scalar
        def _(act):
            A = nc.scalar.activation
            count = load_count(act)

            def x_evac(n, i):
                act.wait_ge(E["px"], 2 * n + 1)
                A(xT[i][:, 0:4, :].rearrange("p k t -> p (k t)"), px[0][:], ACT.Copy).then_inc(E["xT"], 1)

            def tanh(n, i, first=False):
                act.wait_ge(E["pgu"], n + 1 + NB)
                if not first:
                    act.wait_ge(E["h"], n)
                A(th[i % 2][:], pgu[i % 2][:, 0:FF], ACT.Tanh, scale=0.5).then_inc(E["th"], 1)

            x_evac(0, 0)
            tanh(0, 0, first=True)
            x_evac(1, 1)
            with act.Fori(0, NSLOT // NB) as j:
                for i in range(NB):
                    s = j * NB + i
                    with act.If(s < count):
                        with act.If(s + 1 < count):
                            tanh(s + 1, i + 1)
                        act.wait_ge(E["ph"], s + 1)
                        A(hT[:].rearrange("p k t -> p (k t)"), ph[:, 0:FF], ACT.Copy, scale=0.5).then_inc(E["hT"], 1)
                        with act.If(s + 2 < count):
                            x_evac(s + 2, (i + 2) % NB)
                        y_written_out(act, i, j)
                        act.wait_ge(E["py"], 2 * s + 1 + 2 * NB)
                        A(y[i][:, 0:GRP], py[0][:], ACT.Copy).then_inc(E["y"], 1)

        @block.vector
        def _(dve):
            V = nc.vector
            V.tensor_scalar(late[:], rows[:], float(T), -float(T), ALU.is_ge, ALU.mult).then_inc(E["tok"], 1)
            dve.wait_ge(E["tok"], 1)
            V.tensor_tensor(tok[:, 0:NSLOT], rows[:], late[:], ALU.add).then_inc(E["tok"], 1)
            V.memset(h[:], 0.0).then_inc(E["y"], 2)
            V.memset(th[0][:], 0.0).then_inc(E["pgu"], NB)
            V.memset(th[1][:], 0.0).then_inc(E["py"], 2 * NB)
            count = load_count(dve)
            dve.wait_ge(E["y"], 2)

            def x_evac(n, i):
                dve.wait_ge(E["px"], 2 * n + 2)
                V.tensor_copy(xT[i][:, 4:8, :].rearrange("p k t -> p (k t)"), px[1][:]).then_inc(E["xT"], 1)

            def swiglu(n, i, first=False):
                dve.wait_ge(E["th"], n + 1)
                V.scalar_tensor_tensor(th[i % 2][:], th[i % 2][:], 1.0, pgu[i % 2][:, 0:FF], ALU.add, ALU.mult)\
                    .then_inc(E["g"], 1)
                dve.wait_ge(E["g"], n + 1)
                if not first:
                    dve.wait_ge(E["ph"], n)
                V.tensor_tensor(h[:], th[i % 2][:], pgu[i % 2][:, FF:2 * FF], ALU.mult).then_inc(E["h"], 1)

            x_evac(0, 0)
            swiglu(0, 0, first=True)
            x_evac(1, 1)
            with dve.Fori(0, NSLOT // NB) as j:
                for i in range(NB):
                    s = j * NB + i
                    with dve.If(s < count):
                        with dve.If(s + 1 < count):
                            swiglu(s + 1, i + 1)
                        with dve.If(s + 2 < count):
                            x_evac(s + 2, (i + 2) % NB)
                        y_written_out(dve, i, j)
                        dve.wait_ge(E["py"], 2 * s + 2 + 2 * NB)
                        V.tensor_copy(y[i][:, GRP:D], py[1][:]).then_inc(E["y"], 1)

        @block.tensor
        def _(pe):
            mm = nc.tensor.matmul
            count = load_count(pe)

            def x_transposes(n, j, i, first=False):
                pe.wait_ge(E[f"x{i % NB}"], uses(j, i) * 16)
                if not first:
                    pe.wait_ge(E["xT"], 2 * n)
                xv = xg[i % NB][:].rearrange("t (p k) -> t k p", k=KD)
                for q in range(2):
                    for k in range(4):
                        last = nc.tensor.transpose(px[q][:, k * P:(k + 1) * P], xv[:, 4 * q + k, :], ident)
                    last.then_inc(E["px"], 1)

            def gate_up(n, j, i):
                pe.wait_ge(E[f"w{i % NB}"], uses(j, i) * 48)
                pe.wait_ge(E["xT"], 2 * n + 2)
                for q, w in enumerate((wg[i % NB], wu[i % NB])):
                    for k in range(KD):
                        last = mm(pgu[i % 2][:, q * FF:(q + 1) * FF], xT[i % NB][:, k, :], w[:, k, :],
                                  start=(k == 0), stop=(k == KD - 1))
                last.then_inc(E["pgu"], 1)

            x_transposes(0, 0, 0, first=True)
            gate_up(0, 0, 0)
            x_transposes(1, 0, 1)
            with pe.Fori(0, NSLOT // NB) as j:
                for i in range(NB):
                    s = j * NB + i
                    with pe.If(s < count):
                        with pe.If(s + 1 < count):
                            gate_up(s + 1, j, i + 1)
                        pe.wait_ge(E["h"], s + 1)
                        hv = h[:].rearrange("t (p k) -> t k p", k=KF)
                        for k in range(KF):
                            last = nc.tensor.transpose(ph[:, k * P:(k + 1) * P], hv[:, k, :], ident)
                        last.then_inc(E["ph"], 1)
                        with pe.If(s + 2 < count):
                            x_transposes(s + 2, j, i + 2)
                        pe.wait_ge(E["hT"], s + 1)
                        pe.wait_ge(E["y"], 2 * s + 2)
                        for q in range(2):
                            for k in range(KF):
                                last = mm(py[q][:], hT[:, k, :], wd[i][:, k, q * GRP:(q + 1) * GRP],
                                          start=(k == 0), stop=(k == KF - 1))
                            last.then_inc(E["py"], 1)


def combine(nc, a, pool_dma, kept):
    with ExitStack() as ctx:
        def sb(name, *shape, dt=F32):
            return ctx.enter_context(nc.sbuf_tensor("c_" + name, [P, *shape], dt))

        NB = 4
        tab = kept["gates"]
        wn, eps = sb("wn", D), sb("eps", 4)
        ht = [sb(f"ht{i}", D) for i in range(NB)]
        yt = [sb(f"y{i}", 2, D) for i in range(NB)]
        junk, st = sb("junk", D), sb("st", NT, 8)
        names = ["start", "s1", "s2", "sq", "ln", "r0", "nt", "o"] + [f"{n}{i}" for i in range(NB) for n in ("h", "y", "out")]
        E = {n: nc.alloc_semaphore("c_" + n) for n in names}
        block = ctx.enter_context(nc.Block())

        @block.sync
        def _(sp):
            sp.dma_start(wn[:], a["final_norm"].partition_broadcast(P)).then_inc(E["start"], 16)
            sp.dma_start(eps[:], a["consts"][:, C_COL:C_COL + 4]).then_inc(E["start"], 16)
            for t in range(NT):
                i = t % NB
                if t >= NB:
                    sp.wait_ge(E[f"out{i}"], 16 * (t // NB))
                sp.dma_start(ht[i][:], a["h"][t * P:(t + 1) * P, :]).then_inc(E[f"h{i}"], 16)
                if t >= NB:
                    sp.wait_ge(E["s2"], t - NB + 1)
                sp.dma_start(yt[i][:], a["y"].rearrange("(k n p) d -> n p k d", k=2, p=P)[t]).then_inc(E[f"y{i}"], 16)

        @block.vector
        def _(dve):
            V = nc.vector
            dve.wait_ge(E["start"], 32)

            def norm(t):
                i = t % NB
                y = lambda k: st[:, t, k:k + 1]
                dve.wait_ge(E["r0"], t + 1)
                V.tensor_scalar(y(3), y(0), 1.0 / D, EPS, ALU.mult, ALU.add)
                V.tensor_tensor(y(4), y(2), y(2), ALU.mult).then_inc(E["nt"], 1)
                dve.wait_ge(E["nt"], 4 * t + 1)
                V.tensor_tensor(y(5), y(4), y(3), ALU.mult).then_inc(E["nt"], 1)
                dve.wait_ge(E["nt"], 4 * t + 2)
                V.tensor_scalar(y(6), y(5), -0.5, 1.5, ALU.mult, ALU.add).then_inc(E["nt"], 1)
                dve.wait_ge(E["nt"], 4 * t + 3)
                V.tensor_tensor(y(7), y(6), y(2), ALU.mult).then_inc(E["nt"], 1)
                dve.wait_ge(E["nt"], 4 * t + 4)
                V.scalar_tensor_tensor(ht[i][:], ht[i][:], y(7), wn[:], ALU.mult, ALU.mult).then_inc(E["o"], 1)

            for t in range(NT):
                i = t % NB
                dve.wait_ge(E[f"h{i}"], 16 * (t // NB + 1))
                dve.wait_ge(E[f"y{i}"], 16 * (t // NB + 1))
                V.scalar_tensor_tensor(ht[i][:], yt[i][:, 0], tab[:, t, 4:5], ht[i][:], ALU.mult, ALU.add)\
                    .then_inc(E["s1"], 1)
                dve.wait_ge(E["s1"], t + 1)
                V.scalar_tensor_tensor(ht[i][:], yt[i][:, 1], tab[:, t, 5:6], ht[i][:], ALU.mult, ALU.add)\
                    .then_inc(E["s2"], 1)
                if t:
                    norm(t - 1)
            norm(NT - 1)

        @block.scalar
        def _(act):
            A = nc.scalar.activation
            act.wait_ge(E["start"], 32)
            for t in range(NT):
                i = t % NB
                act.wait_ge(E["s2"], t + 1)
                if t:
                    act.wait_ge(E["sq"], t)
                A(junk[:], ht[i][:], ACT.Square, accum_out=st[:, t, 0:1]).then_inc(E["sq"], 1)
                act.wait_ge(E["sq"], t + 1)
                A(st[:, t, 1:2], st[:, t, 0:1], ACT.Ln, scale=1.0 / D, bias=eps[:, COL_EPS:COL_EPS + 1]).then_inc(E["ln"], 1)
                act.wait_ge(E["ln"], t + 1)
                A(st[:, t, 2:3], st[:, t, 1:2], ACT.Exp, scale=-0.5).then_inc(E["r0"], 1)
                if t:
                    act.wait_ge(E["o"], t)
                    act.dma_start(a["out"][(t - 1) * P:t * P, :], ht[(t - 1) % NB][:]).then_inc(E[f"out{(t - 1) % NB}"], 16)
            act.wait_ge(E["o"], NT)
            act.dma_start(a["out"][(NT - 1) * P:, :], ht[(NT - 1) % NB][:]).then_inc(E[f"out{(NT - 1) % NB}"], 16)
            for i in range(NB):
                act.wait_ge(E[f"out{i}"], 16 * NT // NB)


def build(nc, a):
    pool_dma = {n: nc.alloc_semaphore(n) for n in ("s_outh", "s_outg", *(f"e_{n}{i}" for n in ("x", "out") for i in range(EB)))}
    with ExitStack() as ctx:
        kept = {}
        for part in (trunk, router, experts, combine):
            if part is router:
                kept.update(tables(nc, ctx))
            before = set(nc.free_semaphores)
            part(nc, a, pool_dma, kept)
            if part is not combine:
                nc.clear_and_free_semaphores(sorted(before - set(nc.free_semaphores)))
                nc.all_engine_barrier()


def tables(nc, ctx):
    sb = lambda name, *shape, dt=F32: ctx.enter_context(nc.sbuf_tensor("k_" + name, [P, *shape], dt))
    return dict(rows=sb("rows", NSLOT, dt=I32), slots=sb("slots", 2 * NSLOT, dt=I32), gates=sb("gates", NT, 8),
                ident=sb("ident", P))


EXPERT_STEP = 10
TABLE_STEPS = 28

SCRATCH = {
    "mix": ((2 * HEADS, P, T), F32), "h": ((T, D), F32), "xn": ((T, D), F32), "y": ((2 * T, D), F32),
}



def layout(x, norm_mix_w, w_in, hgrn_lb_logits, hgrn_onorm_w, gdn_conv_w, gdn_a_log, gdn_dt_bias,
           gdn_onorm_w, w_out, norm_moe_w, router_group_w, router_expert_w, expert_w_gate,
           expert_w_up, expert_w_down, final_norm_w):
    asc = np.ascontiguousarray
    w = np.asarray(w_in)[0]
    starts = [512, 0, 1536, 1024, 2048, 2560, 3072, 3584]
    blocks = np.stack([w[:, s:s + 512].reshape(KD, P, HEADS, P) for s in starts])
    consts, masks = constant_tables()
    return {
        "consts": consts, "masks": masks,
        "x": asc(np.asarray(x)[0]),
        "norm_mix": asc(np.asarray(norm_mix_w)[0].reshape(KD, P).T),
        "onorm": asc(np.stack([np.asarray(hgrn_onorm_w)[0], np.asarray(gdn_onorm_w)[0]], 1)),
        "w_proj": asc(blocks.transpose(3, 2, 0, 1, 4)),
        "w_ab": asc(w[:, 4096:4104].reshape(KD, P, 8).transpose(1, 0, 2)),
        "lb": asc(np.asarray(hgrn_lb_logits).reshape(2, HEADS, P).transpose(2, 0, 1)),
        "a_log": asc(np.asarray(gdn_a_log)[0]), "dt_bias": asc(np.asarray(gdn_dt_bias)[0]),
        "conv_w": asc(np.asarray(gdn_conv_w)[0].reshape(TAPS, 3, HEADS, P).transpose(3, 2, 1, 0)
                      .reshape(P, HEADS, 3 * TAPS)),
        "w_out": asc(np.asarray(w_out)[0].reshape(KD, P, D).transpose(1, 0, 2)),
        "norm_moe": asc(np.asarray(norm_moe_w)[0]), "final_norm": asc(np.asarray(final_norm_w)),
        "w_router": asc(np.concatenate([np.asarray(router_group_w)[0], np.asarray(router_expert_w)[0]], 1)
                        .reshape(KD, P, 72).transpose(1, 0, 2)),
        "w_gate": np.asarray(expert_w_gate)[0], "w_up": np.asarray(expert_w_up)[0],
        "w_down": np.asarray(expert_w_down)[0],
    }


def kernel(**inputs):
    import concourse.bacc as bacc
    from concourse.bass_utils import run_bass_kernel_spmd

    nc = bacc.Bacc("TRN2", target_bir_lowering=False, num_devices=1)
    arrays = layout(**inputs)
    a = {n: nc.dram_tensor("in_" + n, v.shape, mybir.dt.from_np(v.dtype), kind="ExternalInput").ap()
         for n, v in arrays.items()}
    for n, (shape, dt) in SCRATCH.items():
        a[n] = nc.dram_tensor("tmp_" + n, shape, dt).ap()
    a["out"] = nc.dram_tensor("out", (T, D), F32, kind="ExternalOutput").ap()
    build(nc, a)
    r = run_bass_kernel_spmd(nc, [{"in_" + n: v for n, v in arrays.items()}], core_ids=[0])
    return r.results[0]["out"].reshape(1, T, D)
```

```python
import math
from contextlib import ExitStack

import numpy as np

import concourse.bass as bass
from concourse import mybir

F32 = mybir.dt.float32
I32 = mybir.dt.int32
U32 = mybir.dt.uint32
U8 = mybir.dt.uint8
F32R = mybir.dt.float32r
ALU = mybir.AluOpType
ACT = mybir.ActivationFunctionType
AX = mybir.AxisListType

P = 128
T = 2048
D = 1024
KD = D // P
HEADS = 4
HALF = 1024
NHALF = T // HALF
NC = HALF // P
GRP = 512
NG = HALF // GRP
CPG = GRP // P
TAPS = 4
HALO = TAPS - 1
EPS = 1e-6
NE = 64
EPG = 8
FF = 256
NT = T // P
NSLOT = 96
EB = 4
HB = 8
OOB = 1 << 20
ATT_LEVELS = (64, 32, 16, 8)
SOLVE_LEVELS = (1, 2, 4, 8, 16, 32, 64)

C_ID, C_UI, C_ONE, C_SCAN = 0, 128, 256, 384
C_COL = C_SCAN + HALF
COL_EPS, COL_EPS4, COL_LNHQ, COL_LNGQ = range(4)
C_TRUNK = C_COL + 4
C_US = C_TRUNK
C_I64 = C_US + P
C_I8 = C_I64 + 64
C_SLOT = C_I8 + 8
C_TOK = C_SLOT + P
C_N = C_TOK + NT
M_SOL = 0
M_SOLT = M_SOL + 7 * 64
M_ATTF = M_SOLT + 7 * 64
M_N = M_ATTF + P


def constant_tables():
    c = np.zeros((P, C_N), np.float32)
    i = np.arange(P)
    c[:, C_ID:C_ID + P] = np.eye(P)
    c[:, C_UI:C_UI + P] = i[:, None] <= i[None, :]
    c[:, C_US:C_US + P] = i[:, None] < i[None, :]
    c[:, C_ONE:C_ONE + P] = 1.0
    c[:, C_SCAN:C_SCAN + HALF] = (np.arange(HALF) % P != 0)[None, :]
    c[:, C_I64:C_I64 + 64] = np.arange(64)[None, :]
    c[:, C_I8:C_I8 + 8] = np.arange(8)[None, :]
    c[:, C_SLOT:C_SLOT + P] = np.arange(P)[None, :]
    c[:, C_COL + COL_EPS] = EPS
    c[:, C_COL + COL_EPS4] = 4 * EPS
    c[:, C_COL + COL_LNHQ] = math.log(0.5 * P ** -0.5)
    c[:, C_COL + COL_LNGQ] = math.log(P ** -0.5)
    c[:, C_TOK:C_TOK + NT] = i[:, None] + P * np.arange(NT)[None, :]
    m = np.zeros((P, M_N), np.float32)
    for l, h in enumerate(SOLVE_LEVELS):
        early = i[i // h % 2 == 0]
        late = early + h
        m[:, M_SOL + l * 64:M_SOL + (l + 1) * 64] = i[:, None] // h == early[None, :] // h + 1
        m[:, M_SOLT + l * 64:M_SOLT + (l + 1) * 64] = i[:, None] // h == late[None, :] // h - 1
    m[:, M_ATTF:M_ATTF + P] = (i[:, None] // 8 == i[None, :] // 8) & (i[:, None] <= i[None, :])
    return c, m


def psum_banks():
    pair = lambda *names: [((n, g), None) for n in names for g in range(NG)]
    level = lambda l: [(("A", l, g), None) for g in range(NG)]
    solve = lambda l: [(("P", l, 0), None)] + [(("XT", l - 1, g), None) for g in range(NG if l else 0)] + \
        [(("P", l, 1), None)] + [(("X" if l < 5 else "Y", l, g), None) for g in range(NG)]
    jobs = pair("F", "Q", "Z") + level(0) + level(1) + pair("VF") + level(2) + level(3) + pair("V")
    jobs += pair("Gq", "KL", "AF", "DS", "Gk", "GR")
    jobs += [(("OH", g), 6 + g) for g in range(NG)] + [(("Gv", 0), None)]
    jobs += pair("NH") + [(("N", m), None) for m in range(4)] + [(("Gv", 1), 7)] + pair("KK")
    jobs += [(("QK", g), 6 + g) for g in range(NG)] + pair("AT")
    jobs += [(("KT", 0), None)] + solve(0)[:2] + [(("KT", 1), None)] + solve(0)[2:]
    for l in range(1, 5):
        jobs += solve(l)
    jobs += pair("VT") + solve(5) + pair("WT")
    jobs += [(("OG", g), 6 + g) for g in range(NG)] + [(("Gz", g), 4 + g) for g in range(NG)]
    for c in range(NC):
        jobs += [(("VN", c), c % 2), (("S", c), 2 + c % 2)]
    jobs += [(("NG", g), 6 + g) for g in range(NG)]
    bank, free = {}, 0
    for key, b in jobs:
        bank[key] = free % 6 if b is None else b
        free += b is None
    return bank


BANK = psum_banks()


class Stages:

    def __init__(self, nc, prefix, per, given={}):
        self.per = per
        self.sem = {n: given.get(prefix + n) or nc.alloc_semaphore(prefix + n) for n in per}

    def engine(self, eng, turn=0):
        return Turn(self, eng, turn)


class Turn:

    def __init__(self, stages, eng, turn):
        self.s, self.eng, self.turn, self.n, self.seen = stages, eng, turn, {}, {}

    def wait(self, name, count):
        if count > self.seen.get(name, -1):
            self.seen[name] = count
            self.eng.wait_ge(self.s.sem[name], self.turn * self.s.per[name] + count)

    def wait_last(self, name):
        with self.eng.If(self.turn > 0):
            self.eng.wait_ge(self.s.sem[name], self.turn * self.s.per[name])
            self.eng.nop(nofuse=True)

    def hold(self):
        self.eng.nop(nofuse=True)

    def done(self, ins, name, by=1):
        self.n[name] = self.n.get(name, 0) + by
        ins.then_inc(self.s.sem[name], by)

    def close(self):
        for name, n in self.n.items():
            assert n == self.s.per[name], (name, n, self.s.per[name])


def trunk(nc, a, pool_dma, kept):
    with ExitStack() as ctx:
        def sb(name, *shape, dt=F32):
            return ctx.enter_context(nc.sbuf_tensor(name, [P, *shape], dt))

        cst, msk = sb("cst", C_TRUNK), sb("msk", M_N, dt=U8)
        hT_hi, hT_lo = sb("hT_hi", KD, HALF, dt=F32R), sb("hT_lo", KD, HALF, dt=F32R)
        W = sb("W", KD, P)
        W_hi = [sb(f"W_hi{i}", KD, P, dt=F32R) for i in range(2)]
        W_lo = [sb(f"W_lo{i}", KD, P, dt=F32R) for i in range(2)]
        wab = sb("wab", KD, 8)
        H = {n: sb("h_" + n, HALF) for n in
             ("kh", "cum", "qh", "zh", "v", "d0", "d1", "e0", "e1", "m0", "m1", "att", "qe", "kl", "o", "lf")}
        SH = sb("SH", NC + 1, P)
        arena = sb("arena", 10 * (HALF + HALO))
        G = {n: arena[:, i * (HALF + HALO):(i + 1) * (HALF + HALO)] for i, n in enumerate(
            ("rq", "rk", "rv", "cq", "ck", "cv", "tq", "tk", "tv", "egr"))}
        X8 = [H[n][:] for n in ("qh", "zh", "kh", "m0")] + [arena[:, i * D:(i + 1) * D] for i in range(NC - 4)]
        raw = {n: G["r" + n] for n in "qkv"}
        conv = {n: G["c" + n][:, 0:HALF] for n in "qkv"}
        tmp = {n: G["t" + n][:, 0:HALF] for n in "qkv"}
        EGR, GB = G["egr"][:, 0:HALF], tmp["v"]
        ZG = EGR
        DM, DEC, DECT = (raw[n][:, 0:HALF] for n in "qkv")
        A_, AT_, X_, Y_, PP = (H[n] for n in ("d0", "d1", "e0", "e1", "m0"))
        RK, RV, KDEC, NW, QKD, QG = (H[n] for n in ("m1", "qe", "kl", "v", "cum", "d0"))
        OG = H["lf"]
        KLT = H["d1"]
        abT = H["kl"][0:8, :]
        hTf = [H[n][:].rearrange("p (k t) -> p k t", k=KD) for n in ("d0", "d1", "e0", "e1")]
        SG = sb("SG", P)
        VN = sb("VN", 2, P)
        HALOS = sb("HALOS", HEADS, 3, HALO)
        SALL = sb("SALL", 2, HEADS, P)
        PT = sb("PT", HEADS, 15)
        PC = sb("PC", 15)
        GT = sb("GT", 7, NC, HEADS)
        GC = sb("GC", 7, NC)
        nw, onw = sb("nw", KD), sb("onw", 2)
        lbt = sb("lbt", 2, HEADS)
        agt = sb("agt", 2, HEADS)
        ss = sb("ss", 6, NC)
        gtmp = sb("gtmp", 5, NC, HEADS)
        el = sb("el", NC)
        ps = [ctx.enter_context(nc.psum_tensor(f"ps{i}", [P, GRP], F32)) for i in range(8)]

        ident, UI, ones = cst[:, C_ID:C_ID + P], cst[:, C_UI:C_UI + P], cst[:, C_ONE:C_ONE + P]
        scanm = cst[:, C_SCAN:C_SCAN + HALF]

        def col(n):
            return cst[:, C_COL + n:C_COL + n + 1]

        def gs(b, g):
            return b[:, g * GRP:(g + 1) * GRP]

        def ck(b, c):
            return b[:, c * P:(c + 1) * P]

        def c4(ap):
            return ap.rearrange("p (c t) -> p c t", t=P)

        def halves(ap, h, late):
            return ap.rearrange("p (b w) -> p b w", w=2 * h)[:, :, h:2 * h] if late \
                else ap.rearrange("p (b w) -> p b w", w=2 * h)[:, :, 0:h]

        def merge(V, buf, g, l, late, data):
            h = SOLVE_LEVELS[l]
            o = (M_SOLT if late else M_SOL) + l * 64
            mk = msk[:, o:o + 64]
            if h == 64:
                return V.copy_predicated(halves(gs(buf, g), h, late), mk.unsqueeze(1).to_broadcast([P, CPG, 64]), data)
            out = gs(buf, g).rearrange("p (c b w) -> p c b w", c=CPG, w=2 * h)
            out = out[:, :, :, h:2 * h] if late else out[:, :, :, 0:h]
            mk = mk.rearrange("p (b w) -> p b w", w=h).unsqueeze(1).to_broadcast([P, CPG, 64 // h, h])
            return V.copy_predicated(out, mk, data)

        def half_data(group, h, late):
            if h == 64:
                return halves(group, h, late)
            v = group.rearrange("p (c b w) -> p c b w", c=CPG, w=2 * h)
            return v[:, :, :, h:2 * h] if late else v[:, :, :, 0:h]

        def per_chunk(cols, g):
            return cols[:, g * CPG:(g + 1) * CPG].unsqueeze(2).to_broadcast([P, CPG, P])

        def over_chunks(m):
            return m.unsqueeze(1).to_broadcast([P, CPG, m.shape[1]])

        KG, KGC, KB, KBG, KKD, KHB, KGE = range(7)

        N = Stages(nc, "n_", dict(
            const=64 + 128, xa=64, xb=64, sq=8, ln=2, r0=2, newton=8, xs=8, tr=16, ht=16, ab=8, abT=2, abt=1, absb=1,
            hTf=16, hThi=16, gch=9, lbd=1, gact=7, gcs=1, once=3, onceact=2))
        S = Stages(nc, "s_", dict(
            w=128, whi=8, wlo=8, init=1, pF=2, pQ=2, pZ=2, pVF=2, vf=2, pV=2, pGQ=2, pGK=2, pGV=2, pGZ=2, pGR=2,
            thF=2, thQ=2, thZ=2, v=2, lf=1, rawq=2, rawk=2, rawv=2, c0=3, thG=2, egr=2,
            qhat=2, zh=2, kh=1, cum=1, D=6, E=4, EF=2, EQ=1, EL=1, elast=1, M=4, MF=2, qe=1, kl=1,
            pA=10, att=10, pKL=2, klt=2, pDS=2, hs=8, pOH=2, sqh=2, oh=2, pNH=2, lnh=2, rh=2, h1=2, mixh=2, outh=16,
            conv=9, thc=3, c2=3, sqc=4, pN=4, lnc=4, rc=4, nrm=4, zg=2, dm=2, dx=4, dec=4,
            pKK=2, A=2, pAT=2, at=2, xy=2, eye=2, pP=12, P=12, pX=10, X=10, pXT=10, XT=10, pY=2, Y=2,
            pKT=2, rk=2, kdec=2, pVT=2, rv=2, pWT=2, nw=2, pQK=2, qkd=2, qg=2,
            pVN=8, vn=8, pS=8, sg=8, pOG=2, og=2, sqg=2, pNG=2, lng=2, rg=2, g1=2, mixg=2, outg=16, save=1), pool_dma)

        bank_at = {key: ps[b] for key, b in BANK.items()}
        block = ctx.enter_context(nc.Block())

        @block.sync
        def _(sp):
            def load_x(half, first):
                for t in range(first, first + 4):
                    sp.dma_start(X8[t], a["x"][bass.ds(half * HALF + t * P, P), :])\
                        .then_inc(N.sem["xa" if first == 0 else "xb"], 16)

            sp.dma_start(cst[:], a["consts"][:, 0:C_TRUNK]).then_inc(N.sem["const"], 16)
            sp.dma_start(H["o"][:], a["masks"]).then_inc(N.sem["const"], 16)
            sp.dma_start(nw[:], a["norm_mix"]).then_inc(N.sem["const"], 16)
            sp.dma_start(onw[:], a["onorm"]).then_inc(N.sem["const"], 16)
            sp.dma_start(wab[:], a["w_ab"]).then_inc(N.sem["const"], 16)
            sp.dma_start(lbt[:], a["lb"]).then_inc(N.sem["const"], 16)
            sp.dma_start(agt[:, 0, :], a["a_log"].partition_broadcast(P)).then_inc(N.sem["const"], 16)
            sp.dma_start(agt[:, 1, :], a["dt_bias"].partition_broadcast(P)).then_inc(N.sem["const"], 16)
            for h in range(HEADS):
                sp.dma_start(PT[:, h, 3:15], a["conv_w"][:, h, :]).then_inc(N.sem["const"], 16)

            def load(head, b):
                sp.dma_start(W[:], a["w_proj"][bass.ds(head, 1), :, b].rearrange("h p k c -> p (h k) c"))\
                    .then_inc(S.sem["w"], 16)

            load(0, 0)
            load_x(0, 0)
            load_x(0, 4)
            with sp.Fori(0, NHALF) as half:
                with sp.Fori(0, HEADS) as head:
                    t = S.engine(sp, half * HEADS + head)
                    for b in range(1, 8):
                        t.wait("wlo", b)
                        t.hold()
                        load(head, b)
                    t.wait("wlo", 8)
                    t.hold()
                    with sp.If(head < HEADS - 1):
                        load(nc.s_assert_within(head + 1, 1, HEADS - 1, skip_runtime_bounds_check_because=
                                                "this branch is taken for head < HEADS - 1 alone"), 0)
                    with sp.If(head > HEADS - 2):
                        load(0, 0)
                with sp.If(half < NHALF - 1):
                    last_turn = half * HEADS + HEADS
                    sp.wait_ge(S.sem["mixh"], last_turn * 2)
                    sp.nop(nofuse=True)
                    sp.wait_ge(S.sem["nw"], last_turn * 2)
                    sp.nop(nofuse=True)
                    load_x(nc.s_assert_within(half + 1, 1, NHALF - 1, skip_runtime_bounds_check_because=
                                              "this branch is taken for half < NHALF - 1 alone"), 0)
                    sp.wait_ge(S.sem["mixg"], last_turn * 2)
                    sp.nop(nofuse=True)
                    load_x(nc.s_assert_within(half + 1, 1, NHALF - 1, skip_runtime_bounds_check_because=
                                              "this branch is taken for half < NHALF - 1 alone"), 4)
            sp.wait_ge(S.sem["w"], NHALF * HEADS * 128 + 16)

        @block.gpsimd
        def _(pool):
            nc.gpsimd.memset(H["att"][:], 0.0).then_inc(N.sem["once"], 1)
            nc.gpsimd.memset(SALL[:], 0.0).then_inc(N.sem["once"], 1)
            nc.gpsimd.memset(HALOS[:], 0.0).then_inc(N.sem["once"], 1)
            with pool.Fori(0, NHALF) as half, pool.Fori(0, HEADS) as head:
                t = S.engine(pool, half * HEADS + head)
                t.wait("cum", 1)
                for l in range(6):
                    d = H["d0" if l % 2 == 0 else "d1"]
                    if l >= 2:
                        t.wait("E", l - 1) if l < 5 else t.wait("E", 4)
                    if l < 4:
                        h = ATT_LEVELS[l]
                        v = "p (b w) -> p b w"
                        ci = H["cum"][:].rearrange(v, w=2 * h)
                        ref = ci[:, :, h - 1:h].to_broadcast([P, HALF // (2 * h), 2 * h])
                        out = d[:].rearrange(v, w=2 * h)
                    else:
                        w, at = (8, 3) if l == 4 else (P, P - 1)
                        if l == 5:
                            t.wait("E", 4)
                        ci = H["cum"][:].rearrange("p (b w) -> p b w", w=w)
                        ref = ci[:, :, at:at + 1].to_broadcast([P, HALF // w, w])
                        out = d[:].rearrange("p (b w) -> p b w", w=w)
                    t.done(nc.gpsimd.tensor_tensor(out, ci, ref, ALU.subtract), "D")
                for g in range(NG):
                    t.wait("dx", g + 1)
                    t.hold()
                    o = c4(gs(DEC, g))
                    t.done(nc.gpsimd.affine_select(out=o, in_=o, compare_op=ALU.is_gt, fill=0.0, base=0,
                                                   pattern=[[0, CPG], [-1, P]], channel_multiplier=1), "dec")
                for g in range(NG):
                    t.wait("nrm", NG + g + 1)
                    t.wait("egr", 2)
                    t.wait("xy", 2)
                    t.done(nc.gpsimd.tensor_tensor(gs(QG, g), gs(conv["q"], g), gs(EGR, g), ALU.mult), "qg")
                for g in range(NG):
                    t.wait("dx", NG + g + 1)
                    t.hold()
                    o = c4(gs(DECT, g))
                    t.done(nc.gpsimd.affine_select(out=o, in_=o, compare_op=ALU.is_ge, fill=0.0, base=0,
                                                   pattern=[[0, CPG], [1, P]], channel_multiplier=-1), "dec")
                for stage, rows, src, out in (("mixh", head, H["o"], "outh"), ("mixg", head + HEADS, OG, "outg")):
                    t.wait(stage, 2)
                    t.hold()
                    pool.dma_start(a["mix"][bass.ds(rows, 1), :, bass.ds(half * HALF, HALF)]
                                   .rearrange("h p t -> p (h t)"), src[:]).then_inc(S.sem[out], 16)
                t.close()
            pool.wait_ge(S.sem["outh"], NHALF * HEADS * 16)
            pool.wait_ge(S.sem["outg"], NHALF * HEADS * 16)

        @block.scalar
        def _(act):
            A = nc.scalar.activation
            act.wait_ge(N.sem["const"], 192)
            act.wait_ge(N.sem["lbd"], 1)
            A(lbt[:, 0, :], lbt[:, 1, :], ACT.Exp).then_inc(N.sem["onceact"], 1)
            A(agt[:, 0, :], agt[:, 0, :], ACT.Exp).then_inc(N.sem["onceact"], 1)
            act.wait_ge(S.sem["w"], 16)
            A(W_hi[0][:], W[:], ACT.Copy).then_inc(S.sem["whi"], 1)
            with act.Fori(0, NHALF) as half:
                n = N.engine(act, half)
                for t_ in range(NC):
                    if t_ % 4 == 0:
                        n.wait("xa" if t_ == 0 else "xb", 64)
                    if t_ >= 2:
                        n.wait("sq", t_ - 1)
                    n.done(A(H[("m1", "qe")[t_ % 2]][:], X8[t_], ACT.Square, accum_out=ss[:, 0, t_:t_ + 1]), "sq")
                    if t_ % 4 == 3:
                        w = slice(t_ - 3, t_ + 1)
                        n.wait("sq", t_ + 1)
                        n.done(A(ss[:, 1, w], ss[:, 0, w], ACT.Ln, scale=1.0 / D, bias=col(COL_EPS)), "ln")
                        n.wait("ln", t_ // 4 + 1)
                        n.done(A(ss[:, 2, w], ss[:, 1, w], ACT.Exp, scale=-0.5), "r0")
                for j in range(16):
                    n.wait("hTf", j + 1)
                    k4 = slice(4 * (j % 2), 4 * (j % 2) + 4)
                    n.done(A(hT_hi[:, k4, j // 2 * P:(j // 2 + 1) * P], hTf[j // 2 % 4][:, k4, :], ACT.Copy), "hThi")
                    if j % 8 == 7:
                        n.wait("ab", CPG * (j // 8 + 1))
                        n.done(A(abT[:, j // 8 * GRP:(j // 8 + 1) * GRP], ps[6 + j // 8][0:8, :], ACT.Copy), "abT")
                n.wait("gch", 1)
                n.done(A(gtmp[:, 1], gtmp[:, 0], ACT.Abs), "gact")
                n.wait("gact", 1)
                n.done(A(gtmp[:, 1], gtmp[:, 1], ACT.Exp, scale=-1.0), "gact")
                n.wait("gact", 2)
                n.done(A(gtmp[:, 2], gtmp[:, 1], ACT.Ln, bias=cst[:, C_ONE:C_ONE + 1]), "gact")
                n.wait("absb", 1)
                n.done(A(gtmp[:, 3], gtmp[:, 4], ACT.Tanh, scale=0.5), "gact")
                n.wait("gch", 7)
                n.done(A(gtmp[:, 0], GT[:, KGC], ACT.Exp), "gact")
                n.done(A(GT[:, KGE], gtmp[:, 1], ACT.Exp), "gact")
                n.done(A(GT[:, KKD], gtmp[:, 2], ACT.Exp), "gact")
                with act.Fori(0, HEADS) as head:
                    t = S.engine(act, half * HEADS + head)
                    def split(b):
                        t.wait("w", 16 * (b + 1))
                        t.done(A(W_hi[b % 2][:], W[:], ACT.Copy), "whi")

                    def copies(g, stage, out, src, func=ACT.Copy, need=None, **kw):
                        if need:
                            t.wait(need, g + 1)
                        t.done(A(out, src, func, **kw), stage)

                    def project_out(n_, stage, buf, func=ACT.Copy, off=0, **kw):
                        for g in range(NG):
                            copies(g, stage, buf[:, off + g * GRP:off + (g + 1) * GRP], bank_at[(n_, g)][:], func,
                                   need="p" + n_.upper(), **kw)

                    def first_tap(i):
                        n_ = "qkv"[i]
                        t.wait("raw" + n_, 2)
                        t.done(A(conv[n_], raw[n_][:, 0:HALF], ACT.Copy, scale=PC[:, 3 + 4 * i:4 + 4 * i]), "c0")

                    def decays(l):
                        h = ATT_LEVELS[l]
                        t.wait("D", l + 1)
                        if l >= 2:
                            t.wait("M", l - 1)
                        e = H["e0" if l % 2 == 0 else "e1"][:].rearrange("p (b w) -> p b w", w=2 * h)
                        d = H["d0" if l % 2 == 0 else "d1"][:].rearrange("p (b w) -> p b w", w=2 * h)
                        A(e[:, :, h:2 * h], d[:, :, h:2 * h], ACT.Exp, bias=col(COL_LNHQ))
                        t.done(A(e[:, :, 0:h], d[:, :, 0:h], ACT.Exp, scale=-1.0), "E")

                    def solve_out(l):
                        for g in range(NG):
                            t.wait("pP", 2 * l + g + 1)
                            t.done(A(gs(PP, g), bank_at[("P", l, g)][:], ACT.Copy), "P")
                            for i in range(NG if l and g == 0 else 0):
                                t.wait("pXT", 2 * (l - 1) + i + 1)
                                t.done(A(gs(Y_, i), bank_at[("XT", l - 1, i)][:], ACT.Copy), "XT")

                    split(1)
                    project_out("F", "thF", H["kh"], ACT.Tanh, scale=0.5)
                    t.wait_last("outg")
                    t.wait("init", 1)
                    t.wait("thF", 2)
                    t.done(A(H["lf"][:], H["kh"][:], ACT.Ln, scale=PC[:, 0:1], bias=PC[:, 1:2]), "lf")
                    split(2)
                    project_out("Q", "thQ", H["kl"], ACT.Tanh, scale=0.5)
                    decays(0)
                    split(3)
                    decays(1)
                    t.wait("cum", 1)
                    project_out("Z", "thZ", H["lf"], ACT.Tanh, scale=0.5)
                    decays(2)
                    split(4)
                    decays(3)
                    t.wait("D", 5)
                    t.wait("M", 3)
                    t.done(A(H["e0"][:], H["d0"][:], ACT.Exp, bias=col(COL_LNHQ)), "EF")
                    t.wait("M", 4)
                    t.done(A(H["e1"][:], H["d0"][:], ACT.Exp, scale=-1.0), "EF")
                    t.done(A(el[:], H["cum"][:].rearrange("p (c w) -> p c w", w=P)[:, :, P - 1], ACT.Exp), "elast")
                    t.done(A(H["qe"][:], H["cum"][:], ACT.Exp, bias=col(COL_LNHQ)), "EQ")
                    t.wait("D", 6)
                    t.wait("qhat", 2)
                    t.done(A(H["kl"][:], H["d1"][:], ACT.Exp, scale=-1.0), "EL")
                    t.wait("zh", 2)
                    project_out("VF", "vf", H["lf"])
                    split(5)
                    project_out("V", "v", H["v"])
                    project_out("Gq", "rawq", raw["q"], off=HALO)
                    first_tap(0)
                    project_out("KL", "klt", KLT)
                    split(6)
                    t.wait("conv", 3)
                    t.done(A(tmp["q"], conv["q"], ACT.Tanh, scale=0.5), "thc")
                    project_out("Gk", "rawk", raw["k"], off=HALO)
                    first_tap(1)
                    project_out("GR", "egr", EGR, ACT.Exp)
                    split(7)
                    t.wait("c2", 1)
                    for g in range(NG):
                        t.done(A(gs(tmp["q"], g), gs(conv["q"], g), ACT.Square), "sqc")
                    t.wait_last("outh")
                    for g in range(NG):
                        t.wait("pOH", g + 1)
                        t.done(A(gs(H["o"], g), ps[6 + g][:], ACT.Copy), "oh")
                        t.done(A(gs(H["kh"], g), ps[6 + g][:], ACT.Square), "sqh")
                    t.wait("conv", 6)
                    t.done(A(tmp["k"], conv["k"], ACT.Tanh, scale=0.5), "thc")
                    t.wait("dm", 2)
                    for g in range(NG):
                        t.done(A(gs(DEC, g), gs(DM, g), ACT.Exp, scale=-1.0), "dx")
                    t.wait("c2", 2)
                    for g in range(NG):
                        t.done(A(gs(tmp["k"], g), gs(conv["k"], g), ACT.Square), "sqc")
                    copies(0, "rawv", raw["v"][:, HALO:HALO + GRP], bank_at[("Gv", 0)][:], need="pGV")
                    for g in range(NG):
                        t.wait("pNH", g + 1)
                        t.done(A(gs(H["kh"], g), bank_at[("NH", g)][:], ACT.Ln, scale=1.0 / P, bias=col(COL_EPS)), "lnh")
                    norms = [("k", 0), ("k", 1), ("q", 0), ("q", 1)]
                    for m, (n_, g) in enumerate(norms):
                        t.wait("pN", m + 1)
                        t.done(A(gs(tmp[n_], g), bank_at[("N", m)][:], ACT.Ln, bias=col(COL_EPS4)), "lnc")
                    for m, (n_, g) in enumerate(norms):
                        t.wait("lnc", m + 1)
                        if n_ == "q":
                            t.done(A(gs(tmp[n_], g), gs(tmp[n_], g), ACT.Exp, scale=-0.5, bias=col(COL_LNGQ)), "rc")
                        else:
                            t.done(A(gs(tmp[n_], g), gs(tmp[n_], g), ACT.Exp, scale=-0.5), "rc")
                    for g in range(NG):
                        t.wait("lnh", g + 1)
                        t.done(A(gs(H["kh"], g), gs(H["kh"], g), ACT.Exp, scale=-0.5), "rh")
                    copies(1, "rawv", raw["v"][:, HALO + GRP:HALO + HALF], bank_at[("Gv", 1)][:], need="pGV")
                    first_tap(2)
                    for g in range(NG):
                        copies(g, "at", gs(AT_, g), bank_at[("AT", g)][:], need="pAT")
                    for l in range(4):
                        solve_out(l)
                    t.wait("conv", 9)
                    t.done(A(tmp["v"], conv["v"], ACT.Tanh, scale=0.5), "thc")
                    for g in range(NG):
                        t.done(A(gs(DECT, g), gs(DM, g), ACT.Exp), "dx")
                    solve_out(4)
                    split(8)
                    solve_out(5)
                    project_out("WT", "nw", NW, scale=-1.0)
                    for c in range(NC):
                        t.wait("pVN", c + 1)
                        t.done(A(VN[:, c % 2, :], bank_at[("VN", c)][:, 0:P], ACT.Copy), "vn")
                        if c == CPG:
                            t.wait("pOG", 1)
                            t.done(A(gs(OG, 0), ps[6][:], ACT.Copy), "og")
                        if c == CPG + 1:
                            t.done(A(gs(tmp["q"], 0), ps[6][:], ACT.Square), "sqg")
                        if c == CPG + 2:
                            copies(0, "thG", gs(tmp["v"], 0), bank_at[("Gz", 0)][:], ACT.Tanh, need="pGZ", scale=0.5)
                    t.wait("pOG", 2)
                    t.done(A(gs(tmp["q"], 1), ps[7][:], ACT.Square), "sqg")
                    t.done(A(gs(OG, 1), ps[7][:], ACT.Copy), "og")
                    copies(1, "thG", gs(tmp["v"], 1), bank_at[("Gz", 1)][:], ACT.Tanh, need="pGZ", scale=0.5)
                    project_out("NG", "lng", tmp["k"], ACT.Ln, scale=1.0 / P, bias=col(COL_EPS))
                    for g in range(NG):
                        t.wait("lng", g + 1)
                        t.done(A(gs(tmp["k"], g), gs(tmp["k"], g), ACT.Exp, scale=-0.5), "rg")
                    t.close()

        @block.vector
        def _(dve):
            V = nc.vector
            dve.wait_ge(N.sem["const"], 192)
            once = [0]
            osem = nc.alloc_semaphore("once_dve")

            def link(ins):
                once[0] += 1
                ins.then_inc(osem, 1)
                dve.wait_ge(osem, once[0])

            V.tensor_tensor(lbt[:, 1, :], lbt[:, 1, :], lbt[:, 0, :], ALU.subtract).then_inc(N.sem["lbd"], 1)
            dve.wait_ge(N.sem["onceact"], 2)
            link(V.tensor_scalar(lbt[:, 0, :], lbt[:, 0, :], 1.0, None, ALU.add))
            link(V.reciprocal(lbt[:, 0, :], lbt[:, 0, :]))
            V.tensor_copy(msk[:], H["o"][:])
            V.tensor_scalar(PT[:, :, 0], lbt[:, 0, :], -0.5, 0.5, ALU.mult, ALU.add)
            V.tensor_scalar(PT[:, :, 1], lbt[:, 0, :], 0.5, 0.5, ALU.mult, ALU.add)
            V.tensor_scalar(PT[:, :, 2], lbt[:, 0, :], 0.5, -0.5, ALU.mult, ALU.add)
            V.tensor_scalar(onw[:], onw[:], 0.5, None, ALU.mult)
            link(V.tensor_scalar(agt[:, 0, :], agt[:, 0, :], -1.0, None, ALU.mult))
            dve.wait_ge(S.sem["whi"], 1)
            V.tensor_tensor(W_lo[0][:], W[:], W_hi[0][:].bitcast(F32), ALU.subtract)\
                .then_inc(S.sem["wlo"], 1)
            dve.wait_ge(N.sem["once"], 3)
            with dve.Fori(0, NHALF) as half:
                n = N.engine(dve, half)

                def rms(b):
                    w = slice(4 * b, 4 * b + 4)
                    n.wait("r0", b + 1)
                    V.tensor_scalar(ss[:, 3, w], ss[:, 0, w], 1.0 / D, EPS, ALU.mult, ALU.add)
                    n.done(V.tensor_tensor(ss[:, 4, w], ss[:, 2, w], ss[:, 2, w], ALU.mult), "newton")
                    n.wait("newton", 4 * b + 1)
                    n.done(V.tensor_tensor(ss[:, 4, w], ss[:, 4, w], ss[:, 3, w], ALU.mult), "newton")
                    n.wait("newton", 4 * b + 2)
                    n.done(V.tensor_scalar(ss[:, 4, w], ss[:, 4, w], -0.5, 1.5, ALU.mult, ALU.add), "newton")
                    n.wait("newton", 4 * b + 3)
                    n.done(V.tensor_tensor(ss[:, 5, w], ss[:, 4, w], ss[:, 2, w], ALU.mult), "newton")
                    n.wait("newton", 4 * b + 4)

                for t_ in range(NC):
                    if t_ % 4 == 0:
                        rms(t_ // 4)
                    n.done(V.tensor_scalar(X8[t_], X8[t_], ss[:, 5, t_:t_ + 1], None, ALU.mult), "xs")
                    if t_ >= 1:
                        for q in range(2):
                            ht_evac(n, V, hTf, nw, ps, t_ - 1, q)
                    if t_ >= 2:
                        for q in range(2):
                            ht_rest(n, V, hTf, hT_lo, hT_hi, t_ - 2, q)
                for q in range(2):
                    ht_evac(n, V, hTf, nw, ps, NC - 1, q)
                for t_ in (NC - 2, NC - 1):
                    for q in range(2):
                        ht_rest(n, V, hTf, hT_lo, hT_hi, t_, q)
                n.wait("abt", 1)
                abv = ps[7][:, 0:NC * 8].rearrange("p (c h) -> p c h", h=8)
                dt = agt[:, 1, :].unsqueeze(1).to_broadcast([P, NC, HEADS])
                na = agt[:, 0, :].unsqueeze(1).to_broadcast([P, NC, HEADS])

                def step(ins):
                    n.done(ins, "gch")
                    n.wait("gch", n.n["gch"])

                n.done(V.tensor_copy(gtmp[:, 4], abv[:, :, HEADS:2 * HEADS]), "absb")
                step(V.tensor_tensor(gtmp[:, 0], abv[:, :, 0:HEADS], dt, ALU.add))
                n.wait("gact", 3)
                step(V.scalar_tensor_tensor(gtmp[:, 0], gtmp[:, 0], 0.0, gtmp[:, 2], ALU.max, ALU.add))
                step(V.tensor_tensor(GT[:, KG], gtmp[:, 0], na, ALU.mult))
                n.wait("gact", 4)
                step(V.tensor_scalar(GT[:, KB], gtmp[:, 3], 0.5, 0.5, ALU.mult, ALU.add))
                step(V.tensor_scalar(GT[:, KHB], GT[:, KB], 0.5, None, ALU.mult))
                n.wait("gcs", 1)
                cs = ps[6][:, 0:2 * NC * HEADS].rearrange("p (k c h) -> p k c h", k=2, h=HEADS)
                V.tensor_copy(gtmp[:, 1], cs[:, 1])
                step(V.tensor_copy(GT[:, KGC], cs[:, 0]))
                step(V.tensor_tensor(gtmp[:, 2], gtmp[:, 1], GT[:, KGC], ALU.subtract))
                n.wait("gact", 7)
                step(V.tensor_tensor(GT[:, KBG], gtmp[:, 0], GT[:, KB], ALU.mult))
                step(V.tensor_scalar(GT[:, KB], GT[:, KB], -1.0, None, ALU.mult))
                n.hold()
                with dve.Fori(0, HEADS) as head:
                    t = S.engine(dve, half * HEADS + head)
                    t.hold()
                    V.tensor_copy(PC[:], PT[:, bass.ds(head, 1), :].rearrange("p h n -> p (h n)"))
                    V.tensor_copy(GC[:], GT[:, :, :, bass.ds(head, 1)].rearrange("p k c h -> p k (c h)"))
                    V.tensor_copy(SH[:, 0, :], SALL[:, 0, bass.ds(head, 1), :].rearrange("p h n -> p (h n)"))
                    V.tensor_copy(SG[:], SALL[:, 1, bass.ds(head, 1), :].rearrange("p h n -> p (h n)"))
                    for i, n_ in enumerate("qkv"):
                        V.tensor_copy(raw[n_][:, 0:HALO], HALOS[:, bass.ds(head, 1), i, :].rearrange("p h n -> p (h n)"))
                    t.done(V.tensor_copy(c4(GB), GT[:, KG, :, bass.ds(head, 1)].to_broadcast([P, NC, P])), "init")
                    def split(b):
                        t.wait("whi", b + 1)
                        t.done(V.tensor_tensor(W_lo[b % 2][:], W[:], W_hi[b % 2][:].bitcast(F32), ALU.subtract), "wlo")

                    def silu(g, stage, out, th, n_):
                        t.wait({"Q": "thQ", "Z": "thZ", "Gz": "thG"}[n_], g + 1)
                        t.done(V.scalar_tensor_tensor(gs(out, g), gs(th, g), 1.0, bank_at[(n_, g)][:],
                                                      ALU.add, ALU.mult), stage)

                    def level(l):
                        h = ATT_LEVELS[l]
                        t.wait("E", l + 1)
                        if l >= 2:
                            t.wait("pA", 2 * (l - 1))
                        v = lambda b: b[:].rearrange("p (b w) -> p b w", w=2 * h)
                        m, e = H[f"m{l % 2}"], H[f"e{l % 2}"]
                        V.tensor_tensor(v(m)[:, :, h:2 * h], v(H["qh"])[:, :, h:2 * h], v(e)[:, :, h:2 * h], ALU.mult)
                        t.done(V.tensor_tensor(v(m)[:, :, 0:h], v(H["kh"])[:, :, 0:h], v(e)[:, :, 0:h], ALU.mult), "M")

                    def att(l):
                        h = ATT_LEVELS[l]
                        for g in range(NG):
                            t.wait("pA", 2 * l + g + 1)
                            if l:
                                t.wait("att", 2 * (l - 1) + g + 1)
                            t.hold()
                            t.done(merge(V, H["att"], g, SOLVE_LEVELS.index(h), True,
                                         half_data(bank_at[("A", l, g)][:], h, True)), "att")

                    def conv_tap(i, j):
                        n_ = "qkv"[i]
                        if j == 1:
                            t.wait("c0", i + 1)
                        else:
                            t.wait("conv", 3 * i + j - 1)
                        t.done(V.scalar_tensor_tensor(conv[n_], raw[n_][:, j:j + HALF],
                                                      PC[:, 3 + 4 * i + j:4 + 4 * i + j], conv[n_],
                                                      ALU.mult, ALU.add), "conv")

                    def conv_silu(i):
                        n_ = "qkv"[i]
                        t.wait("thc", i + 1)
                        t.done(V.scalar_tensor_tensor(conv[n_], tmp[n_], 1.0, conv[n_], ALU.add, ALU.mult), "c2")

                    def solve_merge(l):
                        h = SOLVE_LEVELS[l + 1]
                        for g in range(NG):
                            if l < 5:
                                t.wait("pX", 2 * l + g + 1)
                                t.hold()
                                t.done(merge(V, X_, g, l + 1, False, half_data(bank_at[("X", l, g)][:], h, False)), "X")
                            else:
                                t.wait("pY", g + 1)
                                t.hold()
                                t.done(merge(V, Y_, g, l + 1, True, half_data(bank_at[("Y", l, g)][:], h, True)), "Y")

                    split(1)
                    t.wait("init", 1)
                    t.wait("lf", 1)
                    t.done(V.tensor_tensor_scan(H["cum"][:], scanm, H["lf"][:], 0.0, ALU.mult, ALU.add), "cum")
                    t.done(V.tensor_scalar(H["kh"][:], H["kh"][:], PC[:, 2:3], PC[:, 0:1], ALU.mult, ALU.add), "kh")
                    split(2)
                    for g in range(NG):
                        silu(g, "qhat", H["qh"], H["kl"], "Q")
                    t.wait("kh", 1)
                    t.wait("qhat", 2)
                    level(0)
                    split(3)
                    level(1)
                    for g in range(NG):
                        silu(g, "zh", H["zh"], H["lf"], "Z")
                    level(2)
                    split(4)
                    level(3)
                    att(0)
                    att(1)
                    t.wait("EQ", 1)
                    t.done(V.tensor_tensor(H["qe"][:], H["qh"][:], H["qe"][:], ALU.mult), "qe")
                    t.wait("EL", 1)
                    t.done(V.tensor_tensor(H["kl"][:], H["kh"][:], H["kl"][:], ALU.mult), "kl")
                    att(2)
                    att(3)
                    t.wait("EF", 2)
                    t.done(V.tensor_tensor(H["m0"][:], H["qh"][:], H["e0"][:], ALU.mult), "MF")
                    t.done(V.tensor_tensor(H["m1"][:], H["kh"][:], H["e1"][:], ALU.mult), "MF")
                    split(5)
                    for j in range(1, TAPS):
                        conv_tap(0, j)
                    for g in range(NG):
                        t.wait("pA", 9 + g)
                        t.wait("att", 7 + g)
                        t.hold()
                        t.done(V.copy_predicated(c4(gs(H["att"], g)), over_chunks(msk[:, M_ATTF:M_ATTF + P]),
                                                 c4(bank_at[("AF", g)][:])), "att")
                    t.wait("elast", 1)
                    for c in range(NC):
                        t.wait("pDS", c // CPG + 1)
                        if c:
                            t.wait("hs", c)
                        t.done(V.scalar_tensor_tensor(SH[:, c + 1, :], SH[:, c, :], el[:, c:c + 1],
                                                      ck(bank_at[("DS", c // CPG)], c % CPG), ALU.mult, ALU.add), "hs")
                    split(6)
                    conv_silu(0)
                    for j in range(1, TAPS):
                        conv_tap(1, j)
                    for g in range(NG):
                        t.wait("egr", g + 1)
                        t.done(V.tensor_tensor(c4(gs(DM, g)), c4(bank_at[("GR", g)][:]), per_chunk(GC[:, KGC], g),
                                               ALU.subtract), "dm")
                    conv_silu(1)
                    split(7)
                    for m in range(4):
                        t.wait("rc", m + 1)
                        b, g = conv["kq"[m // 2]], m % 2
                        t.done(V.tensor_tensor(gs(b, g), gs(b, g), gs(tmp["kq"[m // 2]], g), ALU.mult), "nrm")
                    for g in range(NG):
                        t.wait("pKK", g + 1)
                        t.wait("dec", g + 1)
                        for c in range(CPG * g, CPG * (g + 1)):
                            last = V.scalar_tensor_tensor(ck(A_, c), ck(bank_at[("KK", g)], c % CPG), GC[:, KB, c:c + 1],
                                                          ck(DEC, c), ALU.mult, ALU.mult)
                        t.done(last, "A")
                        V.tensor_copy(c4(gs(X_, g)), over_chunks(ident))
                        t.done(V.tensor_copy(c4(gs(Y_, g)), over_chunks(ident)), "eye")
                    for g in range(NG):
                        t.wait("at", g + 1)
                        t.wait("eye", g + 1)
                        t.wait("A", g + 1)
                        t.hold()
                        merge(V, X_, g, 0, False, half_data(gs(A_, g), 1, False))
                        t.done(merge(V, Y_, g, 0, True, half_data(gs(AT_, g), 1, True)), "xy")
                    for g in range(NG):
                        t.wait("pKT", g + 1)
                        kt = c4(bank_at[("KT", g)][:])
                        t.done(V.tensor_tensor(c4(gs(RK, g)), kt, per_chunk(GC[:, KBG], g), ALU.mult), "rk")
                        t.done(V.tensor_tensor(c4(gs(KDEC, g)), kt, per_chunk(GC[:, KKD], g), ALU.mult), "kdec")
                    for l in range(6):
                        solve_merge(l)
                        if l < 3:
                            conv_tap(2, l + 1)
                        if l == 3:
                            conv_silu(2)
                            t.hold()
                            for i, n_ in enumerate("qkv"):
                                V.tensor_copy(HALOS[:, bass.ds(head, 1), i, :].rearrange("p h n -> p (h n)"),
                                              raw[n_][:, HALF:HALF + HALO])
                        if l == 4:
                            split(8)
                            for g in range(NG):
                                t.wait("pVT", g + 1)
                                t.done(V.tensor_tensor(c4(gs(RV, g)), c4(bank_at[("VT", g)][:]),
                                                       per_chunk(GC[:, KHB], g), ALU.mult), "rv")
                            for g in range(NG):
                                t.wait("pQK", g + 1)
                                t.wait("dec", NG + g + 1)
                                t.done(V.tensor_tensor(gs(QKD, g), bank_at[("QK", g)][:], gs(DECT, g), ALU.mult), "qkd")
                    for c in range(NC):
                        t.wait("pS", c + 1)
                        t.done(V.scalar_tensor_tensor(SG[:], SG[:], GC[:, KGE, c:c + 1], bank_at[("S", c)][:, 0:P],
                                                      ALU.mult, ALU.add), "sg")
                        if c < 4:
                            g = c // 2
                            t.wait("rh", g + 1)
                            t.wait("oh", g + 1)
                            if c % 2 == 0:
                                t.done(V.tensor_tensor(gs(H["o"], g), gs(H["o"], g), gs(H["kh"], g), ALU.mult), "h1")
                            else:
                                t.wait("h1", g + 1)
                                t.done(V.scalar_tensor_tensor(gs(H["o"], g), gs(H["o"], g), onw[:, 0:1],
                                                              gs(H["zh"], g), ALU.mult, ALU.mult), "mixh")
                        if c == NC - 1:
                            silu(0, "zg", ZG, tmp["v"], "Gz")
                    silu(1, "zg", ZG, tmp["v"], "Gz")
                    t.wait("sg", 8)
                    t.wait("hs", 8)
                    t.hold()
                    V.tensor_copy(SALL[:, 0, bass.ds(head, 1), :].rearrange("p h n -> p (h n)"), SH[:, NC, :])
                    t.done(V.tensor_copy(SALL[:, 1, bass.ds(head, 1), :].rearrange("p h n -> p (h n)"), SG[:]), "save")
                    for g in range(NG):
                        t.wait("rg", g + 1)
                        t.wait("og", g + 1)
                        t.done(V.tensor_tensor(gs(OG, g), gs(OG, g), gs(tmp["k"], g), ALU.mult), "g1")
                        t.wait("g1", g + 1)
                        t.done(V.scalar_tensor_tensor(gs(OG, g), gs(OG, g), onw[:, 1:2], gs(ZG, g),
                                                      ALU.mult, ALU.mult), "mixg")
                    t.wait("save", 1)
                    t.hold()
                    t.close()
                n.close()

        @block.tensor
        def _(pe):
            mm = nc.tensor.matmul

            def mm3(out, l_hi, l_lo, r_hi, r_lo, k):
                mm(out, l_hi, r_hi, start=(k == 0), stop=False)
                mm(out, l_hi, r_lo, start=False, stop=False)
                return mm(out, l_lo, r_hi, start=False, stop=(k == KD - 1))

            pe.wait_ge(N.sem["const"], 192)
            with pe.Fori(0, NHALF) as half:
                n = N.engine(pe, half)

                def gates(t_):
                    n.wait("hTf", 2 * t_ + 2)
                    for k in range(KD):
                        last = mm(ck(ps[6 + t_ // CPG], t_ % CPG)[0:8], wab[:, k, :], hTf[t_ % 4][:, k, :],
                                  start=(k == 0), stop=(k == KD - 1))
                    n.done(last, "ab")

                for t_ in range(NC):
                    n.wait("xs", t_ + 1)
                    for q in range(2):
                        j = 2 * t_ + q
                        if j >= 6:
                            n.wait("hTf", j - 5)
                        for k in range(4):
                            last = nc.tensor.transpose(ps[j % 6][:, k * P:(k + 1) * P],
                                                       X8[t_][:, (4 * q + k) * P:(4 * q + k + 1) * P], ident)
                        n.done(last, "tr")
                    if t_:
                        gates(t_ - 1)
                gates(NC - 1)
                n.wait("abT", 2)
                n.hold()
                for t_ in range(NC):
                    last = nc.tensor.transpose(ps[7][:, t_ * 8:(t_ + 1) * 8], abT[:, t_ * P:(t_ + 1) * P],
                                               ident[0:8, 0:8])
                n.done(last, "abt")
                n.wait("gch", 3)
                gv = GT[:, KG].rearrange("p c h -> p (c h)")
                w = NC * HEADS
                mm(ps[6][:, 0:w], UI, gv, start=True, stop=True)
                n.done(mm(ps[6][:, w:2 * w], ones, gv, start=True, stop=True), "gcs")
                n.wait("ht", 16)
                n.hold()
                with pe.Fori(0, HEADS) as head:
                    t = S.engine(pe, half * HEADS + head)
                    emptied = {}

                    def job(key, *free):
                        b = BANK[key]
                        if b in emptied:
                            t.wait(*emptied[b])
                        emptied[b] = free
                        return ps[b]

                    def part(b, g, out, ks):
                        for k in ks:
                            cols = slice(g * GRP, (g + 1) * GRP)
                            last = mm3(out[:], W_hi[b % 2][:, k, :], W_lo[b % 2][:, k, :], hT_hi[:, k, cols],
                                       hT_lo[:, k, cols], k)
                        return last

                    def project(b, n_, g, free):
                        t.wait("wlo", b + 1)
                        t.done(part(b, g, job((n_, g), free, g + 1), range(KD)), "p" + n_.upper())

                    def level(l):
                        t.wait("M", l + 1)
                        for g in range(NG):
                            out = job(("A", l, g), "att", 2 * l + g + 1)
                            for c in range(CPG):
                                m = ck(H[f"m{l % 2}"], g * CPG + c)
                                last = mm(ck(out, c), m, m, start=True, stop=True)
                            t.done(last, "pA")

                    def products(n_, free, lhs, rhs, need=None, stage=None, per=1, at=0):
                        for g in range(NG):
                            if need:
                                t.wait(need, g + 1)
                            out = job((n_, g), free, at + per * (g + 1))
                            for c in range(CPG):
                                last = mm(ck(out, c), ck(lhs, g * CPG + c), ck(rhs, g * CPG + c), start=True, stop=True)
                            t.done(last, stage or "p" + n_)

                    def turned(n_, free, src, need=None, groups=range(NG)):
                        for g in groups:
                            if need:
                                t.wait(need, g + 1)
                            out = job((n_, g), free, g + 1)
                            for c in range(CPG):
                                last = nc.tensor.transpose(ck(out, c), ck(src, g * CPG + c), ident)
                            t.done(last, "p" + n_)

                    def solve(l):
                        for g in range(NG):
                            if l == 0:
                                t.wait("xy", g + 1)
                                t.wait("at", g + 1)
                            else:
                                t.wait("X", 2 * (l - 1) + g + 1)
                            out = job(("P", l, g), "P", 2 * l + g + 1)
                            for c in range(g * CPG, (g + 1) * CPG):
                                last = mm(ck(out, c % CPG), ck(AT_, c), ck(X_, c), start=True, stop=True)
                            t.done(last, "pP")
                            if l == 0 and g == 1:
                                turned("KT", "kdec", conv["k"], groups=[1])
                            for i in range(NG if l and g == 0 else 0):
                                t.wait("X", 2 * (l - 1) + i + 1)
                                out = job(("XT", l - 1, i), "XT", 2 * (l - 1) + i + 1)
                                for c in range(i * CPG, (i + 1) * CPG):
                                    last = nc.tensor.transpose(ck(out, c % CPG), ck(X_, c), ident)
                                t.done(last, "pXT")
                        for g in range(NG):
                            t.wait("P", 2 * l + g + 1)
                            if l:
                                t.wait("XT", 2 * (l - 1) + g + 1)
                            if l < 5:
                                out = job(("X", l, g), "X", 2 * l + g + 1)
                                for c in range(g * CPG, (g + 1) * CPG):
                                    last = mm(ck(out, c % CPG), ck(Y_, c), ck(PP, c), start=True, stop=True)
                                t.done(last, "pX")
                            else:
                                out = job(("Y", l, g), "Y", g + 1)
                                for c in range(g * CPG, (g + 1) * CPG):
                                    last = mm(ck(out, c % CPG), ck(PP, c), ck(Y_, c), start=True, stop=True)
                                t.done(last, "pY")

                    for b, (n_, free) in enumerate((("F", "thF"), ("Q", "qhat"), ("Z", "zh"))):
                        for g in range(NG):
                            project(b, n_, g, free)
                    level(0)
                    level(1)
                    for g in range(NG):
                        project(3, "VF", g, "vf")
                    level(2)
                    level(3)
                    turned("V", "v", H["lf"], need="vf")
                    for g in range(NG):
                        project(4, "Gq", g, "rawq")
                    t.wait("kl", 1)
                    turned("KL", "klt", H["kl"])
                    t.wait("MF", 2)
                    products("AF", "att", H["m1"], H["m0"], stage="pA", at=8)
                    products("DS", "hs", KLT, H["v"], need="klt", per=CPG)
                    for g in range(NG):
                        project(5, "Gk", g, "rawk")
                    t.wait("init", 1)
                    for g in range(NG):
                        out = job(("GR", g), "dm", g + 1)
                        for c in range(CPG):
                            last = mm(ck(out, c), ck(GB, g * CPG + c), UI, start=True, stop=True)
                        t.done(last, "pGR")
                    t.wait("att", 10)
                    t.wait("qe", 1)
                    for g in range(NG):
                        t.wait("hs", CPG * g + CPG - 1)
                        out = job(("OH", g), "sqh", g + 1)
                        for c in range(g * CPG, (g + 1) * CPG):
                            mm(ck(out, c % CPG), SH[:, c, :], ck(H["qe"], c), start=True, stop=False)
                            last = mm(ck(out, c % CPG), ck(H["v"], c), ck(H["att"], c), start=False, stop=True)
                        t.done(last, "pOH")
                    project(6, "Gv", 0, "rawv")
                    for g in range(NG):
                        t.wait("sqh", g + 1)
                        t.done(mm(job(("NH", g), "lnh", g + 1)[:], ones, gs(H["kh"], g), start=True, stop=True), "pNH")
                    for m, (n_, g) in enumerate((("k", 0), ("k", 1), ("q", 0), ("q", 1))):
                        t.wait("sqc", (3 if n_ == "k" else 1) + g)
                        out = job(("N", m), "lnc", m + 1)
                        t.done(mm(out[:], ones, gs(tmp[n_], g), start=True, stop=True), "pN")
                    project(6, "Gv", 1, "rawv")
                    t.wait("nrm", 2)
                    products("KK", "A", conv["k"], conv["k"])
                    t.wait("nrm", 4)
                    products("QK", "qkd", conv["k"], conv["q"])
                    turned("AT", "at", A_, need="A")
                    turned("KT", "kdec", conv["k"], groups=[0])
                    for l in range(5):
                        solve(l)
                    t.wait("c2", 3)
                    turned("VT", "rv", conv["v"])
                    solve(5)
                    for g in range(NG):
                        t.wait("rk", g + 1)
                        t.wait("Y", g + 1)
                        out = job(("WT", g), "nw", g + 1)
                        for c in range(g * CPG, (g + 1) * CPG):
                            last = mm(ck(out, c % CPG), ck(RK, c), ck(Y_, c), start=True, stop=True)
                        t.done(last, "pWT")
                    for c in range(NC):
                        g = c // CPG
                        if c % CPG == 0:
                            t.wait("wlo", 8)
                            t.wait("nw", NG)
                            for stage in ("rv", "kdec", "qkd", "qg"):
                                t.wait(stage, g + 1)
                            o, gate = job(("OG", g), "sqg", g + 1), job(("Gz", g), "zg", g + 1)
                        out = job(("VN", c), "vn", c + 1)
                        mm(out[:, 0:P], ck(Y_, c), ck(RV, c), start=True, stop=False)
                        if c:
                            t.wait("sg", c)
                        t.done(mm(out[:, 0:P], ck(NW, c), SG[:], start=False, stop=True), "pVN")
                        mm(ck(o, c % CPG), SG[:], ck(QG, c), start=True, stop=False)
                        part(7, g, gate, [2 * (c % CPG)])
                        t.wait("vn", c + 1)
                        out = job(("S", c), "sg", c + 1)
                        t.done(mm(out[:, 0:P], ck(KDEC, c), VN[:, c % 2, :], start=True, stop=True), "pS")
                        last = mm(ck(o, c % CPG), VN[:, c % 2, :], ck(QKD, c), start=False, stop=True)
                        if c % CPG == CPG - 1:
                            t.done(last, "pOG")
                        last = part(7, g, gate, [2 * (c % CPG) + 1])
                        if c % CPG == CPG - 1:
                            t.done(last, "pGZ")
                    for g in range(NG):
                        t.wait("og", g + 1)
                        t.done(mm(job(("NG", g), "lng", g + 1)[:], ones, gs(tmp["q"], g), start=True, stop=True), "pNG")
                    t.hold()
                    t.close()
                n.close()


def ht_evac(n, V, f, nw, ps, t_, q):
    j = 2 * t_ + q
    n.wait("tr", j + 1)
    w = nw[:, 4 * q:4 * q + 4].unsqueeze(2).to_broadcast([P, 4, P])
    n.done(V.tensor_tensor(f[t_ % 4][:, 4 * q:4 * q + 4, :], ps[j % 6][:].rearrange("p (k t) -> p k t", t=P), w,
                           ALU.mult), "hTf")


def ht_rest(n, V, f, lo, hi, t_, q):
    n.wait("hThi", 2 * t_ + q + 1)
    n.wait("ab", t_ + 1)
    at = (slice(None), slice(4 * q, 4 * q + 4), slice(t_ * P, (t_ + 1) * P))
    n.done(V.tensor_tensor(lo[at], f[t_ % 4][:, 4 * q:4 * q + 4, :], hi[at].bitcast(F32), ALU.subtract), "ht")


def router(nc, a, pool_dma, kept):
    with ExitStack() as ctx:
        def sb(name, *shape, dt=F32):
            return ctx.enter_context(nc.sbuf_tensor("r_" + name, [P, *shape], dt))

        cst = sb("cst", C_N)
        wr = sb("wr", KD, EPG + NE)
        wo = [sb(f"wo{i}", D) for i in range(3)]
        wo_hi, wo_lo = sb("wo_hi", KD, D, dt=F32R), sb("wo_lo", KD, D, dt=F32R)
        mix_hi = [sb(f"mix_hi{i}", KD, P, dt=F32R) for i in range(2)]
        mix_lo = [sb(f"mix_lo{i}", KD, P, dt=F32R) for i in range(2)]
        wn = sb("wn", D)
        mixT = [sb(f"mixT{i}", KD, P) for i in range(2)]
        xt = [sb(f"xt{i}", D) for i in range(2)]
        xn = [sb(f"xn{i}", D) for i in range(2)]
        xnT = [sb(f"xnT{i}", KD, P) for i in range(2)]
        junk = sb("junk", D)
        st = sb("st", 2, 8)
        lg = sb("lg", 2, EPG + NE)
        rt = sb("rt", 2, 32)
        m8, i8, i8b = sb("m8", 3, 8), sb("i8", 8, dt=U32), sb("i8b", 8, dt=U32)
        prod, esel = sb("prod", EPG, EPG), sb("esel", EPG)
        oh = sb("oh", 2, 4, NE)
        cnt = sb("cnt", NE)
        tab = kept["gates"]
        sel = sb("sel", NT, NE)
        blk, base = sb("blk", 3, NE), sb("base", NE)
        blk_i = sb("blk_i", 2, NE, dt=I32)
        row_hot, block_id = sb("row_hot", 2 * NT, P), sb("block_id", 2 * NT, NSLOT)
        ri = sb("ri", 3, 2 * NT, dt=I32)
        rf = sb("rf", 5, 2 * NT)
        number = sb("number", 2 * NT)
        rows, slots = kept["rows"], kept["slots"]
        late, expert, miss = sb("late", NE), sb("expert", P), sb("miss", NSLOT)
        ps = [ctx.enter_context(nc.psum_tensor(f"r_ps{i}", [P, GRP], F32)) for i in range(8)]
        ident, US, ones = cst[:, C_ID:C_ID + P], cst[:, C_US:C_US + P], cst[:, C_ONE:C_ONE + P]
        i64, i8c = cst[:, C_I64:C_I64 + NE], cst[:, C_I8:C_I8 + EPG]

        PER = dict(hi=1, lo=1, po=2, h=2, sq=1, ln=1, r0=1, nt=4, xn=1, ptr=2, ev=2, plg=1, lg=1, v=19, pe=2, prk=1, rk=7)
        O = {n: nc.alloc_semaphore("r_" + n) for n in PER}
        O |= {n + str(i): nc.alloc_semaphore(f"r_{n}{i}") for n in ("mix", "xt", "hout", "xnout") for i in range(2)}
        O |= {f"wo{i}": nc.alloc_semaphore(f"r_wo{i}") for i in range(3)}
        O |= {n: nc.alloc_semaphore("r_" + n) for n in ("const", "start", "whi", "wlo", "table", "placed", "pexpert", "prows")}
        block = ctx.enter_context(nc.Block())

        def steps(eng, step, lag):
            for n in range(2):
                step(n, n, 0)
            with eng.Fori(1, NT // 2 - 1) as j:
                for i in range(2):
                    step(j * 2 + i, i, j)
            for n in range(NT - 2, NT + lag):
                step(n, n % 2, n // 2)

        def within(n, lo=0):
            return lo <= n < NT if isinstance(n, int) else True

        def waits(eng):
            def wait(name, n, count):
                eng.wait_ge(O[name], n * PER[name] + count)
            return wait

        @block.sync
        def _(sp):
            for k in range(KD):
                if k >= 3:
                    sp.wait_ge(O["wlo"], k - 2)
                sp.dma_start(wo[k % 3][:], a["w_out"][:, k, :]).then_inc(O[f"wo{k % 3}"], 16)
                if k == 2:
                    for i in range(2):
                        sp.dma_start(mixT[i][:], a["mix"][:, :, i * P:(i + 1) * P].rearrange("k p t -> p k t"))\
                            .then_inc(O[f"mix{i}"], 16)
                        sp.dma_start(xt[i][:], a["x"][i * P:(i + 1) * P, :]).then_inc(O[f"xt{i}"], 16)
            sp.dma_start(cst[:], a["consts"]).then_inc(O["const"], 16)
            sp.dma_start(kept["ident"][:], a["consts"][:, C_ID:C_ID + P]).then_inc(O["const"], 16)
            sp.dma_start(wr[:], a["w_router"]).then_inc(O["const"], 16)
            sp.dma_start(wn[:], a["norm_moe"].partition_broadcast(P)).then_inc(O["const"], 16)
            wait = waits(sp)

            def load(n, i, j):
                rows = bass.ds(n * P, P)
                if not within(n, 2):
                    return
                wait("lo", n - 2, 1)
                sp.nop(nofuse=True)
                sp.dma_start(mixT[i][:], a["mix"][:, :, rows].rearrange("k p t -> p k t")).then_inc(O[f"mix{i}"], 16)
                sp.wait_ge(O[f"hout{i}"], j * 16)
                sp.nop(nofuse=True)
                wait("xn", n - 2, 1)
                sp.nop(nofuse=True)
                sp.dma_start(xt[i][:], a["x"][rows, :]).then_inc(O[f"xt{i}"], 16)

            steps(sp, load, 0)
            sp.wait_ge(O["table"], EXPERT_ROW_STEP)
            e = sp.value_load(slots[0:1, 0:1], min_val=0, max_val=NE - 1)
            load_expert(sp, a, e, kept["w"], kept["w0"])
            for i in range(2):
                sp.wait_ge(O[f"hout{i}"], NT // 2 * 16)
                sp.wait_ge(O[f"xnout{i}"], NT // 2 * 16)

        @block.gpsimd
        def _(pool):
            nc.gpsimd.memset(cnt[:], 0.0).then_inc(O["start"], 1)

        @block.scalar
        def _(act):
            A = nc.scalar.activation
            wait = waits(act)

            def split_hi(n, i, j):
                act.wait_ge(O[f"mix{i}"], j * 16 + 16)
                A(mix_hi[i][:], mixT[i][:], ACT.Copy).then_inc(O["hi"], 1)

            for k in range(KD):
                if k == 2:
                    split_hi(0, 0, 0)
                act.wait_ge(O[f"wo{k % 3}"], k // 3 * 16 + 16)
                A(wo_hi[:, k], wo[k % 3][:], ACT.Copy).then_inc(O["whi"], 1)
            split_hi(1, 1, 0)
            act.wait_ge(O["const"], 64)

            def step(n, i, j):
                rows = bass.ds(n * P, P)
                if within(n):
                    wait("h", n, 2)
                    act.dma_start(a["h"][rows, :], xt[i][:]).then_inc(O[f"hout{i}"], 16)
                    A(junk[:], xt[i][:], ACT.Square, accum_out=st[:, i, 0:1]).then_inc(O["sq"], 1)
                    wait("sq", n, 1)
                    A(st[:, i, 1:2], st[:, i, 0:1], ACT.Ln, scale=1.0 / D,
                      bias=cst[:, C_COL + COL_EPS:C_COL + COL_EPS + 1]).then_inc(O["ln"], 1)
                    wait("ln", n, 1)
                    A(st[:, i, 2:3], st[:, i, 1:2], ACT.Exp, scale=-0.5).then_inc(O["r0"], 1)
                if within(n + 2):
                    split_hi(n + 2, i, j + 1)
                if within(n - 1):
                    r = rt[:, 1 - i]
                    wait("v", n - 1, 2)
                    A(r[:, 8:16], lg[:, 1 - i, 0:EPG], ACT.Exp, bias=r[:, 0:1], accum_out=r[:, 1:2]).then_inc(O["pe"], 1)
                    wait("v", n - 1, 10)
                    A(r[:, 3:4], r[:, 2:3], ACT.Exp).then_inc(O["pe"], 1)
                if within(n):
                    wait("xn", n, 1)
                    act.dma_start(a["xn"][rows, :], xn[i][:]).then_inc(O[f"xnout{i}"], 16)
                    for q in range(2):
                        wait("ptr", n, q + 1)
                        A(xnT[i][:, 4 * q:4 * q + 4, :].rearrange("p k t -> p (k t)"), ps[4 + q][:], ACT.Copy)\
                            .then_inc(O["ev"], 1)

            steps(act, step, 1)

        @block.vector
        def _(dve):
            V = nc.vector
            wait = waits(dve)

            def chain(name, n):
                done = [0]

                def v(ins, hold=False):
                    ins.then_inc(O[name], 1)
                    done[0] += 1
                    wait(name, n, done[0])
                    if hold:
                        dve.nop(nofuse=True)
                return v

            def split_lo(n, i):
                wait("hi", n, 1)
                V.tensor_tensor(mix_lo[i][:], mixT[i][:], mix_hi[i][:].bitcast(F32), ALU.subtract).then_inc(O["lo"], 1)

            for k in range(KD):
                if k == 2:
                    split_lo(0, 0)
                dve.wait_ge(O["whi"], k + 1)
                V.tensor_tensor(wo_lo[:, k], wo[k % 3][:], wo_hi[:, k].bitcast(F32), ALU.subtract).then_inc(O["wlo"], 1)
            split_lo(1, 1)
            dve.wait_ge(O["const"], 64)
            dve.wait_ge(O["start"], 1)

            def residual(n, i, j):
                dve.wait_ge(O[f"xt{i}"], j * 16 + 16)
                for q in range(2):
                    wait("po", n, q + 1)
                    hq = xt[i][:, q * GRP:(q + 1) * GRP]
                    V.tensor_tensor(hq, hq, ps[2 * i + q][:], ALU.add).then_inc(O["h"], 1)

            def norm(n, i, j):
                y = lambda k: st[:, i, k:k + 1]
                wait("r0", n, 1)
                V.tensor_scalar(y(3), y(0), 1.0 / D, EPS, ALU.mult, ALU.add)
                V.tensor_tensor(y(4), y(2), y(2), ALU.mult).then_inc(O["nt"], 1)
                wait("nt", n, 1)
                V.tensor_tensor(y(5), y(4), y(3), ALU.mult).then_inc(O["nt"], 1)
                wait("nt", n, 2)
                V.tensor_scalar(y(6), y(5), -0.5, 1.5, ALU.mult, ALU.add).then_inc(O["nt"], 1)
                wait("nt", n, 3)
                V.tensor_tensor(y(7), y(6), y(2), ALU.mult).then_inc(O["nt"], 1)
                wait("nt", n, 4)
                if within(n, 2):
                    dve.wait_ge(O[f"xnout{i}"], j * 16)
                V.scalar_tensor_tensor(xn[i][:], xt[i][:], y(7), wn[:], ALU.mult, ALU.mult).then_inc(O["xn"], 1)

            def choose(n, i):
                v = chain("v", n)
                r = rt[:, i]
                wait("plg", n, 1)
                V.tensor_copy(lg[:, i, :], ps[6][:, 0:EPG + NE]).then_inc(O["lg"], 1)
                wait("lg", n, 1)
                dve.nop(nofuse=True)
                v(V.max(m8[:, 0], lg[:, i, 0:EPG]))
                v(V.tensor_scalar(r[:, 0:1], m8[:, 0, 0:1], -1.0, None, ALU.mult), hold=True)
                v(V.max_index(i8[:], m8[:, 0], lg[:, i, 0:EPG]))
                v(V.tensor_copy(r[:, 4:5], i8[:, 0:1]))
                v(V.tensor_scalar(m8[:, 2], i8c, r[:, 4:5], None, ALU.is_equal))
                v(V.tensor_tensor(prod[:], lg[:, i, EPG:].rearrange("p (g e) -> p e g", g=EPG),
                                  m8[:, 2].unsqueeze(1).to_broadcast([P, EPG, EPG]), ALU.mult))
                v(V.tensor_reduce(esel[:], prod[:], AX.X, ALU.add), hold=True)
                v(V.max(m8[:, 1], esel[:]), hold=True)
                v(V.max_index(i8b[:], m8[:, 1], esel[:]))
                v(V.tensor_tensor(r[:, 2:3], m8[:, 1, 1:2], m8[:, 1, 0:1], ALU.subtract))
                v(V.tensor_copy(r[:, 16:18], i8b[:, 0:2]))
                v(V.tensor_scalar(r[:, 5:6], r[:, 4:5], float(EPG), None, ALU.mult))
                v(V.tensor_scalar(r[:, 24:26], r[:, 16:18], r[:, 5:6], None, ALU.add))
                v(V.tensor_scalar(oh[:, i, 0], i64, r[:, 24:25], None, ALU.is_equal))
                v(V.tensor_scalar(oh[:, i, 1], i64, r[:, 25:26], None, ALU.is_equal))
                v(V.tensor_tensor(oh[:, i, 2], oh[:, i, 0], oh[:, i, 1], ALU.add))
                wait("pe", n, 2)
                v(V.tensor_scalar(r[:, 6:7], r[:, 3:4], 1.0, r[:, 1:2], ALU.add, ALU.mult))
                v(V.reciprocal(r[:, 28:29], r[:, 6:7]))
                v(V.tensor_tensor(r[:, 29:30], r[:, 28:29], r[:, 3:4], ALU.mult))

            def rank(n, i):
                k = chain("rk", n)
                r, o = rt[:, i], oh[:, i]
                wait("prk", n, 1)
                k(V.tensor_tensor(o[:, 3], ps[7][:, 0:NE], cnt[:], ALU.add))
                V.tensor_tensor(o[:, 0], o[:, 0], o[:, 3], ALU.mult)
                k(V.tensor_tensor(o[:, 1], o[:, 1], o[:, 3], ALU.mult))
                k(V.tensor_reduce(r[:, 26:27], o[:, 0], AX.X, ALU.add))
                k(V.tensor_reduce(r[:, 27:28], o[:, 1], AX.X, ALU.add))
                k(V.tensor_tensor(cnt[:], ps[7][:, NE:2 * NE], cnt[:], ALU.add))
                k(V.memset(r[:, 30:32], 0.0), hold=True)
                k(V.tensor_copy(tab[:, bass.ds(n, 1), :].rearrange("p n k -> p (n k)"), r[:, 24:32]))

            def step(n, i, j):
                if within(n):
                    residual(n, i, j)
                if within(n - 2):
                    rank(n - 2, i)
                if within(n):
                    norm(n, i, j)
                if within(n - 1):
                    choose(n - 1, 1 - i)
                if within(n + 2):
                    split_lo(n + 2, i)

            steps(dve, step, 2)
            n = [0]

            def w(ins):
                n[0] += 1
                ins.then_inc(O["table"], 1)
                dve.wait_ge(O["table"], n[0])

            w(V.tensor_scalar(blk[:, 2], cnt[:], float(P - 1), None, ALU.add))
            w(V.tensor_copy(blk_i[:, 0], blk[:, 2]))
            w(V.tensor_scalar(blk_i[:, 1], blk_i[:, 0], 7, None, ALU.arith_shift_right))
            nb, up = blk[:, 0], blk[:, 1]
            w(V.tensor_copy(nb, blk_i[:, 1]))
            w(V.tensor_tensor_scan(up, ones[:, 0:NE], nb, 0.0, ALU.mult, ALU.add))
            w(V.tensor_tensor(base[:], up, nb, ALU.subtract))
            w(V.tensor_scalar(late[:], up, cst[:, C_TOK:C_TOK + 1], None, ALU.is_le))
            w(V.tensor_reduce(rf[:, 0, 0:1], late[:], AX.X, ALU.add))
            w(V.tensor_scalar(rf[:, 0, 0:1], rf[:, 0, 0:1], float(NE - 1), None, ALU.min))
            w(V.tensor_copy(expert[:], rf[:, 0, 0:1].to_broadcast([P, P])))
            assert n[0] == EXPERT_STEP
            w(V.tensor_copy(slots[:, NSLOT:2 * NSLOT], up[:, NE - 1:NE].to_broadcast([P, NSLOT])))
            dve.wait_ge(O["pexpert"], 1)
            w(V.tensor_copy(slots[:, 0:NSLOT], ps[1][:, 0:NSLOT]))
            assert n[0] == EXPERT_ROW_STEP
            for i in range(2):
                w(V.tensor_tensor(sel[:], i64.unsqueeze(1).to_broadcast([P, NT, NE]),
                                  tab[:, :, i:i + 1].to_broadcast([P, NT, NE]), ALU.is_equal))
                w(V.tensor_tensor(sel[:], sel[:], base[:].unsqueeze(1).to_broadcast([P, NT, NE]), ALU.mult))
                w(V.tensor_reduce(rf[:, 0, i * NT:(i + 1) * NT], sel[:], AX.X, ALU.add))
                w(V.tensor_copy(ri[:, 0, i * NT:(i + 1) * NT], tab[:, :, 2 + i]))
                w(V.tensor_scalar(number[:, i * NT:(i + 1) * NT], cst[:, C_TOK:C_TOK + NT], float(T * i + 1), None, ALU.add))
            w(V.tensor_scalar(ri[:, 1], ri[:, 0], 7, None, ALU.arith_shift_right))
            w(V.tensor_scalar(ri[:, 2], ri[:, 0], P - 1, None, ALU.bitwise_and))
            w(V.tensor_copy(rf[:, 1], ri[:, 1]))
            w(V.tensor_copy(rf[:, 2], ri[:, 2]))
            w(V.tensor_tensor(rf[:, 3], rf[:, 0], rf[:, 1], ALU.add))
            w(V.tensor_tensor(row_hot[:], cst[:, C_SLOT:C_SLOT + P].unsqueeze(1).to_broadcast([P, 2 * NT, P]),
                              rf[:, 2].unsqueeze(2).to_broadcast([P, 2 * NT, P]), ALU.is_equal))
            assert n[0] == TABLE_STEPS
            for k in range(2 * NT):
                V.tensor_scalar(block_id[:, k], cst[:, C_SLOT:C_SLOT + NSLOT], rf[:, 3, k:k + 1], number[:, k:k + 1],
                                ALU.is_equal, ALU.mult).then_inc(O["placed"], 1)
            dve.wait_ge(O["prows"], 1)
            V.tensor_scalar(miss[:], ps[0][:, 0:NSLOT], 1.0, float(OOB), ALU.is_lt, ALU.mult).then_inc(O["placed"], 1)
            dve.wait_ge(O["placed"], 2 * NT + 1)
            V.scalar_tensor_tensor(rows[:], ps[0][:, 0:NSLOT], -1.0, miss[:], ALU.add, ALU.add)

        @block.tensor
        def _(pe):
            mm = nc.tensor.matmul
            wait = waits(pe)

            def out_proj(n, i, j):
                wait("lo", n, 1)
                for q in range(2):
                    if within(n, 2):
                        wait("h", n - 2, q + 1)
                    for k in range(KD):
                        if isinstance(n, int) and n + q == 0:
                            pe.wait_ge(O["wlo"], k + 1)
                        cols = slice(q * GRP, (q + 1) * GRP)
                        mm(ps[2 * i + q][:], mix_hi[i][:, k, :], wo_hi[:, k, cols], start=(k == 0), stop=False)
                        mm(ps[2 * i + q][:], mix_hi[i][:, k, :], wo_lo[:, k, cols], start=False, stop=False)
                        last = mm(ps[2 * i + q][:], mix_lo[i][:, k, :], wo_hi[:, k, cols], start=False, stop=(k == KD - 1))
                    last.then_inc(O["po"], 1)

            def transposes(n, i):
                wait("xn", n, 1)
                for q in range(2):
                    if within(n, 1):
                        wait("ev", n - 1, q + 1)
                    for k in range(4):
                        last = nc.tensor.transpose(ps[4 + q][:, k * P:(k + 1) * P],
                                                   xn[i][:, (4 * q + k) * P:(4 * q + k + 1) * P], ident)
                    last.then_inc(O["ptr"], 1)

            def logits(n, i):
                if within(n, 1):
                    wait("lg", n - 1, 1)
                for k in range(KD):
                    if k % 4 == 0:
                        wait("ev", n, k // 4 + 1)
                    last = mm(ps[6][:, 0:EPG + NE], xnT[i][:, k, :], wr[:, k, :], start=(k == 0), stop=(k == KD - 1))
                last.then_inc(O["plg"], 1)

            def ranks(n, i):
                wait("v", n, 16)
                if within(n, 1):
                    wait("rk", n - 1, 5)
                mm(ps[7][:, 0:NE], US, oh[:, i, 2], start=True, stop=True)
                mm(ps[7][:, NE:2 * NE], ones, oh[:, i, 2], start=True, stop=True).then_inc(O["prk"], 1)

            def step(n, i, j):
                if within(n + 1):
                    out_proj(n + 1, 1 - i, j + i)
                if within(n):
                    transposes(n, i)
                if within(n - 1):
                    ranks(n - 1, 1 - i)
                if within(n):
                    logits(n, i)

            out_proj(0, 0, 0)
            pe.wait_ge(O["const"], 64)
            steps(pe, step, 1)
            pe.wait_ge(O["table"], EXPERT_STEP)
            mm(ps[1][:, 0:P], expert[:], ident, start=True, stop=True).then_inc(O["pexpert"], 1)
            pe.wait_ge(O["table"], TABLE_STEPS)
            for k in range(2 * NT):
                pe.wait_ge(O["placed"], k + 1)
                last = mm(ps[0][:, 0:NSLOT], row_hot[:, k], block_id[:, k], start=(k == 0), stop=(k == 2 * NT - 1))
            last.then_inc(O["prows"], 1)


def experts(nc, a, pool_dma, kept):
    with ExitStack() as ctx:
        def sb(name, *shape, dt=F32):
            return ctx.enter_context(nc.sbuf_tensor("e_" + name, [P, *shape], dt))

        NB = EB
        KF = FF // P
        rows, slots, ident = kept["rows"], kept["slots"], kept["ident"][:]
        tok, late = sb("tok", NSLOT + NB, dt=I32), sb("late", NSLOT)
        gi = [sb(f"gi{i}", 1, dt=I32) for i in range(NB)]
        oi = [sb(f"oi{i}", 1, dt=I32) for i in range(NB)]
        wg = [kept["w"][0]] + [sb(f"wg{i}", KD, FF) for i in range(1, NB)]
        wu = [kept["w"][1]] + [sb(f"wu{i}", KD, FF) for i in range(1, NB)]
        wd = [kept["w"][2]] + [sb(f"wd{i}", KF, D) for i in range(1, NB)]
        xg = [sb(f"xg{i}", D) for i in range(NB)]
        xT = [sb(f"xT{i}", KD, P) for i in range(NB)]
        th = [sb(f"th{i}", FF) for i in range(2)]
        h = sb("h", FF)
        hT = sb("hT", KF, P)
        y = [sb(f"y{i}", D) for i in range(NB)]
        pgu = [ctx.enter_context(nc.psum_tensor(f"e_gu{i}", [P, 2 * FF], F32)) for i in range(2)]
        px = [ctx.enter_context(nc.psum_tensor(f"e_px{i}", [P, GRP], F32)) for i in range(2)]
        ph = ctx.enter_context(nc.psum_tensor("e_ph", [P, GRP], F32))
        py = [ctx.enter_context(nc.psum_tensor(f"e_py{i}", [P, GRP], F32)) for i in range(2)]
        names = ["zero", "tok", "gi", "oi", "px", "xT", "pgu", "th", "g", "h", "ph", "hT", "py", "y"] \
            + [f"w{i}" for i in range(1, NB)]
        E = {n: nc.alloc_semaphore("e_" + n) for n in names}
        E["w0"] = kept["w0"]
        E |= {n[2:]: sem for n, sem in pool_dma.items() if n.startswith("e_")}
        block = ctx.enter_context(nc.Block())

        def load_count(eng):
            return eng.value_load(slots[0:1, NSLOT:NSLOT + 1], min_val=2 * T // P, max_val=NSLOT - 1)

        def uses(j, i):
            return j + 1 + i // NB

        def y_written_out(eng, i, j):
            with eng.If(j > 0):
                eng.wait_ge(E[f"out{i}"], j * 16)
                eng.nop(nofuse=True)

        @block.sync
        def _(sp):
            count = load_count(sp)
            sp.wait_ge(E["x0"], 16)
            with sp.Fori(0, NSLOT // NB) as j, sp.If(j * NB < count):
                for i in range(NB):
                    s = j * NB + i

                    def down_free():
                        sp.wait_ge(E["py"], s * 2 + 2)
                        sp.nop(nofuse=True)

                    def load_block():
                        e = sp.value_load(slots[0:1, bass.ds(s, 1)], min_val=0, max_val=NE - 1)
                        sp.wait_ge(E["pgu"], s + 1)
                        sp.nop(nofuse=True)
                        load_expert(sp, a, e, (wg[i], wu[i], wd[i]), E[f"w{i}"], down_free)

                    with sp.If(s < count):
                        if i == 0:
                            with sp.If(j > 0):
                                load_block()
                        else:
                            load_block()
            for t in range(HB):
                sp.dma_start(kept["h"][t][:], a["h"][t * P:(t + 1) * P, :]).then_inc(kept["loaded"][t], 16)
            sp.dma_start(kept["wn"][:], a["final_norm"].partition_broadcast(P)).then_inc(kept["params"], 16)
            sp.dma_start(kept["eps"][:], a["consts"][:, C_COL:C_COL + 4]).then_inc(kept["params"], 16)

        @block.gpsimd
        def _(pool):
            count = load_count(pool)
            pool.wait_ge(E["tok"], 2)

            def gather(n, i):
                nc.gpsimd.tensor_copy(gi[i][:], tok[:, bass.ds(n, 1)]).then_inc(E["gi"], 1)
                pool.wait_ge(E["gi"], n + 1)
                pool.nop(nofuse=True)
                pool.indirect_dma_start(out=xg[i][:], out_offset=None, in_=a["xn"],
                                        in_offset=bass.IndirectOffsetOnAxis(ap=gi[i][:], axis=0),
                                        bounds_check=T - 1, oob_is_err=False).then_inc(E[f"x{i}"], 16)

            for i in range(NB):
                nc.gpsimd.memset(xg[i][:], 0.0).then_inc(E["zero"], 1)
                pool.wait_ge(E["zero"], i + 1)
                gather(i, i)
            with pool.Fori(0, NSLOT // NB) as j, pool.If(j * NB < count):
                for i in range(NB):
                    s = j * NB + i
                    with pool.If(s < count):
                        y_written_out(pool, i, j)
                        nc.gpsimd.tensor_copy(oi[i][:], rows[:, bass.ds(s, 1)]).then_inc(E["oi"], 1)
                        pool.wait_ge(E["oi"], s + 1)
                        pool.nop(nofuse=True)
                        pool.wait_ge(E["y"], 2 * s + 4)
                        pool.nop(nofuse=True)
                        pool.indirect_dma_start(out=a["y"], in_=y[i][:], in_offset=None,
                                                out_offset=bass.IndirectOffsetOnAxis(ap=oi[i][:], axis=0),
                                                bounds_check=2 * T - 1, oob_is_err=False).then_inc(E[f"out{i}"], 16)
                    with pool.If(s + NB < count):
                        pool.wait_ge(E["px"], 2 * s + 2)
                        pool.nop(nofuse=True)
                        gather(s + NB, i)
            for i in range(NB):
                pool.wait_ge(E[f"out{i}"], ((count + (NB - 1 - i)) // NB) * 16)
                pool.nop(nofuse=True)

        @block.scalar
        def _(act):
            A = nc.scalar.activation
            count = load_count(act)

            def x_evac(n, i):
                act.wait_ge(E["px"], 2 * n + 1)
                A(xT[i][:, 0:4, :].rearrange("p k t -> p (k t)"), px[0][:], ACT.Copy).then_inc(E["xT"], 1)

            def tanh(n, i, first=False):
                act.wait_ge(E["pgu"], n + 1 + NB)
                if not first:
                    act.wait_ge(E["h"], n)
                A(th[i % 2][:], pgu[i % 2][:, 0:FF], ACT.Tanh, scale=0.5).then_inc(E["th"], 1)

            x_evac(0, 0)
            tanh(0, 0, first=True)
            x_evac(1, 1)
            with act.Fori(0, NSLOT // NB) as j, act.If(j * NB < count):
                for i in range(NB):
                    s = j * NB + i
                    with act.If(s < count):
                        with act.If(s + 1 < count):
                            tanh(s + 1, i + 1)
                        act.wait_ge(E["ph"], s + 1)
                        A(hT[:].rearrange("p k t -> p (k t)"), ph[:, 0:FF], ACT.Copy, scale=0.5).then_inc(E["hT"], 1)
                        with act.If(s + 2 < count):
                            x_evac(s + 2, (i + 2) % NB)
                        y_written_out(act, i, j)
                        act.wait_ge(E["py"], 2 * s + 1 + 2 * NB)
                        A(y[i][:, 0:GRP], py[0][:], ACT.Copy).then_inc(E["y"], 1)

        @block.vector
        def _(dve):
            V = nc.vector
            V.tensor_scalar(late[:], rows[:], float(T), -float(T), ALU.is_ge, ALU.mult).then_inc(E["tok"], 1)
            dve.wait_ge(E["tok"], 1)
            V.tensor_tensor(tok[:, 0:NSLOT], rows[:], late[:], ALU.add).then_inc(E["tok"], 1)
            V.memset(h[:], 0.0).then_inc(E["y"], 2)
            V.memset(th[0][:], 0.0).then_inc(E["pgu"], NB)
            V.memset(th[1][:], 0.0).then_inc(E["py"], 2 * NB)
            count = load_count(dve)
            dve.wait_ge(E["y"], 2)

            def x_evac(n, i):
                dve.wait_ge(E["px"], 2 * n + 2)
                V.tensor_copy(xT[i][:, 4:8, :].rearrange("p k t -> p (k t)"), px[1][:]).then_inc(E["xT"], 1)

            def swiglu(n, i, first=False):
                dve.wait_ge(E["th"], n + 1)
                V.scalar_tensor_tensor(th[i % 2][:], th[i % 2][:], 1.0, pgu[i % 2][:, 0:FF], ALU.add, ALU.mult)\
                    .then_inc(E["g"], 1)
                dve.wait_ge(E["g"], n + 1)
                if not first:
                    dve.wait_ge(E["ph"], n)
                V.tensor_tensor(h[:], th[i % 2][:], pgu[i % 2][:, FF:2 * FF], ALU.mult).then_inc(E["h"], 1)

            x_evac(0, 0)
            swiglu(0, 0, first=True)
            x_evac(1, 1)
            with dve.Fori(0, NSLOT // NB) as j, dve.If(j * NB < count):
                for i in range(NB):
                    s = j * NB + i
                    with dve.If(s < count):
                        with dve.If(s + 1 < count):
                            swiglu(s + 1, i + 1)
                        with dve.If(s + 2 < count):
                            x_evac(s + 2, (i + 2) % NB)
                        y_written_out(dve, i, j)
                        dve.wait_ge(E["py"], 2 * s + 2 + 2 * NB)
                        V.tensor_copy(y[i][:, GRP:D], py[1][:]).then_inc(E["y"], 1)

        @block.tensor
        def _(pe):
            mm = nc.tensor.matmul
            count = load_count(pe)

            def x_transposes(n, j, i, first=False):
                pe.wait_ge(E[f"x{i % NB}"], uses(j, i) * 16)
                if not first:
                    pe.wait_ge(E["xT"], 2 * n)
                xv = xg[i % NB][:].rearrange("t (p k) -> t k p", k=KD)
                for q in range(2):
                    for k in range(4):
                        last = nc.tensor.transpose(px[q][:, k * P:(k + 1) * P], xv[:, 4 * q + k, :], ident)
                    last.then_inc(E["px"], 1)

            def gate_up(n, j, i):
                pe.wait_ge(E[f"w{i % NB}"], uses(j, i) * 48)
                pe.wait_ge(E["xT"], 2 * n + 2)
                for q, w in enumerate((wg[i % NB], wu[i % NB])):
                    for k in range(KD):
                        last = mm(pgu[i % 2][:, q * FF:(q + 1) * FF], xT[i % NB][:, k, :], w[:, k, :],
                                  start=(k == 0), stop=(k == KD - 1))
                last.then_inc(E["pgu"], 1)

            x_transposes(0, 0, 0, first=True)
            gate_up(0, 0, 0)
            x_transposes(1, 0, 1)
            with pe.Fori(0, NSLOT // NB) as j, pe.If(j * NB < count):
                for i in range(NB):
                    s = j * NB + i
                    with pe.If(s < count):
                        with pe.If(s + 1 < count):
                            gate_up(s + 1, j, i + 1)
                        pe.wait_ge(E["h"], s + 1)
                        hv = h[:].rearrange("t (p k) -> t k p", k=KF)
                        for k in range(KF):
                            last = nc.tensor.transpose(ph[:, k * P:(k + 1) * P], hv[:, k, :], ident)
                        last.then_inc(E["ph"], 1)
                        with pe.If(s + 2 < count):
                            x_transposes(s + 2, j, i + 2)
                        pe.wait_ge(E["hT"], s + 1)
                        pe.wait_ge(E["y"], 2 * s + 2)
                        for q in range(2):
                            for k in range(KF):
                                last = mm(py[q][:], hT[:, k, :], wd[i][:, k, q * GRP:(q + 1) * GRP],
                                          start=(k == 0), stop=(k == KF - 1))
                            last.then_inc(E["py"], 1)


def combine(nc, a, pool_dma, kept):
    with ExitStack() as ctx:
        def sb(name, *shape, dt=F32):
            return ctx.enter_context(nc.sbuf_tensor("c_" + name, [P, *shape], dt))

        NB = HB
        tab, wn, eps, ht = kept["gates"], kept["wn"], kept["eps"], kept["h"]
        yt = [sb(f"y{i}", 2, D) for i in range(NB)]
        junk, st = sb("junk", D), sb("st", NT, 8)
        E = {n: nc.alloc_semaphore("c_" + n) for n in ["s1", "s2", "sq", "ln", "r0", "nt", "o"]
             + [f"{n}{i}" for i in range(NB) for n in ("y", "out")]}
        E |= {f"h{i}": kept["loaded"][i] for i in range(NB)} | {"start": kept["params"]}
        block = ctx.enter_context(nc.Block())

        @block.sync
        def _(sp):
            for t in range(NT):
                i = t % NB
                if t >= NB:
                    sp.wait_ge(E[f"out{i}"], 16 * (t // NB))
                    sp.dma_start(ht[i][:], a["h"][t * P:(t + 1) * P, :]).then_inc(E[f"h{i}"], 16)
                    sp.wait_ge(E["s2"], t - NB + 1)
                sp.dma_start(yt[i][:], a["y"].rearrange("(k n p) d -> n p k d", k=2, p=P)[t]).then_inc(E[f"y{i}"], 16)

        @block.vector
        def _(dve):
            V = nc.vector
            dve.wait_ge(E["start"], 32)

            def norm(t):
                i = t % NB
                y = lambda k: st[:, t, k:k + 1]
                dve.wait_ge(E["r0"], t + 1)
                V.tensor_scalar(y(3), y(0), 1.0 / D, EPS, ALU.mult, ALU.add)
                V.tensor_tensor(y(4), y(2), y(2), ALU.mult).then_inc(E["nt"], 1)
                dve.wait_ge(E["nt"], 4 * t + 1)
                V.tensor_tensor(y(5), y(4), y(3), ALU.mult).then_inc(E["nt"], 1)
                dve.wait_ge(E["nt"], 4 * t + 2)
                V.tensor_scalar(y(6), y(5), -0.5, 1.5, ALU.mult, ALU.add).then_inc(E["nt"], 1)
                dve.wait_ge(E["nt"], 4 * t + 3)
                V.tensor_tensor(y(7), y(6), y(2), ALU.mult).then_inc(E["nt"], 1)
                dve.wait_ge(E["nt"], 4 * t + 4)
                V.scalar_tensor_tensor(ht[i][:], ht[i][:], y(7), wn[:], ALU.mult, ALU.mult).then_inc(E["o"], 1)

            for t in range(NT):
                i = t % NB
                dve.wait_ge(E[f"h{i}"], 16 * (t // NB + 1))
                dve.wait_ge(E[f"y{i}"], 16 * (t // NB + 1))
                V.scalar_tensor_tensor(ht[i][:], yt[i][:, 0], tab[:, t, 4:5], ht[i][:], ALU.mult, ALU.add)\
                    .then_inc(E["s1"], 1)
                dve.wait_ge(E["s1"], t + 1)
                V.scalar_tensor_tensor(ht[i][:], yt[i][:, 1], tab[:, t, 5:6], ht[i][:], ALU.mult, ALU.add)\
                    .then_inc(E["s2"], 1)
                if t:
                    norm(t - 1)
            norm(NT - 1)

        @block.scalar
        def _(act):
            A = nc.scalar.activation
            act.wait_ge(E["start"], 32)
            for t in range(NT):
                i = t % NB
                act.wait_ge(E["s2"], t + 1)
                if t:
                    act.wait_ge(E["sq"], t)
                A(junk[:], ht[i][:], ACT.Square, accum_out=st[:, t, 0:1]).then_inc(E["sq"], 1)
                act.wait_ge(E["sq"], t + 1)
                A(st[:, t, 1:2], st[:, t, 0:1], ACT.Ln, scale=1.0 / D, bias=eps[:, COL_EPS:COL_EPS + 1]).then_inc(E["ln"], 1)
                act.wait_ge(E["ln"], t + 1)
                A(st[:, t, 2:3], st[:, t, 1:2], ACT.Exp, scale=-0.5).then_inc(E["r0"], 1)
                if t:
                    act.wait_ge(E["o"], t)
                    act.dma_start(a["out"][(t - 1) * P:t * P, :], ht[(t - 1) % NB][:]).then_inc(E[f"out{(t - 1) % NB}"], 16)
            act.wait_ge(E["o"], NT)
            act.dma_start(a["out"][(NT - 1) * P:, :], ht[(NT - 1) % NB][:]).then_inc(E[f"out{(NT - 1) % NB}"], 16)
            for i in range(NB):
                act.wait_ge(E[f"out{i}"], 16 * NT // NB)


def build(nc, a):
    pool_dma = {n: nc.alloc_semaphore(n) for n in ("s_outh", "s_outg", *(f"e_{n}{i}" for n in ("x", "out") for i in range(EB)))}
    with ExitStack() as ctx:
        kept = {}
        for part in (trunk, router, experts, combine):
            if part is router:
                kept.update(tables(nc, ctx))
            if part is experts:
                kept.update(prefetched(nc, ctx))
            before = set(nc.free_semaphores)
            part(nc, a, pool_dma, kept)
            if part is not combine:
                nc.clear_and_free_semaphores(sorted(before - set(nc.free_semaphores)))
                nc.all_engine_barrier()


def load_expert(sp, a, e, w, sem, down_free=None):
    (wg, wu, wd) = w
    sp.dma_start(wg[:], a["w_gate"][bass.ds(e, 1)].rearrange("e (p k) f -> p (e k) f", k=KD)).then_inc(sem, 16)
    sp.dma_start(wu[:], a["w_up"][bass.ds(e, 1)].rearrange("e (p k) f -> p (e k) f", k=KD)).then_inc(sem, 16)
    if down_free:
        down_free()
    sp.dma_start(wd[:], a["w_down"][bass.ds(e, 1)].rearrange("e (p k) d -> p (e k) d", k=FF // P)).then_inc(sem, 16)


def tables(nc, ctx):
    sb = lambda name, *shape, dt=F32: ctx.enter_context(nc.sbuf_tensor("k_" + name, [P, *shape], dt))
    return dict(rows=sb("rows", NSLOT, dt=I32), slots=sb("slots", 2 * NSLOT, dt=I32), gates=sb("gates", NT, 8),
                ident=sb("ident", P), w=(sb("wg", KD, FF), sb("wu", KD, FF), sb("wd", FF // P, D)),
                w0=nc.alloc_semaphore("k_w0"))


def prefetched(nc, ctx):
    sb = lambda name, *shape: ctx.enter_context(nc.sbuf_tensor("k_" + name, [P, *shape], F32))
    return dict(h=[sb(f"h{i}", D) for i in range(HB)], wn=sb("wn", D), eps=sb("eps", 4),
                loaded=[nc.alloc_semaphore(f"k_h{i}") for i in range(HB)], params=nc.alloc_semaphore("k_params"))


EXPERT_STEP = 10
EXPERT_ROW_STEP = 12
TABLE_STEPS = 28

SCRATCH = {
    "mix": ((2 * HEADS, P, T), F32), "h": ((T, D), F32), "xn": ((T, D), F32), "y": ((2 * T, D), F32),
}



def layout(x, norm_mix_w, w_in, hgrn_lb_logits, hgrn_onorm_w, gdn_conv_w, gdn_a_log, gdn_dt_bias,
           gdn_onorm_w, w_out, norm_moe_w, router_group_w, router_expert_w, expert_w_gate,
           expert_w_up, expert_w_down, final_norm_w):
    asc = np.ascontiguousarray
    w = np.asarray(w_in)[0]
    starts = [512, 0, 1536, 1024, 2048, 2560, 3072, 3584]
    blocks = np.stack([w[:, s:s + 512].reshape(KD, P, HEADS, P) for s in starts])
    consts, masks = constant_tables()
    return {
        "consts": consts, "masks": masks,
        "x": asc(np.asarray(x)[0]),
        "norm_mix": asc(np.asarray(norm_mix_w)[0].reshape(KD, P).T),
        "onorm": asc(np.stack([np.asarray(hgrn_onorm_w)[0], np.asarray(gdn_onorm_w)[0]], 1)),
        "w_proj": asc(blocks.transpose(3, 2, 0, 1, 4)),
        "w_ab": asc(w[:, 4096:4104].reshape(KD, P, 8).transpose(1, 0, 2)),
        "lb": asc(np.asarray(hgrn_lb_logits).reshape(2, HEADS, P).transpose(2, 0, 1)),
        "a_log": asc(np.asarray(gdn_a_log)[0]), "dt_bias": asc(np.asarray(gdn_dt_bias)[0]),
        "conv_w": asc(np.asarray(gdn_conv_w)[0].reshape(TAPS, 3, HEADS, P).transpose(3, 2, 1, 0)
                      .reshape(P, HEADS, 3 * TAPS)),
        "w_out": asc(np.asarray(w_out)[0].reshape(KD, P, D).transpose(1, 0, 2)),
        "norm_moe": asc(np.asarray(norm_moe_w)[0]), "final_norm": asc(np.asarray(final_norm_w)),
        "w_router": asc(np.concatenate([np.asarray(router_group_w)[0], np.asarray(router_expert_w)[0]], 1)
                        .reshape(KD, P, 72).transpose(1, 0, 2)),
        "w_gate": np.asarray(expert_w_gate)[0], "w_up": np.asarray(expert_w_up)[0],
        "w_down": np.asarray(expert_w_down)[0],
    }


def kernel(**inputs):
    import concourse.bacc as bacc
    from concourse.bass_utils import run_bass_kernel_spmd

    nc = bacc.Bacc("TRN2", target_bir_lowering=False, num_devices=1)
    arrays = layout(**inputs)
    a = {n: nc.dram_tensor("in_" + n, v.shape, mybir.dt.from_np(v.dtype), kind="ExternalInput").ap()
         for n, v in arrays.items()}
    for n, (shape, dt) in SCRATCH.items():
        a[n] = nc.dram_tensor("tmp_" + n, shape, dt).ap()
    a["out"] = nc.dram_tensor("out", (T, D), F32, kind="ExternalOutput").ap()
    build(nc, a)
    r = run_bass_kernel_spmd(nc, [{"in_" + n: v for n, v in arrays.items()}], core_ids=[0])
    return r.results[0]["out"].reshape(1, T, D)
```
